# Optimizing a Trainium2 kernel written in Bass

```python
import math
import jax, jax.numpy as jnp
from jax import lax
import numpy as np

D_MODEL = 1024
BATCH = 1
SEQ = 256
DEPTH = 1
DEC_BATCH = 8
DEC_SEQ = 8
PAST_LEN = 2048
PAGE_SIZE = 128

N_META = 16
RET_HEADS = 4
RET_DK = D_MODEL // RET_HEADS
RET_DV = 2 * RET_DK
RET_CHUNK = 128
CONV_CH = D_MODEL
CONV_WIDTH = 31
N_EXPERTS = 16
N_GROUPS = 4
EXPERTS_PER_GROUP = N_EXPERTS // N_GROUPS
TOP_K = 2
D_EXPERT = D_MODEL
ROPE_BASE = 10000.0
LN_EPS = 1e-5

N_Q = RET_HEADS * RET_DK
N_K = RET_HEADS * RET_DK
N_V = RET_HEADS * RET_DV
N_G = RET_HEADS * RET_DV
N_GLU = 2 * CONV_CH
N_MERGE = 2 * D_MODEL
N_IN = N_Q + N_K + N_V + N_G + N_GLU + N_MERGE
SPLITS = (N_Q, N_Q + N_K, N_Q + N_K + N_V, N_Q + N_K + N_V + N_G,
          N_Q + N_K + N_V + N_G + CONV_CH, N_Q + N_K + N_V + N_G + N_GLU,
          N_Q + N_K + N_V + N_G + N_GLU + D_MODEL)

kernel_name = "retention_conformer_conv_grouped_moe_deepnorm_step"

def _layernorm(x, g, b):
    xf = x.astype(jnp.float32)
    mu = jnp.mean(xf, axis=-1, keepdims=True)
    var = jnp.mean(jnp.square(xf - mu), axis=-1, keepdims=True)
    y = (xf - mu) * lax.rsqrt(var + LN_EPS) * g.astype(jnp.float32) + b.astype(jnp.float32)
    return y.astype(x.dtype)

def _headnorm(o):
    mu = jnp.mean(o, axis=-1, keepdims=True)
    var = jnp.mean(jnp.square(o - mu), axis=-1, keepdims=True)
    return (o - mu) * lax.rsqrt(var + LN_EPS)

def _rope(x, pos):
    xf = x.astype(jnp.float32)
    inv = ROPE_BASE ** (-jnp.arange(0, RET_DK, 2, dtype=jnp.float32) / RET_DK)
    ang = pos[:, None] * inv[None, :]
    cos = jnp.cos(ang)[None, :, None, :]
    sin = jnp.sin(ang)[None, :, None, :]
    x1, x2 = xf[..., 0::2], xf[..., 1::2]
    return jnp.stack([x1 * cos - x2 * sin, x1 * sin + x2 * cos], axis=-1).reshape(xf.shape)

def _ret_chunk(q, k, v, s, log_g):
    c = q.shape[2]
    i = jnp.arange(c, dtype=jnp.float32)
    diff = i[:, None] - i[None, :]
    dmask = jnp.where(diff >= 0,
                      jnp.exp(jnp.maximum(diff, 0.0)[None] * log_g[:, None, None]), 0.0)
    att = jnp.einsum('bhqd,bhkd->bhqk', q, k) * dmask[None]
    inner = jnp.einsum('bhqk,bhkv->bhqv', att, v)
    q_dec = jnp.exp((i + 1.0)[None, :] * log_g[:, None])
    cross = jnp.einsum('bhqd,bhdv->bhqv', q * q_dec[None, :, :, None], s)
    k_dec = jnp.exp((c - 1.0 - i)[None, :] * log_g[:, None])
    s_new = (jnp.exp(c * log_g)[None, :, None, None] * s
             + jnp.einsum('bhkd,bhkv->bhdv', k * k_dec[None, :, :, None], v))
    return inner + cross, s_new

def _ret_blocks(q, k, v, s, log_g):
    b, h, l, _ = q.shape
    n = l // RET_CHUNK

    def split(a):
        return a.reshape(b, h, n, RET_CHUNK, a.shape[-1]).transpose(2, 0, 1, 3, 4)

    def step(carry, blk):
        qc, kc, vc = blk
        o, carry = _ret_chunk(qc, kc, vc, carry, log_g)
        return carry, o

    s, o = lax.scan(step, s, (split(q), split(k), split(v)))
    return o.transpose(1, 2, 0, 3, 4).reshape(b, h, l, RET_DV), s

def _retention(q, k, v, s, log_g, lead):
    parts = []
    if lead > 0:
        o0, s = _ret_chunk(q[:, :, :lead], k[:, :, :lead], v[:, :, :lead], s, log_g)
        parts.append(o0)
        q, k, v = q[:, :, lead:], k[:, :, lead:], v[:, :, lead:]
    if q.shape[2] % RET_CHUNK == 0:
        o1, s = _ret_blocks(q, k, v, s, log_g)
    else:
        o1, s = _ret_chunk(q, k, v, s, log_g)
    parts.append(o1)
    return jnp.concatenate(parts, axis=2), s

def _moe(x, w_router, b_router, w_gate, w_up, w_down):
    b, l, d = x.shape
    xt = x.reshape(b * l, d)
    logits = (xt @ w_router).astype(jnp.float32) + b_router.astype(jnp.float32)
    probs = jax.nn.softmax(logits, axis=-1)
    grouped = probs.reshape(-1, N_GROUPS, EXPERTS_PER_GROUP)
    gsel = jnp.argmax(jnp.max(grouped, axis=-1), axis=-1)
    in_group = jnp.take_along_axis(grouped, gsel[:, None, None], axis=1)[:, 0]
    vals, idx = lax.top_k(in_group, TOP_K)
    wts = vals / jnp.sum(vals, axis=-1, keepdims=True)
    eidx = gsel[:, None] * EXPERTS_PER_GROUP + idx
    gates = jnp.sum(jax.nn.one_hot(eidx, N_EXPERTS, dtype=jnp.float32) * wts[..., None], axis=1)
    gates = gates.astype(x.dtype)
    y = jnp.zeros_like(xt)
    for e in range(N_EXPERTS):
        he = jax.nn.silu(xt @ w_gate[e]) * (xt @ w_up[e])
        y = y + gates[:, e:e + 1] * (he @ w_down[e])
    return y.reshape(b, l, d)

def _layer(x, pos, s_ret, conv_buf, lead, log_g, alpha,
           w_in, b_in, w_ret_o, conv_w, conv_b, conv_ln_g, conv_ln_b,
           w_conv_o, b_conv_o, w_out, ln1_g, ln1_b, ln2_g, ln2_b,
           w_gate, w_up, w_down, w_router, b_router):
    b, l, _ = x.shape
    h = x @ w_in + b_in
    q, k, v, g, u_a, u_b, m_r, m_c = jnp.split(h, SPLITS, axis=-1)
    q = _rope(q.reshape(b, l, RET_HEADS, RET_DK), pos).transpose(0, 2, 1, 3)
    k = (_rope(k.reshape(b, l, RET_HEADS, RET_DK), pos) * (RET_DK ** -0.5)).transpose(0, 2, 1, 3)
    v = v.reshape(b, l, RET_HEADS, RET_DV).astype(jnp.float32).transpose(0, 2, 1, 3)
    o, s_new = _retention(q, k, v, s_ret.astype(jnp.float32), log_g, lead)
    o = _headnorm(o).transpose(0, 2, 1, 3).reshape(b, l, N_V).astype(x.dtype)
    ret_out = (jax.nn.silu(g) * o) @ w_ret_o
    u = u_a * jax.nn.sigmoid(u_b)
    ext = jnp.concatenate([conv_buf.astype(u.dtype), u], axis=1)
    c = lax.conv_general_dilated(ext, conv_w[:, None, :].astype(ext.dtype), window_strides=(1,),
                                 padding='VALID', dimension_numbers=('NWC', 'WIO', 'NWC'),
                                 feature_group_count=CONV_CH) + conv_b
    buf_new = ext[:, ext.shape[1] - (CONV_WIDTH - 1):]
    c = jax.nn.silu(_layernorm(c, conv_ln_g, conv_ln_b))
    conv_out = c @ w_conv_o + b_conv_o
    mixed = (jax.nn.sigmoid(m_r) * ret_out + jax.nn.sigmoid(m_c) * conv_out) @ w_out
    x = _layernorm(alpha * x + mixed, ln1_g, ln1_b)
    x = _layernorm(alpha * x + _moe(x, w_router, b_router, w_gate, w_up, w_down), ln2_g, ln2_b)
    return x, s_new.astype(s_ret.dtype), buf_new.astype(conv_buf.dtype)

def setup_inputs(seed: int = 0) -> dict:
    key = jax.random.key(seed)
    ks = jax.random.split(key, 24)
    f32 = jnp.float32
    beta = (8.0 * DEPTH) ** -0.25
    nrm = lambda k_, shp: jax.random.normal(k_, shp, dtype=f32)
    col_scale = jnp.ones((N_IN,), f32).at[N_Q + N_K:N_Q + N_K + N_V].set(beta)
    return {
        "x_prompt": nrm(ks[0], (BATCH, SEQ, D_MODEL)),
        "x_sample": nrm(ks[1], (DEC_BATCH, DEC_SEQ, D_MODEL)),
        "state_ret": 0.1 * nrm(ks[2], (DEPTH, DEC_BATCH, RET_HEADS, RET_DK, RET_DV)),
        "state_conv": 0.5 * nrm(ks[3], (DEPTH, DEC_BATCH, CONV_WIDTH - 1, CONV_CH)),
        "meta_tokens": nrm(ks[4], (N_META, D_MODEL)),
        "w_in": nrm(ks[5], (DEPTH, D_MODEL, N_IN)) * (D_MODEL ** -0.5) * col_scale,
        "b_in": 0.02 * nrm(ks[6], (DEPTH, N_IN)),
        "w_ret_o": nrm(ks[7], (DEPTH, N_V, D_MODEL)) * (N_V ** -0.5) * beta,
        "conv_w": nrm(ks[8], (DEPTH, CONV_WIDTH, CONV_CH)) * (CONV_WIDTH ** -0.5),
        "conv_b": 0.02 * nrm(ks[9], (DEPTH, CONV_CH)),
        "conv_ln_g": 1.0 + 0.02 * nrm(ks[10], (DEPTH, CONV_CH)),
        "conv_ln_b": 0.02 * nrm(ks[11], (DEPTH, CONV_CH)),
        "w_conv_o": nrm(ks[12], (DEPTH, CONV_CH, D_MODEL)) * (CONV_CH ** -0.5) * beta,
        "b_conv_o": 0.02 * nrm(ks[13], (DEPTH, D_MODEL)),
        "w_out": nrm(ks[14], (DEPTH, D_MODEL, D_MODEL)) * (D_MODEL ** -0.5) * beta,
        "ln1_g": 1.0 + 0.02 * nrm(ks[15], (DEPTH, D_MODEL)),
        "ln1_b": 0.02 * nrm(ks[16], (DEPTH, D_MODEL)),
        "ln2_g": 1.0 + 0.02 * nrm(ks[17], (DEPTH, D_MODEL)),
        "ln2_b": 0.02 * nrm(ks[18], (DEPTH, D_MODEL)),
        "w_router": nrm(ks[19], (D_MODEL, N_EXPERTS)) * (D_MODEL ** -0.5),
        "b_router": 0.01 * nrm(ks[20], (N_EXPERTS,)),
        "w_gate": nrm(ks[21], (DEPTH, N_EXPERTS, D_MODEL, D_EXPERT)) * (D_MODEL ** -0.5),
        "w_up": nrm(ks[22], (DEPTH, N_EXPERTS, D_MODEL, D_EXPERT)) * (D_MODEL ** -0.5),
        "w_down": nrm(ks[23], (DEPTH, N_EXPERTS, D_EXPERT, D_MODEL)) * (D_EXPERT ** -0.5) * beta,
    }

def reference(x_prompt, x_sample, state_ret, state_conv, meta_tokens, w_in, b_in, w_ret_o,
              conv_w, conv_b, conv_ln_g, conv_ln_b, w_conv_o, b_conv_o, w_out,
              ln1_g, ln1_b, ln2_g, ln2_b, w_router, b_router, w_gate, w_up, w_down):
    alpha = (2.0 * DEPTH) ** 0.25
    log_g = jnp.log(1.0 - 2.0 ** (-5.0 - jnp.arange(RET_HEADS, dtype=jnp.float32)))
    bp = x_prompt.shape[0]
    xp = jnp.concatenate([jnp.broadcast_to(meta_tokens.astype(x_prompt.dtype)[None],
                                           (bp, N_META, D_MODEL)), x_prompt], axis=1)
    xs = x_sample
    pos_p = jnp.arange(xp.shape[1], dtype=jnp.float32)
    pos_s = float(PAST_LEN) + jnp.arange(xs.shape[1], dtype=jnp.float32)
    s0_p = jnp.zeros((bp, RET_HEADS, RET_DK, RET_DV), state_ret.dtype)
    buf0_p = jnp.zeros((bp, CONV_WIDTH - 1, CONV_CH), state_conv.dtype)
    ret_p, conv_p, ret_s, conv_s = [], [], [], []
    for li in range(DEPTH):
        lw = (w_in[li], b_in[li], w_ret_o[li], conv_w[li], conv_b[li], conv_ln_g[li], conv_ln_b[li],
              w_conv_o[li], b_conv_o[li], w_out[li], ln1_g[li], ln1_b[li], ln2_g[li], ln2_b[li],
              w_gate[li], w_up[li], w_down[li], w_router, b_router)
        xp, sp, cp = _layer(xp, pos_p, s0_p, buf0_p, N_META, log_g, alpha, *lw)
        xs, ss, cs = _layer(xs, pos_s, state_ret[li], state_conv[li], 0, log_g, alpha, *lw)
        ret_p.append(sp)
        conv_p.append(cp)
        ret_s.append(ss)
        conv_s.append(cs)
    y_prompt = xp[:, N_META:]
    y_sample = xs
    return (y_prompt, y_sample, jnp.stack(ret_p), jnp.stack(conv_p), jnp.stack(ret_s), jnp.stack(conv_s))


_drawn_inputs = setup_inputs


def setup_inputs(seed=0):
    import zlib

    import numpy as np

    out = dict(_drawn_inputs(seed))
    spreads = {}
    factors = {'conv_ln_g': 4.014,
     'conv_ln_b': 8.0,
     'b_conv_o': 3.886,
     'ln2_g': 8.191,
     'ln2_b': 8.308,
     'b_router': 2.851}
    for name, (base, spread) in spreads.items():
        noise = np.random.default_rng([zlib.crc32(name.encode()), seed]).standard_normal(out[name].shape)
        drawn = base * np.exp(spread * noise) if base else spread * noise
        out[name] = __import__('jax').numpy.asarray(drawn.astype(out[name].dtype))
    for name, factor in factors.items():
        out[name] = (out[name] * factor).astype(out[name].dtype)
    return out
```

```python
import numpy as np
import concourse.bass as bass
from concourse import mybir
from contextlib import ExitStack

D = 1024
KT = D // 128
H = 4
DK, DV = 256, 512
NB, NI = 8, 8
NS = NB * NI
NM, SEQ = 16, 256
NP = NM + SEQ
T = NS + NP
TT = 112
NT = T // TT
CW = 31
EL = NB * (CW - 1 + NI)
EXT = EL + CW - 1 + NP
NE, NG, EG = 16, 4, 4
PAST = 2048
EPS = 1e-5
ALPHA = 2.0 ** 0.25
OFF = dict(q=0, k=D, v=2 * D, g=4 * D, ua=6 * D, ub=7 * D, mr=8 * D, mc=9 * D)
ATT_W = [T - i * TT for i in range(NT)]
ATT_AT = [0, ATT_W[0], ATT_W[0] + ATT_W[1]]
HQ, HKP, HKS, HGAM, HS = 0, NS, NS + NT, NS + NT + NB, NS + NT + NB + 1
TB = {}
_at = 0
for _n, _w in (("cos", T), ("sin", T), ("heads", H * HS),
               ("ident", 128), ("mean", 128)):
    TB[_n] = (_at, _at + _w)
    _at += _w
TBW = _at
VUB, VUA, VG, VCB, VCW = 0, 2, 4, 8, 10
NV = VCW + 2 * CW
VQK = NV
NVQ = NV + 4
V2 = dict(mc=0, mr=8, lng=16, lnb=24, bco=32)


def constants():
    f = np.float32
    log_g = np.log(f(1.0) - f(2.0) ** (f(-5.0) - np.arange(H, dtype=f))).astype(np.float64)
    pos = np.concatenate([PAST + np.arange(NS) % NI, np.arange(NP)]).astype(f)
    inv = (10000.0 ** (-np.arange(0, DK, 2, dtype=np.float64) / DK)).astype(f)
    ang = (pos[None, :] * inv[:, None]).astype(f).astype(np.float64)
    step = np.concatenate([np.arange(NS) % NI, np.arange(NP)])
    seq = np.concatenate([np.arange(NS) // NI, np.full(NP, NB)])
    diff = step[None, :] - step[:, None]
    ok = (seq[None, :] == seq[:, None]) & (diff >= 0)
    scale = DK ** -0.5
    dec = np.zeros((H, TT, sum(ATT_W)), f)
    tab = np.zeros((128, TBW), f)

    def put(name, a):
        tab[:a.shape[0], TB[name][0]:TB[name][1]] = a

    put("cos", np.cos(ang))
    put("sin", np.sin(ang))
    put("ident", np.eye(128))
    put("mean", np.full((128, 128), 1.0 / D))
    heads = np.zeros((128, H, HS))
    for h in range(H):
        lg = log_g[h]
        full = np.where(ok, np.exp(np.maximum(diff, 0) * lg) * scale, 0.0)
        for i in range(NT):
            dec[h, :, ATT_AT[i]:ATT_AT[i] + ATT_W[i]] = full[i * TT:(i + 1) * TT, i * TT:]
        heads[:, h, HQ:HQ + NS] = np.exp((np.arange(NS) % NI + 1.0) * lg)[None, :]
        kp = np.where(seq == NB, np.exp((NP - 1.0 - step) * lg) * scale, 0.0)
        heads[:TT, h, HKP:HKP + NT] = kp.reshape(NT, TT).T
        for b in range(NB):
            heads[:NS, h, HKS + b] = np.where(np.arange(NS) // NI == b, np.exp((NI - 1.0 - np.arange(NS) % NI) * lg) * scale, 0.0)
        heads[:, h, HGAM] = np.exp(NI * lg)
    put("heads", heads.reshape(128, -1))
    return {"tables": tab, "decay": dec}


class Stage:

    def __init__(self, before, names, times=1):
        self.base = before.base + before.n * before.times if before else 0
        self.uses0 = before.uses_after() if before else [1] * 8
        self.n, self.times = len(names), times
        turn = list(before.turn) if before else [0, 0]
        self.at, self.bank, self.local = {}, {}, {}
        self.per = [0] * 8
        for i, name in enumerate(names):
            kind, name = name[0], name[1:]
            self.at[name] = i
            if kind == "-":
                continue
            k = "FP".index(kind)
            bank = 4 * k + turn[k] % 4
            turn[k] += 1
            self.bank[name] = bank
            self.local[name] = self.per[bank]
            self.per[bank] += 1
        self.turn = turn

    def uses_after(self):
        return [u + p * self.times for u, p in zip(self.uses0, self.per)]

    def done(self, name, it=0):
        return it * self.n + (self.base + self.at[name] + 1)

    def start(self, it=0):
        return it * self.n + self.base

    def used(self, name, it=0):
        b = self.bank[name]
        return it * self.per[b] + (self.uses0[b] + self.local[name])

    def emptied(self, name, it=0):
        b = self.bank[name]
        return it * self.per[b] + self.uses0[b]


def at_least(eng, sem, value):
    if not isinstance(value, int) or value > 0:
        eng.wait_ge(sem, value)


def alone(eng, waits_met):
    eng.sem_inc(waits_met, 1)


class Units:

    def __init__(self, before, n, times, last, tail):
        self.base = before.base + before.n * before.times if before else 0
        self.n, self.times, self.last, self.tail = n, times, last, tail

    def idx(self, u, it=0):
        return it * self.n + (self.base + u)


def program(nc, x_prompt, x_sample, state_ret, state_conv, meta_tokens, w_in, b_in, w_ret_o, conv_w, conv_b,
            conv_ln_g, conv_ln_b, w_conv_o, b_conv_o, w_out, ln1_g, ln1_b, ln2_g, ln2_b, w_router, b_router,
            w_gate, w_up, w_down, tables, decay,
            y_prompt, y_sample, new_ret_prompt, new_conv_prompt, new_ret_sample, new_conv_sample):
    f32, f32r = mybir.dt.float32, mybir.dt.float32r
    ALU, ACT, AX = mybir.AluOpType, mybir.ActivationFunctionType, mybir.AxisListType
    ds = bass.ds
    W2 = TT * 2

    ctx = ExitStack()
    with ctx:
        base = [(nc.sbuf_base + 31) // 32 * 32]
        high = [0]

        def sb(name, shape, dt=f32):
            size = 4 * int(np.prod(shape[1:]))
            t = nc.alloc_sbuf_tensor_at(name, shape, dt, offset=base[0])
            base[0] += (size + 31) // 32 * 32
            high[0] = max(high[0], base[0])
            return t

        def sem(name):
            return ctx.enter_context(nc.semaphore(name))

        tab = sb("tab", [128, TBW])
        vec = sb("vec", [128, H, NVQ])
        vec2 = sb("vec2", [128, 40])
        wr_sb = sb("wr_sb", [128, KT, NE])
        br_bc = sb("br_bc", [TT, NE])
        persistent = base[0]
        xT_hi = sb("xT_hi", [128, KT, T], f32r)
        xT_lo = sb("xT_lo", [128, KT, T], f32r)
        raw = sb("raw", [128, 2, 2048])
        hi = sb("hi", [128, 2, 2048], f32r)
        lo = sb("lo", [128, 2, 2048], f32r)
        cT = sb("cT", [128, KT, T])
        retT = sb("retT", [128, KT, T])
        phase = base[0]
        st = sb("st", [128, NB, 2, DV])
        dec = sb("dec", [TT, sum(ATT_W)])
        E = sb("E", [128, 2, EXT])
        us = sb("us", [128, 2, NS])
        hist = sb("hist", [120, 2, 256])
        hv = sb("hv", [128, NVQ])
        hs = sb("hs", [128, HS])
        sub = sb("sub", [128, 2, T])
        qr = sb("qr", [128, 2, T])
        kr = sb("kr", [128, 2, T])
        rt = sb("rt", [128, 4, T])
        v_tok = sb("v_tok", [TT, NT, DV])
        vb = sb("vb", [TT, DV])
        kdp = sb("kdp", [TT, NT, 256])
        kds = sb("kds", [NS, NB, 256])
        att = sb("att", [TT, sum(ATT_W)])
        qdiag = sb("qdiag", [128, 2, NB * (NS + NI)])
        o_tok = sb("o_tok", [TT, NT, DV])
        sg_f = sb("sg_f", [128, 4, TT])
        sg_hi = sb("sg_hi", [128, 4, T], f32r)
        sg_lo = sb("sg_lo", [128, 4, T], f32r)
        ps_out = sb("ps_out", [128, 2, DV])
        u_tok = sb("u_tok", [NS, 256])
        up_tok = sb("up_tok", [CW - 1, 256])
        stats = sb("stats", [TT, NT, 6])
        mv = sb("mv", [TT, NT, 2])
        rs = sb("rs", [TT, 2, NT])
        base[0] = phase
        x_in = sb("x_in", [TT, NT, D])
        vrows = sb("vrows", [NV, H, 128])
        qkrows = sb("qkrows", [8, 256])
        v2rows = sb("v2rows", [40, 128])
        assert base[0] <= phase + 4 * NB * 2 * DV
        base[0] = phase
        x_tok = sb("x_tok", [TT, NT, D])
        x1 = sb("x1", [TT, NT, D])
        c_hi = sb("c_hi", [128, KT, T], f32r)
        c_lo = sb("c_lo", [128, KT, T], f32r)
        gc = sb("gc", [128, KT, T])
        gr = sb("gr", [128, KT, T])
        m_hi = sb("m_hi", [128, KT, T], f32r)
        csq = nc.alloc_sbuf_tensor_at("csq", [128, KT, T], f32, offset=base[0] - 4 * KT * T)
        m_lo = xT_lo
        rstd_c = sb("rstd_c", [128, T])
        lnst = sb("lnst", [TT, NT, 12])
        lnmv = sb("lnmv", [TT, NT, 4])
        ln_bc = sb("ln_bc", [TT, 2, D])
        MR, MH = 4, 3
        base[0] = persistent
        y = sb("y", [TT, NT, D])
        x1T_hi = sb("x1T_hi", [128, KT, T], f32r)
        x1T_lo = sb("x1T_lo", [128, KT, T], f32r)
        gates = sb("gates", [TT, NT, NE])
        gt = sb("gt", [TT, 8, NT, NE])
        gs = sb("gs", [TT, 8, NT])
        gg = sb("gg", [TT, NT, NG])
        g_e = sb("g_e", [TT, NT])
        iota_r = sb("iota_r", [TT, NT, NE])
        mhi = sb("mhi", [128, MH, 2048], f32r)
        mlo = sb("mlo", [128, MH, 2048], f32r)
        assert base[0] <= phase, (base[0], phase)
        base[0] = phase
        h_hi = sb("h_hi", [128, KT, T], f32r)
        h_lo = sb("h_lo", [128, KT, T], f32r)
        base[0] = phase + 2 * 4 * NT * D
        mraw = sb("mraw", [128, MR, 2048])
        sgm = sb("sgm", [128, 2, 2, T])
        h_f = sb("h_f", [128, 2, T])
        ln2_bc = sb("ln2_bc", [TT, 2, D])
        x1T_f = sb("x1T_f", [128, KT, T])
        mst = sb("mst", [TT, NT, 12])
        mmv = sb("mmv", [TT, NT, 4])
        assert high[0] <= nc.sbuf_usable_end, (high[0], nc.sbuf_usable_end)

        bank = [ctx.enter_context(nc.psum_tensor(f"bank{i}", [128, 512], f32)) for i in range(8)]
        ident = tab[:, TB["ident"][0]:TB["ident"][1]]

        PRE = Stage(None, [f"Pxt{i}" for i in range(6)] + ["Pvec", "Pbqk", "Pvec2"])
        HEAD = Stage(PRE, ["Phist0", "Phist1", "Fub0", "Fub1", "Fua0", "Fua1", "Fq0", "Fq1", "Fk0", "Fk1",
                           "PuS", "PuP", "-vp0", "-vp1", "-vp2", "Pv0", "Pv1", "Pv2", "Pkt0", "Pkt1",
                           "Patt0", "Patt1", "Patt2", "Fg0", "Fg1", "Fg2", "Fg3", "Po0", "Po1", "Po2"]
                     + [f"Pst{b}{p}" for b in range(NB) for p in range(2)] + ["Pps0", "Pps1"]
                     + [f"PoT{i}" for i in range(NT)] + [f"Fwr{m}" for m in range(8)], H)
        MEAN = Stage(HEAD, ["Pmean"])
        GATE = Stage(MEAN, ["Fmc0", "Fmc1", "Fmr0", "Fmr1"], 4)
        VAR = Stage(GATE, ["Pvar"])
        CONV = Stage(VAR, ["Fc0", "Fc1", "Fc2", "Fc3"], 2)
        WOUT = Stage(CONV, [x for n in range(2) for x in [f"-wp{n}{t}" for t in range(NT)] + [f"Pw{n}{t}" for t in range(NT)]])
        X1T = Stage(WOUT, [f"Pxt{i}" for i in range(6)] + ["Plog"])
        MNAMES = [x for j in range(4) for x in (f"Fg{2 * j}", f"Fg{2 * j + 1}", f"Fu{2 * j}", f"Fu{2 * j + 1}")]
        MNAMES += [x for n in range(2) for x in [f"-dp{n}{t}" for t in range(NT)] + [f"Pd{n}{t}" for t in range(NT)]]
        MOE = Stage(X1T, MNAMES, NE)

        U_HEAD = Units(None, 10, H, ["ub1", "ua1", "q1", "k1", "vp2", "v2", "g1", "g3", "wr3", "wr7"], [4])
        U_GATE = Units(U_HEAD, 2, 4, ["mc1", "mr1"], [2])
        U_CONV = Units(U_GATE, 2, 2, ["c1", "c3"], [2])
        U_WOUT = Units(U_CONV, 4, 1, ["wp02", "w02", "wp12", "w12"], [2])
        N_UNITS = U_WOUT.base + 4
        U_MOE = Units(None, 12, NE, [f"{x}{2 * j + 1}" for j in range(4) for x in "gu"] + ["dp02", "d02", "dp12", "d12"], [3, 3])

        LEAD, MLEAD = 2, MR
        group_done = sem("group_done")
        evac = [sem(f"evac{i}") for i in range(8)]
        raw_full = [sem(f"raw_full{i}") for i in range(2)]
        hi_ready, lo_ready = sem("hi_ready"), sem("lo_ready")
        mraw_full = [sem(f"mraw_full{i}") for i in range(MR)]
        mhi_ready, mlo_ready = sem("mhi_ready"), sem("mlo_ready")
        s_tab, s_x, s_rows, s_xhi = sem("s_tab"), sem("s_x"), sem("s_rows"), sem("s_xhi")
        st_full = [sem(f"st_full{b}") for b in range(NB)]
        st_out = [sem(f"st_out{b}") for b in range(NB)]
        dec_full, hist_full, vb_full = sem("dec_full"), sem("hist_full"), sem("vb_full")
        hv_ready = sem("hv_ready")
        rope_ready, qdiag_ready = sem("rope_ready"), sem("qdiag_ready")
        sghi_ready, sglo_ready = sem("sghi_ready"), sem("sglo_ready")
        out_sem, ps_stored, u_stored = sem("out_sem"), sem("ps_stored"), sem("u_stored")
        rv_ready, rstd_done = sem("rv_ready"), sem("rstd_done")
        dve_step = sem("dve_step")
        act_step = sem("act_step")
        csub_ready, csq_ready, cn_ready, csilu_ready = (sem(n) for n in ("csub_ready", "csq_ready", "cn_ready", "csilu_ready"))
        chi_ready, clo_ready = sem("chi_ready"), sem("clo_ready")
        mf_ready, mhi_done, mlo_done = sem("mf_ready"), sem("mhi_done"), sem("mlo_done")
        s_xres, s_ln, s_ln2, s_wrt = sem("s_xres"), sem("s_ln"), sem("s_ln2"), sem("s_wrt")
        x1_ready, x1hi_ready, x1lo_ready = (sem(n) for n in ("x1_ready", "x1hi_ready", "x1lo_ready"))
        lg_ready, exp_ready, iota_ready = sem("lg_ready"), sem("exp_ready"), sem("iota_ready")
        hhi_ready, hlo_ready = sem("hhi_ready"), sem("hlo_ready")
        y_ready, moved_up = sem("y_ready"), sem("moved_up")
        head_stored = sem("head_stored")
        waits_met = sem("waits_met")

        w_in_v = w_in[0].rearrange("(t p) n -> p t n", p=128)
        w_ret_v = w_ret_o[0].rearrange("(t p) n -> p t n", p=128)
        w_conv_v = w_conv_o[0].rearrange("(t p) n -> p t n", p=128)
        w_out_v = w_out[0].rearrange("(t p) n -> p t n", p=128)

        nc_ok = ctx.enter_context(nc.allow_non_contiguous_dma("small vectors and slices of rows"))
        block = ctx.enter_context(nc.Block())

        def F_view(t, slot):
            return t[:, slot, :].rearrange("p (k n) -> p k n", k=KT)

        def T_view(t, slot):
            return t[:, slot, :].rearrange("p (k n) -> p k n", k=4)

        def samples(ap):
            return ap[:, 0:EL].rearrange("p (b w) -> p b w", b=NB)

        @block.sync
        def _(sp):
            sp.sem_inc(lo_ready, LEAD)
            sp.sem_inc(mlo_ready, MLEAD)
            for i in range(8):
                sp.sem_inc(evac[i], 1)
            sp.dma_start(tab[:], tables).then_inc(s_tab, 16)
            sp.dma_start(x_in[0:NS, 0, :], x_sample.rearrange("b i d -> (b i) d")).then_inc(s_x, 16)
            sp.dma_start(x_in[NS:NS + NM, 0, :], meta_tokens).then_inc(s_x, 16)
            sp.dma_start(x_in[NS + NM:TT, 0, :], x_prompt[0, 0:TT - NS - NM, :]).then_inc(s_x, 16)
            for t in range(1, NT):
                a = t * TT - NS - NM
                sp.dma_start(x_in[:, t, :], x_prompt[0, a:a + TT, :]).then_inc(s_x, 16)

            def unit(units, u, it, parts, view=F_view):
                c = units.idx(u, it)
                at_least(sp, lo_ready, c - 1 + LEAD)
                alone(sp, waits_met)
                slot = u % 2
                for a, b, src in parts:
                    sp.dma_start(view(raw, slot)[:, :, a:b], src).then_inc(raw_full[slot], 16)

            with sp.Fori(0, H) as h:
                for u, name in enumerate(("ub", "ua", "q", "k")):
                    unit(U_HEAD, u, h, [(0, 256, w_in_v[:, :, ds(h * 256 + OFF[name], 256)])])
                for j in range(2):
                    unit(U_HEAD, 4 + j, h, [(0, DV, w_in_v[:, 4 * j:4 * j + 4, ds(h * DV + OFF["v"], DV)])], T_view)
                for j in range(2):
                    unit(U_HEAD, 6 + j, h, [(0, 256, w_in_v[:, :, ds(h * DV + (OFF["g"] + 256 * j), 256)])])
                for j in range(2):
                    unit(U_HEAD, 8 + j, h, [(0, 512, w_ret_v[:, ds(h * 4, 4), 512 * j:512 * j + 512])], T_view)
            with sp.Fori(0, 4) as j:
                for u, name in enumerate(("mc", "mr")):
                    unit(U_GATE, u, j, [(0, 256, w_in_v[:, :, ds(j * 256 + OFF[name], 256)])])
            with sp.Fori(0, 2) as j:
                for u in range(2):
                    unit(U_CONV, u, j, [(0, 256, w_conv_v[:, :, ds(j * 512 + 256 * u, 256)])])
            for n in range(2):
                for half in range(2):
                    unit(U_WOUT, 2 * n + half, 0, [(0, 512, w_out_v[:, 4 * half:4 * half + 4, 512 * n:512 * n + 512])], T_view)

            sp.wait_ge(group_done, WOUT.done("w12"))
            sp.wait_ge(x1_ready, NT)
            sp.dma_start(ln2_bc[:, 0, :], ln2_g.to_broadcast([TT, D])).then_inc(s_ln2, 16)
            sp.dma_start(ln2_bc[:, 1, :], ln2_b.to_broadcast([TT, D])).then_inc(s_ln2, 16)
            with sp.Fori(0, NE) as e:
                for u in range(12):
                    c = U_MOE.idx(u, e)
                    at_least(sp, mlo_ready, c - (MR - 1) + MLEAD)
                    alone(sp, waits_met)
                    slot = u % MR
                    if u < 8:
                        src = (w_gate, w_up)[u % 2][0][ds(e, 1)].rearrange("e (t p) n -> p (e t) n", p=128)
                        sp.dma_start(F_view(mraw, slot), src[:, :, 256 * (u // 2):256 * (u // 2) + 256]).then_inc(mraw_full[slot], 16)
                    else:
                        n, half = divmod(u - 8, 2)
                        src = w_down[0][ds(e, 1)].rearrange("e (t p) n -> p (e t) n", p=128)
                        sp.dma_start(T_view(mraw, slot), src[:, 4 * half:4 * half + 4, 512 * n:512 * n + 512]).then_inc(mraw_full[slot], 16)

            for t in range(NT):
                sp.wait_ge(y_ready, t + 1)
                if t == 0:
                    sp.dma_start(y_sample.rearrange("b i d -> (b i) d"), y[0:NS, 0, :]).then_inc(out_sem, 16)
                    sp.dma_start(y_prompt[0, 0:TT - NS - NM, :], y[NS + NM:TT, 0, :]).then_inc(out_sem, 16)
                else:
                    a = t * TT - NS - NM
                    sp.dma_start(y_prompt[0, a:a + TT, :], y[:, t, :]).then_inc(out_sem, 16)
            sp.wait_ge(out_sem, 16 * (NT + 1))

        N_ROWS = 12

        @block.gpsimd
        def _(pool):
            def rows(dst, src):
                pool.dma_start(dst, src).then_inc(s_rows, 16)

            b_v = b_in[0].rearrange("(a p) -> a p", p=128)
            hj = lambda off, j: b_in[0, off:off + H * j * 128].rearrange("(h j p) -> j h p", h=H, j=j)
            rows(vrows[VUB:VUB + 2, :, :], hj(OFF["ub"], 2))
            rows(vrows[VUA:VUA + 2, :, :], hj(OFF["ua"], 2))
            rows(vrows[VG:VG + 4, :, :], hj(OFF["g"], 4))
            rows(vrows[VCB:VCB + 2, :, :], conv_b[0].rearrange("(h j p) -> j h p", h=H, j=2))
            for j in range(2):
                rows(vrows[VCW + j * CW:VCW + (j + 1) * CW, :, :],
                     conv_w[0].rearrange("w (h j p) -> j w h p", h=H, j=2)[j])
            rows(qkrows[:, :], b_in[0, 0:2 * D].rearrange("(a p) -> a p", p=256))
            for name, src in (("mc", b_v[OFF["mc"] // 128:OFF["mc"] // 128 + 8, :]),
                              ("mr", b_v[OFF["mr"] // 128:OFF["mr"] // 128 + 8, :]),
                              ("lng", conv_ln_g[0].rearrange("(a p) -> a p", p=128)),
                              ("lnb", conv_ln_b[0].rearrange("(a p) -> a p", p=128)),
                              ("bco", b_conv_o[0].rearrange("(a p) -> a p", p=128))):
                rows(v2rows[V2[name]:V2[name] + 8, :], src)
            pool.dma_start(wr_sb[:], w_router.rearrange("(t p) n -> p t n", p=128)).then_inc(s_wrt, 16)
            pool.dma_start(br_bc[:], b_router.rearrange("(a n) -> a n", a=1).to_broadcast([TT, NE])).then_inc(s_wrt, 16)
            pool.dma_start(new_conv_sample[0, :, 0:CW - 1 - NI, :], state_conv[0, :, NI:CW - 1, :]).then_inc(moved_up, 16)
            pool.wait_ge(group_done, PRE.done("vec2"))
            pool.sem_inc(head_stored, 1)
            with pool.Fori(0, H) as h:
                at_least(pool, group_done, HEAD.start(h))
                alone(pool, waits_met)
                pool.dma_start(hist[:, :, :], state_conv[0].rearrange("(a b) w c -> (b w) a c", a=2)[:, :, ds(h * 256, 256)]
                               ).then_inc(hist_full, 16)
                pool.dma_start(vb[:, :], b_in[0:1, ds(h * DV + OFF["v"], DV)].to_broadcast([TT, DV])).then_inc(vb_full, 16)
                pool.dma_start(dec[:, :], decay[ds(h, 1)].rearrange("h p n -> p (h n)")).then_inc(dec_full, 16)
                for b in range(NB):
                    pool.dma_start(st[:, b, :, :], state_ret[0, b][ds(h, 1)].rearrange("h (p t) n -> p (h t) n", t=2)
                                   ).then_inc(st_full[b], 16)
                pool.wait_ge(evac[HEAD.bank["uS"]], HEAD.used("uS", h) + 1)
                alone(pool, waits_met)
                for b in range(NB):
                    pool.dma_start(new_conv_sample[0, b, CW - 1 - NI:CW - 1, ds(h * 256, 256)],
                                   u_tok[b * NI:(b + 1) * NI, :]).then_inc(u_stored, 16)
                pool.wait_ge(evac[HEAD.bank["uP"]], HEAD.used("uP", h) + 1)
                alone(pool, waits_met)
                pool.dma_start(new_conv_prompt[0, 0, :, ds(h * 256, 256)], up_tok[:, :]).then_inc(u_stored, 16)
                for b in range(NB):
                    for p in range(2):
                        n = f"st{b}{p}"
                        pool.wait_ge(evac[HEAD.bank[n]], HEAD.used(n, h) + 1)
                        alone(pool, waits_met)
                    pool.dma_start(new_ret_sample[0, b][ds(h, 1)].rearrange("h (p t) n -> p (h t) n", t=2), st[:, b, :, :]
                                   ).then_inc(st_out[b], 16)
                pool.wait_ge(evac[HEAD.bank["ps1"]], HEAD.used("ps1", h) + 1)
                alone(pool, waits_met)
                pool.dma_start(new_ret_prompt[0, 0][ds(h, 1)].rearrange("h (p t) n -> p (h t) n", t=2), ps_out[:, :, :]
                               ).then_inc(ps_stored, 16)
                for b in range(NB):
                    pool.wait_ge(st_out[b], h * 16 + 16)
                    alone(pool, waits_met)
                pool.wait_ge(ps_stored, h * 16 + 16)
                alone(pool, waits_met)
                pool.wait_ge(u_stored, h * (16 * (NB + 1)) + 16 * (NB + 1))
                pool.sem_inc(head_stored, 1)
            pool.wait_ge(group_done, MEAN.start())
            pool.wait_ge(evac[HEAD.bank["wr7"]], HEAD.used("wr7", H - 1) + 1)
            pool.dma_start(x_tok[0:NS, 0, :], x_sample.rearrange("b i d -> (b i) d")).then_inc(s_xres, 16)
            pool.dma_start(x_tok[NS:NS + NM, 0, :], meta_tokens).then_inc(s_xres, 16)
            pool.dma_start(x_tok[NS + NM:TT, 0, :], x_prompt[0, 0:TT - NS - NM, :]).then_inc(s_xres, 16)
            for t in range(1, NT):
                a = t * TT - NS - NM
                pool.dma_start(x_tok[:, t, :], x_prompt[0, a:a + TT, :]).then_inc(s_xres, 16)
            pool.dma_start(ln_bc[:, 0, :], ln1_g.to_broadcast([TT, D])).then_inc(s_ln, 16)
            pool.dma_start(ln_bc[:, 1, :], ln1_b.to_broadcast([TT, D])).then_inc(s_ln, 16)
            pool.wait_ge(group_done, WOUT.done("w12"))
            pool.wait_ge(x1_ready, NT)
            for e in range(NE):
                i = pool.memset(iota_r[:, :, e:e + 1], float(NE - e))
            i.then_inc(iota_ready, 1)
            pool.wait_ge(moved_up, 16)

        @block.tensor
        def _(pe):
            def group(stage, name, it, mms, begin=True, m=128, n=512):
                for out, a, b, s, e in mms:
                    i = pe.matmul(out, a, b, start=s, stop=e)
                i.then_inc(group_done, 1)

            def room(stage, name, it):
                at_least(pe, evac[stage.bank[name]], stage.used(name, it))

            def split_ready(units, u, it):
                pe.wait_ge(lo_ready, units.idx(u, it) + (1 + LEAD))

            def three(out, w_h, w_l, x_h, x_l, first, last):
                return [(out, w_h, x_h, first, False), (out, w_h, x_l, False, False), (out, w_l, x_h, False, last)]

            def f_group(stage, name, it, wh, wl, cols, xh, xl, kts=KT):
                room(stage, name, it)
                out = bank[stage.bank[name]][:, 0:T]
                mms = []
                for k in range(kts):
                    mms += three(out, wh[:, k, cols], wl[:, k, cols], xh[:, k, :], xl[:, k, :], k == 0, k == kts - 1)
                group(stage, name, it, mms)

            def t_unit(stage, half, parts, finals, it, wh, wl, xh, xl):
                for t in range(NT):
                    name = finals[t]
                    if half == 0:
                        room(stage, name, it)
                    out = bank[stage.bank[name]][0:TT, :]
                    mms = []
                    for k in range(4):
                        kk = 4 * half + k
                        first, last = half == 0 and k == 0, half == 1 and k == 3
                        xs = slice(t * TT, (t + 1) * TT)
                        mms += [(out, xh[:, kk, xs], wh[:, k, :], first, False), (out, xh[:, kk, xs], wl[:, k, :], False, False),
                                (out, xl[:, kk, xs], wh[:, k, :], False, last)]
                    group(stage, name, it, mms)

            def turn(stage, name, it, parts):
                room(stage, name, it)
                alone(pe, waits_met)
                for out, in_, n in parts:
                    i = pe.transpose(out, in_, ident[0:n, 0:n])
                i.then_inc(group_done, 1)

            pe.wait_ge(s_tab, 16)
            pe.wait_ge(s_x, 16 * 5)
            for t in range(NT):
                for j in range(2):
                    n = f"xt{2 * t + j}"
                    b = bank[PRE.bank[n]]
                    turn(PRE, n, 0, [(b[:, i * TT:(i + 1) * TT], x_in[:, t, (4 * j + i) * 128:(4 * j + i + 1) * 128], TT) for i in range(4)])
            pe.wait_ge(s_rows, 16 * N_ROWS)
            b = bank[PRE.bank["vec"]]
            turn(PRE, "vec", 0, [(b[:, h * NV:(h + 1) * NV], vrows[:, h, :], NV) for h in range(H)])
            b = bank[PRE.bank["bqk"]]
            turn(PRE, "bqk", 0, [(b[:, 8 * p:8 * p + 8], qkrows[:, p:256:2], 8) for p in range(2)])
            b = bank[PRE.bank["vec2"]]
            turn(PRE, "vec2", 0, [(b[:, 0:40], v2rows[:, :], 40)])
            for n in [f"xt{i}" for i in range(6)]:
                pe.wait_ge(evac[PRE.bank[n]], PRE.used(n) + 1)

            with pe.Fori(0, H) as h:
                pe.wait_ge(hist_full, h * 16 + 16)
                for c in range(2):
                    b = bank[HEAD.bank[f"hist{c}"]]
                    turn(HEAD, f"hist{c}", h, [(b[:, a * 120:a * 120 + 120], hist[:, a, c * 128:(c + 1) * 128], 120) for a in range(2)])
                for u, name in enumerate(("ub", "ua", "q", "k")):
                    split_ready(U_HEAD, u, h)
                    wh, wl = F_view(hi, u % 2), F_view(lo, u % 2)
                    for m in range(2):
                        cols = slice(m * 128, (m + 1) * 128) if u < 2 else slice(m, 256, 2)
                        f_group(HEAD, f"{name}{m}", h, wh, wl, cols, xT_hi, xT_lo)
                for c in range(2):
                    pe.wait_ge(evac[HEAD.bank[f"ua{c}"]], HEAD.used(f"ua{c}", h) + 1)
                b = bank[HEAD.bank["uS"]]
                turn(HEAD, "uS", h, [(b[0:NS, c * 128:(c + 1) * 128], us[:, c, :], 128) for c in range(2)])
                b = bank[HEAD.bank["uP"]]
                turn(HEAD, "uP", h, [(b[0:CW - 1, c * 128:(c + 1) * 128], E[:, c, EXT - CW + 1:EXT], 128) for c in range(2)])
                for half in range(2):
                    split_ready(U_HEAD, 4 + half, h)
                    t_unit(HEAD, half, None, [f"v{t}" for t in range(NT)], h, T_view(hi, half), T_view(lo, half), xT_hi, xT_lo)
                pe.wait_ge(rope_ready, h * 4 + 4)
                for g, tiles in enumerate(((0, 1), (2,))):
                    b = bank[HEAD.bank[f"kt{g}"]]
                    turn(HEAD, f"kt{g}", h, [(b[0:TT, (2 * i + p) * 128:(2 * i + p + 1) * 128], kr[:, p, t * TT:(t + 1) * TT], 128)
                                             for i, t in enumerate(tiles) for p in range(2)])
                for i in range(NT):
                    name = f"att{i}"
                    room(HEAD, name, h)
                    out = bank[HEAD.bank[name]][0:TT, 0:ATT_W[i]]
                    group(HEAD, name, h, [(out, kr[:, p, i * TT:(i + 1) * TT], qr[:, p, i * TT:T], p == 0, p == 1) for p in range(2)])
                for j in range(2):
                    u = 6 + j
                    split_ready(U_HEAD, u, h)
                    for m in range(2):
                        f_group(HEAD, f"g{2 * j + m}", h, F_view(hi, u % 2), F_view(lo, u % 2), slice(m * 128, (m + 1) * 128), xT_hi, xT_lo)
                for t in range(NT):
                    pe.wait_ge(evac[HEAD.bank[f"v{t}"]], HEAD.used(f"v{t}", h) + 1)
                    pe.wait_ge(evac[HEAD.bank[f"att{t}"]], HEAD.used(f"att{t}", h) + 1)
                for t in range(NT):
                    name = f"o{t}"
                    room(HEAD, name, h)
                    out = bank[HEAD.bank[name]][0:TT, :]
                    mms = [(out, att[:, ATT_AT[i] + (t - i) * TT:ATT_AT[i] + (t - i + 1) * TT], v_tok[:, i, :], i == 0, i == t)
                           for i in range(t + 1)]
                    if t == 0:
                        for a, l, r, s, e in mms:
                            pe.matmul(a, l, r, start=s, stop=e)
                        pe.wait_ge(qdiag_ready, h * 2 + 2)
                        for b in range(NB):
                            pe.wait_ge(st_full[b], h * 16 + 16)
                        o64 = bank[HEAD.bank[name]][0:NS, :]
                        for b in range(NB):
                            for p in range(2):
                                i = pe.matmul(o64, qdiag[:, p, b * NS:(b + 1) * NS], st[:, b, p, :], start=False, stop=(b == NB - 1 and p == 1), skip_group_check=True)
                        i.then_inc(group_done, 1)
                    else:
                        group(HEAD, name, h, mms)
                pe.wait_ge(evac[HEAD.bank["kt0"]], HEAD.used("kt0", h) + 1)
                pe.wait_ge(evac[HEAD.bank["kt1"]], HEAD.used("kt1", h) + 1)
                for b in range(NB):
                    for p in range(2):
                        name = f"st{b}{p}"
                        room(HEAD, name, h)
                        group(HEAD, name, h, [(bank[HEAD.bank[name]][:, :], kds[:, b, p * 128:(p + 1) * 128], v_tok[0:NS, 0, :], True, True)])
                for p in range(2):
                    name = f"ps{p}"
                    room(HEAD, name, h)
                    group(HEAD, name, h, [(bank[HEAD.bank[name]][:, :], kdp[:, t, p * 128:(p + 1) * 128], v_tok[:, t, :], t == 0, t == NT - 1) for t in range(NT)])
                for t in range(NT):
                    pe.wait_ge(evac[HEAD.bank[f"o{t}"]], HEAD.used(f"o{t}", h) + 1)
                    b = bank[HEAD.bank[f"oT{t}"]]
                    turn(HEAD, f"oT{t}", h, [(b[:, j * TT:(j + 1) * TT], o_tok[:, t, j * 128:(j + 1) * 128], TT) for j in range(4)])
                pe.wait_ge(sglo_ready, h * NT + NT)
                for j in range(2):
                    split_ready(U_HEAD, 8 + j, h)
                    for m in range(4):
                        f_group(HEAD, f"wr{4 * j + m}", h, T_view(hi, j), T_view(lo, j), slice(m * 128, (m + 1) * 128), sg_hi, sg_lo, 4)

            ones = tab[:, TB["mean"][0]:TB["mean"][1]]
            pe.wait_ge(evac[HEAD.bank["wr7"]], HEAD.used("wr7", H - 1) + 1)
            room(MEAN, "mean", 0)
            group(MEAN, "mean", 0, [(bank[MEAN.bank["mean"]][:, 0:T], ones, cT[:, k, :], k == 0, k == KT - 1) for k in range(KT)])
            with pe.Fori(0, 4) as j:
                for u, name in enumerate(("mc", "mr")):
                    split_ready(U_GATE, u, j)
                    for m in range(2):
                        f_group(GATE, f"{name}{m}", j, F_view(hi, u), F_view(lo, u), slice(m * 128, (m + 1) * 128), xT_hi, xT_lo)
            pe.wait_ge(csq_ready, 1)
            room(VAR, "var", 0)
            group(VAR, "var", 0, [(bank[VAR.bank["var"]][:, 0:T], ones, csq[:, k, :], k == 0, k == KT - 1) for k in range(KT)])
            pe.wait_ge(clo_ready, 1)
            with pe.Fori(0, 2) as j:
                for u in range(2):
                    split_ready(U_CONV, u, j)
                    for m in range(2):
                        f_group(CONV, f"c{2 * u + m}", j, F_view(hi, u), F_view(lo, u), slice(m * 128, (m + 1) * 128), c_hi, c_lo)
            pe.wait_ge(mlo_done, 1)
            for n in range(2):
                for half in range(2):
                    split_ready(U_WOUT, 2 * n + half, 0)
                    t_unit(WOUT, half, None, [f"w{n}{t}" for t in range(NT)], 0, T_view(hi, half), T_view(lo, half), m_hi, m_lo)
            for t in range(NT):
                pe.wait_ge(x1_ready, t + 1)
                for j in range(2):
                    n = f"xt{2 * t + j}"
                    b = bank[X1T.bank[n]]
                    turn(X1T, n, 0, [(b[:, i * TT:(i + 1) * TT], x1[:, t, (4 * j + i) * 128:(4 * j + i + 1) * 128], TT) for i in range(4)])
            for n in range(6):
                pe.wait_ge(evac[X1T.bank[f"xt{n}"]], X1T.used(f"xt{n}") + 1)
            pe.wait_ge(s_wrt, 32)
            room(X1T, "log", 0)
            out = bank[X1T.bank["log"]]
            for t in range(NT):
                for k in range(KT):
                    i = pe.matmul(out[0:TT, t * NE:(t + 1) * NE], x1T_f[:, k, t * TT:(t + 1) * TT], wr_sb[:, k, :], start=(k == 0), stop=(k == KT - 1))
            i.then_inc(group_done, 1)
            pe.wait_ge(x1lo_ready, 6)
            with pe.Fori(0, NE) as e:
                for u in range(12):
                    pe.wait_ge(mlo_ready, U_MOE.idx(u, e) + (1 + MLEAD))
                    s = u % MH
                    if u < 8:
                        for m in range(2):
                            f_group(MOE, f"{'gu'[u % 2]}{2 * (u // 2) + m}", e, F_view(mhi, s), F_view(mlo, s), slice(m * 128, (m + 1) * 128), x1T_hi, x1T_lo)
                    else:
                        n, half = divmod(u - 8, 2)
                        if u == 8:
                            pe.wait_ge(hlo_ready, e * 4 + 4)
                        t_unit(MOE, half, None, [f"d{n}{t}" for t in range(NT)], e, T_view(mhi, s), T_view(mlo, s), h_hi, h_lo)

        def split_hi(act, units, stage, u, it, R, RH, src, dst, full, ready):
            slot, hslot = u % R, u % RH
            act.wait_ge(full[slot], (it * (units.n // R) + ((units.base + u) // R + 1)) * 16)
            if u >= RH:
                act.wait_ge(group_done, stage.done(units.last[u - RH], it))
            else:
                act.wait_ge(group_done, stage.start(it) - sum(units.tail[:RH - 1 - u]))
            act.activation(dst[:, hslot, :], src[:, slot, :], ACT.Copy).then_inc(ready, 1)

        def split_lo(dve, units, u, it, R, RH, src, h, l, hready, lready):
            dve.wait_ge(hready, units.idx(u, it) + 1)
            dve.tensor_tensor(l[:, u % RH, :], src[:, u % R, :], h[:, u % RH, :].bitcast(f32), ALU.subtract).then_inc(lready, 1)

        def took(stage, name, it=0):
            return evac[stage.bank[name]], stage.used(name, it) + 1

        @block.scalar
        def _(act):
            def S(units, stage, u, it):
                split_hi(act, units, stage, u, it, 2, 2, raw, hi, raw_full, hi_ready)

            def SM(u, it):
                split_hi(act, U_MOE, MOE, u, it, MR, MH, mraw, mhi, mraw_full, mhi_ready)

            def full(stage, name, it=0):
                act.wait_ge(group_done, stage.done(name, it))
                return bank[stage.bank[name]], evac[stage.bank[name]]

            for i in range(6):
                b, e = full(PRE, f"xt{i}")
                t, j = divmod(i, 2)
                act.activation(xT_hi[:, 4 * j:4 * j + 4, t * TT:(t + 1) * TT], b[:, 0:4 * TT].rearrange("p (k n) -> p k n", k=4), ACT.Copy).then_inc(s_xhi, 1)
            b, e = full(PRE, "vec")
            act.activation(vec[:, :, 0:NV], b[:, 0:H * NV].rearrange("p (h n) -> p h n", h=H), ACT.Copy).then_inc(e, 1)
            b, e = full(PRE, "bqk")
            for p in range(2):
                i = act.activation(vec[:, :, VQK:VQK + 4].rearrange("p h (q r) -> p r q h", r=2)[:, p],
                                   b[:, 8 * p:8 * p + 8].rearrange("p (q h) -> p q h", q=2), ACT.Copy)
            i.then_inc(e, 1)
            b, e = full(PRE, "vec2")
            act.activation(vec2[:, :], b[:, 0:40], ACT.Copy).then_inc(e, 1)

            with act.Fori(0, H) as h:
                S(U_HEAD, HEAD, 0, h)
                S(U_HEAD, HEAD, 1, h)
                act.wait_ge(hv_ready, h * 2 + 2)
                for c in range(2):
                    b, e = full(HEAD, f"hist{c}", h)
                    act.activation(samples(E[:, c, :])[:, :, 0:CW - 1], b[:, 0:240].rearrange("p (b w) -> p b w", b=NB), ACT.Copy).then_inc(e, 1)
                for c in range(2):
                    b, e = full(HEAD, f"ub{c}", h)
                    act.activation(sub[:, c, :], b[:, 0:T], ACT.Sigmoid, bias=hv[:, VUB + c:VUB + c + 1]).then_inc(e, 1)
                for u in (2, 3, 4, 5):
                    S(U_HEAD, HEAD, u, h)
                act.wait_ge(head_stored, h + 1)
                b, e = full(HEAD, "uS", h)
                act.activation(u_tok[:, :], b[0:NS, 0:256], ACT.Copy).then_inc(e, 1)
                b, e = full(HEAD, "uP", h)
                act.activation(up_tok[:, :], b[0:CW - 1, 0:256], ACT.Copy).then_inc(e, 1)
                S(U_HEAD, HEAD, 6, h)
                S(U_HEAD, HEAD, 7, h)
                b, e = full(HEAD, "kt0", h)
                for t in range(2):
                    act.activation(kdp[:, t, :], b[0:TT, t * 256:(t + 1) * 256], ACT.Copy, scale=hs[0:TT, HKP + t:HKP + t + 1])
                for s in range(NB):
                    i = act.activation(kds[:, s, :], b[0:NS, 0:256], ACT.Copy, scale=hs[0:NS, HKS + s:HKS + s + 1])
                i.then_inc(e, 1)
                b, e = full(HEAD, "kt1", h)
                act.activation(kdp[:, 2, :], b[0:TT, 0:256], ACT.Copy, scale=hs[0:TT, HKP + 2:HKP + 3]).then_inc(e, 1)
                act.wait_ge(rope_ready, h * 4 + 4)
                for j in range(2):
                    for m in range(2 * j, 2 * j + 2):
                        b, e = full(HEAD, f"g{m}", h)
                        act.activation(rt[:, m, :], b[:, 0:T], ACT.Silu, bias=hv[:, VG + m:VG + m + 1]).then_inc(e, 1)
                    S(U_HEAD, HEAD, 8 + j, h)
                act.wait_ge(rv_ready, h + 1)
                act.activation(rs[:, 1, :], rs[:, 0, :], ACT.Sqrt).then_inc(rstd_done, 1)
                for p in range(2):
                    b, e = full(HEAD, f"ps{p}", h)
                    act.activation(ps_out[:, p, :], b[:, :], ACT.Copy).then_inc(e, 1)
                for t in range(NT):
                    act.wait_ge(*took(HEAD, f"oT{t}", h))
                    act.activation(sg_hi[:, :, t * TT:(t + 1) * TT], sg_f[:, :, :], ACT.Copy).then_inc(sghi_ready, 1)

            act.wait_ge(head_stored, H + 1)
            act.wait_ge(csub_ready, 8)
            act.activation(csq[:, :, :], cT[:, :, :], ACT.Square).then_inc(csq_ready, 1)
            for j in range(4):
                for u, (name, g) in enumerate((("mc", gc), ("mr", gr))):
                    S(U_GATE, GATE, u, j)
                for u, (name, g) in enumerate((("mc", gc), ("mr", gr))):
                    for m in range(2):
                        b, e = full(GATE, f"{name}{m}", j)
                        k = 2 * j + m
                        act.activation(g[:, k, :], b[:, 0:T], ACT.Sigmoid, bias=vec2[:, V2[name] + k:V2[name] + k + 1]).then_inc(e, 1)
            S(U_CONV, CONV, 0, 0)
            act.wait_ge(rv_ready, H + 1)
            act.activation(rstd_c[:, :], rstd_c[:, :], ACT.Sqrt).then_inc(rstd_done, 1)
            for k in range(KT):
                act.wait_ge(cn_ready, k + 1)
                act.activation(cT[:, k, :], cT[:, k, :], ACT.Silu, scale=vec2[:, V2["lng"] + k:V2["lng"] + k + 1],
                               bias=vec2[:, V2["lnb"] + k:V2["lnb"] + k + 1]).then_inc(csilu_ready, 1)
            act.wait_ge(csilu_ready, KT)
            act.activation(c_hi[:, :, :], cT[:, :, :], ACT.Copy).then_inc(chi_ready, 1)
            S(U_CONV, CONV, 1, 0)
            S(U_CONV, CONV, 0, 1)
            S(U_CONV, CONV, 1, 1)
            S(U_WOUT, WOUT, 0, 0)
            S(U_WOUT, WOUT, 1, 0)
            act.wait_ge(mf_ready, 1)
            act.activation(m_hi[:, :, :], gc[:, :, :], ACT.Copy).then_inc(mhi_done, 1)
            S(U_WOUT, WOUT, 2, 0)
            S(U_WOUT, WOUT, 3, 0)
            for t in range(NT):
                act.wait_ge(rv_ready, H + 2 + t)
                act.activation(lnmv[:, t, 3:4], lnmv[:, t, 2:3], ACT.Sqrt).then_inc(rstd_done, 1)
            for i in range(6):
                t, j = divmod(i, 2)
                act.wait_ge(*took(X1T, f"xt{i}"))
                act.activation(x1T_hi[:, 4 * j:4 * j + 4, t * TT:(t + 1) * TT], x1T_f[:, 4 * j:4 * j + 4, t * TT:(t + 1) * TT], ACT.Copy).then_inc(x1hi_ready, 1)
            act.wait_ge(lg_ready, 1)
            act.activation(gt[:, 1, :, :], gt[:, 0, :, :], ACT.Exp).then_inc(exp_ready, 1)

            with act.Fori(0, NE) as e_:
                for u in range(14):
                    if u < 12:
                        SM(u, e_)
                    v = u - 2
                    if v < 0 or v >= 8:
                        continue
                    j = v // 2
                    if v % 2 == 0:
                        for m in range(2):
                            b, e = full(MOE, f"g{2 * j + m}", e_)
                            act.activation(sgm[:, j % 2, m, :], b[:, 0:T], ACT.Silu).then_inc(e, 1)
                    else:
                        for m in range(2):
                            act.wait_ge(*took(MOE, f"u{2 * j + m}", e_))
                        act.activation(h_hi[:, 2 * j:2 * j + 2, :], h_f[:, :, :], ACT.Copy).then_inc(hhi_ready, 1)
            for t in range(NT):
                act.wait_ge(rv_ready, H + 2 + NT + t)
                act.activation(mmv[:, t, 3:4], mmv[:, t, 2:3], ACT.Sqrt).then_inc(rstd_done, 1)

        @block.vector
        def _(dve):
            step = {"base": 0, "it": 0, "n": 0, "local": 0}

            def count(ins):
                ins.then_inc(dve_step, 1)
                step["local"] += 1
                return step["it"] * step["n"] + (step["base"] + step["local"])

            def link(ins):
                dve.wait_ge(dve_step, count(ins))

            def turns(it, n):
                step.update(base=step["base"] + step["local"], it=it, n=n, local=0)

            def turns_end(times):
                assert step["local"] == step["n"], step
                step.update(base=step["base"] + step["n"] * times, it=0, n=0, local=0)

            def L(units, u, it):
                split_lo(dve, units, u, it, 2, 2, raw, hi, lo, hi_ready, lo_ready)

            def LM(u, it):
                split_lo(dve, U_MOE, u, it, MR, MH, mraw, mhi, mlo, mhi_ready, mlo_ready)

            def full(stage, name, it=0):
                dve.wait_ge(group_done, stage.done(name, it))
                return bank[stage.bank[name]], evac[stage.bank[name]]

            i = dve.memset(E[:, :, EL:EL + CW - 1], 0.0)
            count(i)
            count(dve.memset(retT[:, :, :], 0.0))
            count(dve.memset(qdiag[:, :, :], 0.0))
            for i in range(6):
                b, e = full(PRE, f"xt{i}")
                t, j = divmod(i, 2)
                a = (slice(None), slice(4 * j, 4 * j + 4), slice(t * TT, (t + 1) * TT))
                dve.wait_ge(s_xhi, i + 1)
                dve.tensor_tensor(xT_lo[a], b[:, 0:4 * TT].rearrange("p (k n) -> p k n", k=4), xT_hi[a].bitcast(f32), ALU.subtract).then_inc(e, 1)
            dve.wait_ge(s_tab, 16)
            for n in ("vec", "bqk", "vec2"):
                dve.wait_ge(*took(PRE, n))
            dve.wait_ge(dve_step, 3)

            def conv(c, h):
                out = cT[:, ds(h * 2 + c, 1), :].rearrange("p a n -> p (a n)")
                parts = [(out[:, NS:T], lambda w: E[:, c, EL + w:EL + w + NP]),
                         (out[:, 0:NS].rearrange("p (b i) -> p b i", b=NB), lambda w: samples(E[:, c, :])[:, :, w:w + NI])]
                last = [None, None]
                for w in range(CW):
                    tap = hv[:, VCW + c * CW + w:VCW + c * CW + w + 1]
                    for q, (o, src) in enumerate(parts):
                        if w == 0:
                            ins = dve.tensor_scalar(o, src(w), tap, hv[:, VCB + c:VCB + c + 1], ALU.mult, ALU.add)
                        else:
                            dve.wait_ge(dve_step, last[q])
                            ins = dve.scalar_tensor_tensor(o, src(w), tap, o, ALU.mult, ALU.add)
                        last[q] = count(ins)
                dve.wait_ge(dve_step, last[1])

            with dve.Fori(0, H) as h:
                turns(h, 4 * CW + 2 * NT + 1)
                dve.tensor_copy(hv[:, :], vec[:, ds(h, 1), :].rearrange("p a n -> p (a n)")).then_inc(hv_ready, 1)
                dve.tensor_copy(hs[:, :], tab[:, ds(h * HS + TB["heads"][0], HS)]).then_inc(hv_ready, 1)
                dve.wait_ge(hv_ready, h * 2 + 2)
                for u in range(3):
                    L(U_HEAD, u, h)
                for c in range(2):
                    b, e = full(HEAD, f"ua{c}", h)
                    dve.wait_ge(*took(HEAD, f"ub{c}", h))
                    bias = hv[:, VUA + c:VUA + c + 1]
                    dve.scalar_tensor_tensor(samples(E[:, c, :])[:, :, CW - 1:CW - 1 + NI], b[:, 0:NS].rearrange("p (b i) -> p b i", b=NB),
                                             bias, sub[:, c, 0:NS].rearrange("p (b i) -> p b i", b=NB), ALU.add, ALU.mult)
                    dve.scalar_tensor_tensor(us[:, c, :], b[:, 0:NS], bias, sub[:, c, 0:NS], ALU.add, ALU.mult)
                    dve.scalar_tensor_tensor(E[:, c, EL + CW - 1:EXT], b[:, NS:T], bias, sub[:, c, NS:T], ALU.add, ALU.mult).then_inc(e, 1)
                L(U_HEAD, 3, h)
                cos, sin = tab[:, TB["cos"][0]:TB["cos"][1]], tab[:, TB["sin"][0]:TB["sin"][1]]
                for n, (name, r) in enumerate((("q", qr), ("k", kr))):
                    for m, (f0, f1) in enumerate(((cos, sin), (sin, cos))):
                        b, e = full(HEAD, f"{name}{m}", h)
                        bias = hv[:, VQK + 2 * n + m:VQK + 2 * n + m + 1]
                        dve.scalar_tensor_tensor(rt[:, 2 * m, :], b[:, 0:T], bias, f0, ALU.add, ALU.mult)
                        dve.scalar_tensor_tensor(rt[:, 2 * m + 1, :], b[:, 0:T], bias, f1, ALU.add, ALU.mult).then_inc(e, 1)
                    for m in range(2):
                        dve.wait_ge(*took(HEAD, f"{name}{m}", h))
                    dve.tensor_tensor(r[:, 0, :], rt[:, 0, :], rt[:, 2, :], ALU.subtract).then_inc(rope_ready, 1)
                    dve.tensor_tensor(r[:, 1, :], rt[:, 1, :], rt[:, 3, :], ALU.add).then_inc(rope_ready, 1)
                    dve.wait_ge(rope_ready, h * 4 + (2 * n + 2))
                    L(U_HEAD, 4 + n, h)
                for p in range(2):
                    dve.tensor_tensor(qdiag[:, p, :].rearrange("p (b x) -> p b x", b=NB)[:, :, 0:NI],
                                      qr[:, p, 0:NS].rearrange("p (b i) -> p b i", b=NB),
                                      hs[:, HQ:HQ + NS].rearrange("p (b i) -> p b i", b=NB), ALU.mult).then_inc(qdiag_ready, 1)
                for c in range(2):
                    dve.wait_ge(*took(HEAD, f"hist{c}", h))
                    dve.wait_ge(*took(HEAD, f"ua{c}", h))
                conv(0, h)
                dve.wait_ge(vb_full, h * 16 + 16)
                for t in range(NT):
                    b, e = full(HEAD, f"v{t}", h)
                    dve.tensor_tensor(v_tok[:, t, :], b[0:TT, :], vb[:, :], ALU.add).then_inc(e, 1)
                L(U_HEAD, 6, h)
                L(U_HEAD, 7, h)
                dve.wait_ge(dec_full, h * 16 + 16)
                for t in range(NT):
                    b, e = full(HEAD, f"att{t}", h)
                    a = slice(ATT_AT[t], ATT_AT[t] + ATT_W[t])
                    dve.tensor_tensor(att[:, a], b[0:TT, 0:ATT_W[t]], dec[:, a], ALU.mult).then_inc(e, 1)
                conv(1, h)
                L(U_HEAD, 8, h)
                L(U_HEAD, 9, h)
                for t in range(NT):
                    b, e = full(HEAD, f"o{t}", h)
                    link(dve.bn_stats(stats[:, t, :], b[0:TT, :]))
                    alone(dve, waits_met)
                    link(dve.bn_aggr(mv[:, t, :], stats[:, t, :]))
                link(dve.tensor_scalar(rs[:, 0, :], mv[:, :, 1], EPS, None, ALU.add))
                dve.reciprocal(rs[:, 0, :], rs[:, 0, :]).then_inc(rv_ready, 1)
                dve.wait_ge(rstd_done, h + 1)
                for t in range(NT):
                    b, e = full(HEAD, f"o{t}", h)
                    dve.tensor_scalar(o_tok[:, t, :], b[0:TT, :], mv[:, t, 0:1], rs[:, 1, t:t + 1], ALU.subtract, ALU.mult).then_inc(e, 1)
                for s in range(NB):
                    for p in range(2):
                        b, e = full(HEAD, f"st{s}{p}", h)
                        dve.scalar_tensor_tensor(st[:, s, p, :], st[:, s, p, :], hs[:, HGAM:HGAM + 1], b[:, :], ALU.mult, ALU.add).then_inc(e, 1)
                for m in range(4):
                    dve.wait_ge(*took(HEAD, f"g{m}", h))
                for t in range(NT):
                    cols = slice(t * TT, (t + 1) * TT)
                    b, e = full(HEAD, f"oT{t}", h)
                    dve.tensor_tensor(sg_f[:, :, :], b[:, 0:4 * TT].rearrange("p (j n) -> p j n", j=4), rt[:, :, cols], ALU.mult).then_inc(e, 1)
                    dve.wait_ge(sghi_ready, h * NT + (t + 1))
                    dve.tensor_tensor(sg_lo[:, :, cols], sg_f[:, :, :], sg_hi[:, :, cols].bitcast(f32), ALU.subtract).then_inc(sglo_ready, 1)
                    dve.wait_ge(sglo_ready, h * NT + (t + 1))
                for m in range(8):
                    b, e = full(HEAD, f"wr{m}", h)
                    dve.tensor_tensor(retT[:, m, :], b[:, 0:T], retT[:, m, :], ALU.add).then_inc(e, 1)
                dve.wait_ge(*took(HEAD, "wr7", h))
                turns_end(H)

            b, e = full(MEAN, "mean")
            for k in range(KT):
                dve.tensor_tensor(cT[:, k, :], cT[:, k, :], b[:, 0:T], ALU.subtract).then_inc(csub_ready, 1)
            dve.wait_ge(csub_ready, KT)
            dve.tensor_copy(rstd_c[:, 0:1], b[:, 0:1]).then_inc(e, 1)
            for j in range(4):
                for u in range(2):
                    L(U_GATE, u, j)
            for n in ("mc0", "mc1", "mr0", "mr1"):
                dve.wait_ge(*took(GATE, n, 3))
            link(dve.tensor_tensor(retT[:, :, :], retT[:, :, :], gr[:, :, :], ALU.mult))
            b, e = full(VAR, "var")
            dve.tensor_scalar(rstd_c[:, :], b[:, 0:T], EPS, None, ALU.add).then_inc(e, 1)
            dve.wait_ge(*took(VAR, "var"))
            dve.reciprocal(rstd_c[:, :], rstd_c[:, :]).then_inc(rv_ready, 1)
            dve.wait_ge(rstd_done, H + 1)
            for k in range(KT):
                dve.tensor_tensor(cT[:, k, :], cT[:, k, :], rstd_c[:, :], ALU.mult).then_inc(cn_ready, 1)
            L(U_CONV, 0, 0)
            dve.wait_ge(chi_ready, 1)
            dve.tensor_tensor(c_lo[:, :, :], cT[:, :, :], c_hi[:, :, :].bitcast(f32), ALU.subtract).then_inc(clo_ready, 1)
            L(U_CONV, 1, 0)
            for j in range(2):
                if j:
                    L(U_CONV, 0, 1)
                for u in range(2):
                    if u == 1 and j:
                        L(U_CONV, 1, 1)
                    for m in range(2):
                        k = 4 * j + 2 * u + m
                        b, e = full(CONV, f"c{2 * u + m}", j)
                        dve.scalar_tensor_tensor(gc[:, k, :], b[:, 0:T], vec2[:, V2["bco"] + k:V2["bco"] + k + 1], gc[:, k, :], ALU.add, ALU.mult).then_inc(e, 1)
            L(U_WOUT, 0, 0)
            L(U_WOUT, 1, 0)
            for m in range(4):
                dve.wait_ge(*took(CONV, f"c{m}", 1))
            dve.tensor_tensor(gc[:, :, :], gc[:, :, :], retT[:, :, :], ALU.add).then_inc(mf_ready, 1)
            dve.wait_ge(mf_ready, 1)
            dve.wait_ge(mhi_done, 1)
            dve.tensor_tensor(m_lo[:, :, :], gc[:, :, :], m_hi[:, :, :].bitcast(f32), ALU.subtract).then_inc(mlo_done, 1)
            L(U_WOUT, 2, 0)
            L(U_WOUT, 3, 0)
            dve.wait_ge(s_xres, 16 * 5)
            dve.wait_ge(s_ln, 32)

            def layernorm(x, t, bc, mst_, mmv_, k, ready):
                for n in range(2):
                    link(dve.bn_stats(mst_[:, t, 6 * n:6 * n + 6], x[:, t, 512 * n:512 * n + 512]))
                link(dve.bn_aggr(mmv_[:, t, 0:2], mst_[:, t, 0:12]))
                link(dve.tensor_scalar(mmv_[:, t, 2:3], mmv_[:, t, 1:2], EPS, None, ALU.add))
                dve.reciprocal(mmv_[:, t, 2:3], mmv_[:, t, 2:3]).then_inc(rv_ready, 1)
                dve.wait_ge(rstd_done, k + t + 1)
                link(dve.tensor_scalar(x[:, t, :], x[:, t, :], mmv_[:, t, 0:1], mmv_[:, t, 3:4], ALU.subtract, ALU.mult))
                link(dve.tensor_tensor(x[:, t, :], x[:, t, :], bc[:, 0, :], ALU.mult))
                dve.tensor_tensor(x[:, t, :], x[:, t, :], bc[:, 1, :], ALU.add).then_inc(ready, 1)

            for n in range(2):
                for t in range(NT):
                    b, e = full(WOUT, f"w{n}{t}")
                    cols = slice(512 * n, 512 * n + 512)
                    dve.scalar_tensor_tensor(x1[:, t, cols], x_tok[:, t, cols], ALPHA, b[0:TT, :], ALU.mult, ALU.add).then_inc(e, 1)
                    if n:
                        for q in range(2):
                            dve.wait_ge(*took(WOUT, f"w{q}{t}"))
                        layernorm(x1, t, ln_bc, lnst, lnmv, H + 1, x1_ready)
            dve.wait_ge(x1_ready, NT)
            for i in range(6):
                t, j = divmod(i, 2)
                b, e = full(X1T, f"xt{i}")
                dve.tensor_copy(x1T_f[:, 4 * j:4 * j + 4, t * TT:(t + 1) * TT], b[:, 0:4 * TT].rearrange("p (k n) -> p k n", k=4)).then_inc(e, 1)
            for i in range(6):
                t, j = divmod(i, 2)
                a = (slice(None), slice(4 * j, 4 * j + 4), slice(t * TT, (t + 1) * TT))
                dve.wait_ge(x1hi_ready, i + 1)
                dve.tensor_tensor(x1T_lo[a], x1T_f[a], x1T_hi[a].bitcast(f32), ALU.subtract).then_inc(x1lo_ready, 1)
            count(dve.tensor_scalar(y[:, :, :], x1[:, :, :], ALPHA, None, ALU.mult))

            def wide(x):
                return x.unsqueeze(2).to_broadcast([TT, NT, NE])

            b, e = full(X1T, "log")
            for t in range(NT):
                i = dve.tensor_tensor(gt[:, 0, t, :], b[0:TT, t * NE:(t + 1) * NE], br_bc[:, :], ALU.add)
                if t < NT - 1:
                    count(i)
            i.then_inc(e, 1)
            dve.wait_ge(*took(X1T, "log"))
            link(dve.tensor_reduce(gs[:, 0, :], gt[:, 0, :, :], AX.X, ALU.max))
            dve.tensor_tensor(gt[:, 0, :, :], gt[:, 0, :, :], wide(gs[:, 0, :]), ALU.subtract).then_inc(lg_ready, 1)
            dve.wait_ge(exp_ready, 1)
            dve.wait_ge(iota_ready, 1)
            P = gt[:, 1, :, :]
            link(dve.tensor_reduce(gs[:, 1, :], P, AX.X, ALU.add))
            link(dve.reciprocal(gs[:, 2, :], gs[:, 1, :]))
            link(dve.tensor_tensor(P, P, wide(gs[:, 2, :]), ALU.mult))
            link(dve.tensor_reduce(gs[:, 3, :], P, AX.X, ALU.max))
            link(dve.tensor_tensor(gt[:, 2, :, :], P, wide(gs[:, 3, :]), ALU.is_equal))
            link(dve.tensor_tensor(gt[:, 2, :, :], gt[:, 2, :, :], iota_r[:, :, :], ALU.mult))
            link(dve.tensor_reduce(gs[:, 4, :], gt[:, 2, :, :], AX.X, ALU.max))
            link(dve.tensor_tensor(gt[:, 3, :, :], iota_r[:, :, :], wide(gs[:, 4, :]), ALU.is_equal))
            link(dve.tensor_reduce(gg[:, :, :], gt[:, 3, :, :].rearrange("p t (g e) -> p t g e", g=NG), AX.X, ALU.max))
            for q in range(EG):
                link(dve.tensor_tensor(gt[:, 4, :, q:NE:EG], gg[:, :, :], gt[:, 3, :, q:NE:EG], ALU.subtract))
            link(dve.tensor_tensor(gt[:, 5, :, :], P, gt[:, 4, :, :], ALU.mult))
            link(dve.tensor_reduce(gs[:, 5, :], gt[:, 5, :, :], AX.X, ALU.max))
            link(dve.tensor_tensor(gt[:, 6, :, :], gt[:, 5, :, :], wide(gs[:, 5, :]), ALU.is_equal))
            link(dve.tensor_tensor(gt[:, 6, :, :], gt[:, 6, :, :], gt[:, 4, :, :], ALU.mult))
            link(dve.tensor_tensor(gt[:, 6, :, :], gt[:, 6, :, :], iota_r[:, :, :], ALU.mult))
            link(dve.tensor_reduce(gs[:, 6, :], gt[:, 6, :, :], AX.X, ALU.max))
            link(dve.tensor_tensor(gt[:, 6, :, :], iota_r[:, :, :], wide(gs[:, 6, :]), ALU.is_equal))
            link(dve.tensor_tensor(gs[:, 7, :], gs[:, 3, :], gs[:, 5, :], ALU.add))
            link(dve.reciprocal(gs[:, 7, :], gs[:, 7, :]))
            link(dve.tensor_tensor(gs[:, 3, :], gs[:, 3, :], gs[:, 7, :], ALU.mult))
            link(dve.tensor_tensor(gs[:, 5, :], gs[:, 5, :], gs[:, 7, :], ALU.mult))
            link(dve.tensor_tensor(gt[:, 3, :, :], gt[:, 3, :, :], wide(gs[:, 3, :]), ALU.mult))
            link(dve.tensor_tensor(gt[:, 6, :, :], gt[:, 6, :, :], wide(gs[:, 5, :]), ALU.mult))
            link(dve.tensor_tensor(gates[:, :, :], gt[:, 3, :, :], gt[:, 6, :, :], ALU.add))

            with dve.Fori(0, NE) as e_:
                turns(e_, 1)
                at_least(dve, evac[MOE.bank["d12"]], MOE.emptied("d12", e_))
                link(dve.tensor_copy(g_e[:, :], gates[:, :, ds(e_, 1)].rearrange("p t a -> p (t a)")))
                for u in range(14):
                    if u < 12:
                        LM(u, e_)
                    v = u - 2
                    if v < 0:
                        continue
                    if v < 8 and v % 2:
                        j = v // 2
                        for m in range(2):
                            b, e = full(MOE, f"u{2 * j + m}", e_)
                            dve.wait_ge(*took(MOE, f"g{2 * j + m}", e_))
                            dve.tensor_tensor(h_f[:, m, :], b[:, 0:T], sgm[:, j % 2, m, :], ALU.mult).then_inc(e, 1)
                        for m in range(2):
                            dve.wait_ge(*took(MOE, f"u{2 * j + m}", e_))
                        dve.wait_ge(hhi_ready, e_ * 4 + (j + 1))
                        dve.tensor_tensor(h_lo[:, 2 * j:2 * j + 2, :], h_f[:, :, :], h_hi[:, 2 * j:2 * j + 2, :].bitcast(f32), ALU.subtract).then_inc(hlo_ready, 1)
                        dve.wait_ge(hlo_ready, e_ * 4 + (j + 1))
                    elif v in (9, 11):
                        n = (v - 8) // 2
                        for t in range(NT):
                            b, e = full(MOE, f"d{n}{t}", e_)
                            o = y[:, t, 512 * n:512 * n + 512]
                            at_least(dve, e, MOE.used(f"d{n}{t}", e_))
                            dve.scalar_tensor_tensor(o, b[0:TT, :], g_e[:, t:t + 1], o, ALU.mult, ALU.add).then_inc(e, 1)
                turns_end(NE)
            dve.wait_ge(s_ln2, 32)
            for n in range(2):
                for t in range(NT):
                    dve.wait_ge(*took(MOE, f"d{n}{t}", NE - 1))
            for t in range(NT):
                layernorm(y, t, ln2_bc, mst, mmv, H + 1 + NT, y_ready)


_INS = ["x_prompt", "x_sample", "state_ret", "state_conv", "meta_tokens", "w_in", "b_in", "w_ret_o", "conv_w", "conv_b",
        "conv_ln_g", "conv_ln_b", "w_conv_o", "b_conv_o", "w_out", "ln1_g", "ln1_b", "ln2_g", "ln2_b", "w_router",
        "b_router", "w_gate", "w_up", "w_down", "tables", "decay"]
_OUTS = [((1, SEQ, D), "float32"), ((NB, NI, D), "float32"), ((1, 1, H, DK, DV), "float32"), ((1, 1, CW - 1, D), "float32"),
         ((1, NB, H, DK, DV), "float32"), ((1, NB, CW - 1, D), "float32")]


def kernel(**inputs):
    import numpy as _np
    import concourse.bacc as _bacc
    from concourse import mybir as _mybir
    from concourse.bass_utils import run_bass_kernel_spmd as _run

    nc = _bacc.Bacc("TRN2", target_bir_lowering=False, num_devices=1)
    inputs = {**inputs, **constants()}
    arrays, args = {}, []
    for name in _INS:
        a = _np.ascontiguousarray(inputs[name])
        arrays[f"in_{name}_dram"] = a
        args.append(nc.dram_tensor(f"in_{name}_dram", a.shape, _mybir.dt.from_np(a.dtype), kind="ExternalInput").ap())
    for i, (shape, dtype) in enumerate(_OUTS):
        args.append(nc.dram_tensor(f"out_{i}_dram", shape, _mybir.dt.from_np(_np.dtype(dtype)), kind="ExternalOutput").ap())
    program(nc, *args)
    r = _run(nc, [arrays], core_ids=[0])
    return tuple(r.results[0][f"out_{i}_dram"] for i in range(len(_OUTS)))
```

```python
import numpy as np
import concourse.bass as bass
from concourse import mybir
from contextlib import ExitStack

D = 1024
KT = D // 128
H = 4
DK, DV = 256, 512
NB, NI = 8, 8
NS = NB * NI
NM, SEQ = 16, 256
NP = NM + SEQ
T = NS + NP
TT = 112
NT = T // TT
CW = 31
EL = NB * (CW - 1 + NI)
EXT = EL + CW - 1 + NP
NE, NG, EG = 16, 4, 4
CAP = 96
PAST = 2048
EPS = 1e-5
ALPHA = 2.0 ** 0.25
OFF = dict(q=0, k=D, v=2 * D, g=4 * D, ua=6 * D, ub=7 * D, mr=8 * D, mc=9 * D)
ATT_W = [T - i * TT for i in range(NT)]
ATT_AT = [0, ATT_W[0], ATT_W[0] + ATT_W[1]]
HQ, HKP, HKS, HGAM, HS = 0, NS, NS + NT, NS + NT + NB, NS + NT + NB + 1
TB = {}
_at = 0
for _n, _w in (("cos", T), ("sin", T), ("heads", H * HS),
               ("ident", 128), ("mean", 128),
               ("before", TT), ("ones", TT)):
    TB[_n] = (_at, _at + _w)
    _at += _w
TBW = _at
VUB, VUA, VG, VCB, VCW = 0, 2, 4, 8, 10
NV = VCW + 2 * CW
VQK = NV
NVQ = NV + 4
V2 = dict(mc=0, mr=8, lng=16, lnb=24, bco=32)


def constants():
    f = np.float32
    log_g = np.log(f(1.0) - f(2.0) ** (f(-5.0) - np.arange(H, dtype=f))).astype(np.float64)
    pos = np.concatenate([PAST + np.arange(NS) % NI, np.arange(NP)]).astype(f)
    inv = (10000.0 ** (-np.arange(0, DK, 2, dtype=np.float64) / DK)).astype(f)
    ang = (pos[None, :] * inv[:, None]).astype(f).astype(np.float64)
    step = np.concatenate([np.arange(NS) % NI, np.arange(NP)])
    seq = np.concatenate([np.arange(NS) // NI, np.full(NP, NB)])
    diff = step[None, :] - step[:, None]
    ok = (seq[None, :] == seq[:, None]) & (diff >= 0)
    scale = DK ** -0.5
    dec = np.zeros((H, TT, sum(ATT_W)), f)
    tab = np.zeros((128, TBW), f)

    def put(name, a):
        tab[:a.shape[0], TB[name][0]:TB[name][1]] = a

    put("cos", np.cos(ang))
    put("sin", np.sin(ang))
    put("ident", np.eye(128))
    put("mean", np.full((128, 128), 1.0 / D))
    put("before", np.triu(np.ones((TT, TT)), 1))
    put("ones", np.ones((TT, TT)))
    heads = np.zeros((128, H, HS))
    for h in range(H):
        lg = log_g[h]
        full = np.where(ok, np.exp(np.maximum(diff, 0) * lg) * scale, 0.0)
        for i in range(NT):
            dec[h, :, ATT_AT[i]:ATT_AT[i] + ATT_W[i]] = full[i * TT:(i + 1) * TT, i * TT:]
        heads[:, h, HQ:HQ + NS] = np.exp((np.arange(NS) % NI + 1.0) * lg)[None, :]
        kp = np.where(seq == NB, np.exp((NP - 1.0 - step) * lg) * scale, 0.0)
        heads[:TT, h, HKP:HKP + NT] = kp.reshape(NT, TT).T
        for b in range(NB):
            heads[:NS, h, HKS + b] = np.where(np.arange(NS) // NI == b, np.exp((NI - 1.0 - np.arange(NS) % NI) * lg) * scale, 0.0)
        heads[:, h, HGAM] = np.exp(NI * lg)
    put("heads", heads.reshape(128, -1))
    return {"tables": tab, "decay": dec}


class Stage:

    def __init__(self, before, names, times=1):
        self.base = before.base + before.n * before.times if before else 0
        self.uses0 = before.uses_after() if before else [1] * 8
        self.n, self.times = len(names), times
        turn = list(before.turn) if before else [0, 0]
        self.at, self.bank, self.local = {}, {}, {}
        self.per = [0] * 8
        for i, name in enumerate(names):
            kind, name = name[0], name[1:]
            self.at[name] = i
            if kind == "-":
                continue
            k = "FP".index(kind)
            bank = 4 * k + turn[k] % 4
            turn[k] += 1
            self.bank[name] = bank
            self.local[name] = self.per[bank]
            self.per[bank] += 1
        self.turn = turn

    def uses_after(self):
        return [u + p * self.times for u, p in zip(self.uses0, self.per)]

    def done(self, name, it=0):
        return it * self.n + (self.base + self.at[name] + 1)

    def start(self, it=0):
        return it * self.n + self.base

    def used(self, name, it=0):
        b = self.bank[name]
        return it * self.per[b] + (self.uses0[b] + self.local[name])

    def emptied(self, name, it=0):
        b = self.bank[name]
        return it * self.per[b] + self.uses0[b]


def at_least(eng, sem, value):
    if not isinstance(value, int) or value > 0:
        eng.wait_ge(sem, value)


def alone(eng, waits_met):
    eng.sem_inc(waits_met, 1)


class Units:

    def __init__(self, before, n, times, last, tail):
        self.base = before.base + before.n * before.times if before else 0
        self.n, self.times, self.last, self.tail = n, times, last, tail

    def idx(self, u, it=0):
        return it * self.n + (self.base + u)


def program(nc, x_prompt, x_sample, state_ret, state_conv, meta_tokens, w_in, b_in, w_ret_o, conv_w, conv_b,
            conv_ln_g, conv_ln_b, w_conv_o, b_conv_o, w_out, ln1_g, ln1_b, ln2_g, ln2_b, w_router, b_router,
            w_gate, w_up, w_down, tables, decay,
            y_prompt, y_sample, new_ret_prompt, new_conv_prompt, new_ret_sample, new_conv_sample,
            x_slots, y_slots):
    f32, f32r = mybir.dt.float32, mybir.dt.float32r
    ALU, ACT, AX = mybir.AluOpType, mybir.ActivationFunctionType, mybir.AxisListType
    ds = bass.ds
    W2 = TT * 2

    ctx = ExitStack()
    with ctx:
        base = [(nc.sbuf_base + 31) // 32 * 32]
        high = [0]

        def sb(name, shape, dt=f32):
            size = 4 * int(np.prod(shape[1:]))
            t = nc.alloc_sbuf_tensor_at(name, shape, dt, offset=base[0])
            base[0] += (size + 31) // 32 * 32
            high[0] = max(high[0], base[0])
            return t

        def sem(name):
            return ctx.enter_context(nc.semaphore(name))

        tab = sb("tab", [128, TBW])
        vec = sb("vec", [128, H, NVQ])
        vec2 = sb("vec2", [128, 40])
        zeros = sb("zeros", [128, 256])
        wr_sb = sb("wr_sb", [128, KT, NE])
        br_bc = sb("br_bc", [TT, NE])
        persistent = base[0]
        xT_hi = sb("xT_hi", [128, KT, T], f32r)
        xT_lo = sb("xT_lo", [128, KT, T], f32r)
        raw = sb("raw", [128, 2, 2048])
        hi = sb("hi", [128, 2, 2048], f32r)
        lo = sb("lo", [128, 2, 2048], f32r)
        cT = sb("cT", [128, KT, T])
        retT = sb("retT", [128, KT, T])
        phase = base[0]
        st = sb("st", [128, NB, 2, DV])
        dec = sb("dec", [TT, sum(ATT_W)])
        E = sb("E", [128, 2, EXT])
        us = sb("us", [128, 2, NS])
        hist = sb("hist", [120, 2, 256])
        hv = sb("hv", [128, NVQ])
        hs = sb("hs", [128, HS])
        sub = sb("sub", [128, 2, T])
        qr = sb("qr", [128, 2, T])
        kr = sb("kr", [128, 2, T])
        rt = sb("rt", [128, 4, T])
        v_tok = sb("v_tok", [TT, NT, DV])
        vb = sb("vb", [TT, DV])
        kdp = sb("kdp", [TT, NT, 256])
        kds = sb("kds", [NS, NB, 256])
        att = sb("att", [TT, sum(ATT_W)])
        qdiag = sb("qdiag", [128, 2, NB * (NS + NI)])
        o_tok = sb("o_tok", [TT, NT, DV])
        sg_f = sb("sg_f", [128, 4, TT])
        sg_hi = sb("sg_hi", [128, 4, T], f32r)
        sg_lo = sb("sg_lo", [128, 4, T], f32r)
        ps_out = sb("ps_out", [128, 2, DV])
        u_tok = sb("u_tok", [NS, 256])
        up_tok = sb("up_tok", [CW - 1, 256])
        stats = sb("stats", [TT, NT, 6])
        mv = sb("mv", [TT, NT, 2])
        rs = sb("rs", [TT, 2, NT])
        base[0] = phase
        x_in = sb("x_in", [TT, NT, D])
        vrows = sb("vrows", [NV, H, 128])
        qkrows = sb("qkrows", [8, 256])
        v2rows = sb("v2rows", [40, 128])
        assert base[0] <= phase + 4 * NB * 2 * DV
        base[0] = phase
        x_tok = sb("x_tok", [TT, NT, D])
        x1 = sb("x1", [TT, NT, D])
        c_hi = sb("c_hi", [128, KT, T], f32r)
        c_lo = sb("c_lo", [128, KT, T], f32r)
        gc = sb("gc", [128, KT, T])
        gr = sb("gr", [128, KT, T])
        m_hi = sb("m_hi", [128, KT, T], f32r)
        csq = nc.alloc_sbuf_tensor_at("csq", [128, KT, T], f32, offset=base[0] - 4 * KT * T)
        m_lo = xT_lo
        rstd_c = sb("rstd_c", [128, T])
        lnst = sb("lnst", [TT, NT, 12])
        lnmv = sb("lnmv", [TT, NT, 4])
        ln_bc = sb("ln_bc", [TT, 2, D])
        MR, MH = 6, 3
        DR = 4
        base[0] = persistent
        y = sb("y", [TT, NT, D])
        gates = sb("gates", [TT, NT, NE])
        gt = sb("gt", [TT, 8, NT, NE])
        gs = sb("gs", [TT, 8, NT])
        gg = sb("gg", [TT, NT, NG])
        g_e = sb("g_e", [TT, NT])
        iota_r = sb("iota_r", [TT, NT, NE])
        slot = sb("slot", [TT, 2, NT], mybir.dt.int32)
        most = sb("most", [TT, 2])
        most_i = sb("most_i", [TT, 1], mybir.dt.int32)
        mst = sb("mst", [TT, NT, 12])
        mmv = sb("mmv", [TT, NT, 4])
        mhi = sb("mhi", [128, MH, 2048], f32r)
        mlo = sb("mlo", [128, MH, 2048], f32r)
        x1T_f = sb("x1T_f", [128, KT, T])
        xg_hi = sb("xg_hi", [128, 2, KT, CAP], f32r)
        shared = base[0]
        xg_lo = sb("xg_lo", [128, 2, KT, CAP], f32r)
        assert base[0] <= phase, (base[0], phase)
        base[0] = phase
        h_tok = sb("h_tok", [CAP, D])
        hT_hi = sb("hT_hi", [128, KT, CAP], f32r)
        hT_lo = sb("hT_lo", [128, KT, CAP], f32r)
        assert base[0] <= phase + 4 * NT * D
        base[0] = phase + 4 * NT * D
        yo = sb("yo", [CAP, 2, D])
        base[0] = phase + 2 * 4 * NT * D
        mraw = sb("mraw", [128, MR, 2048])
        xg_tok = sb("xg_tok", [CAP, 2, D])
        sgt = sb("sgt", [CAP, 512])
        ln2_bc = sb("ln2_bc", [TT, 2, D])
        base[0] = phase + 2 * 4 * NT * D
        y_back = sb("y_back", [TT, 2 * NT, D])
        base[0] = phase
        h_hi = sb("h_hi", [128, KT, T], f32r)
        h_lo = sb("h_lo", [128, KT, T], f32r)
        base[0] = phase + 2 * 4 * NT * D + DR * 8192
        x1T_hi = sb("x1T_hi", [128, KT, T], f32r)
        x1T_lo = sb("x1T_lo", [128, KT, T], f32r)
        assert base[0] <= phase + 2 * 4 * NT * D + MR * 8192 + 2 * 4 * D
        base[0] = shared - 4 * 2 * KT * CAP
        sgm = sb("sgm", [128, 2, 2, T])
        h_f = sb("h_f", [128, 2, T])
        assert base[0] <= phase
        assert high[0] <= nc.sbuf_usable_end, (high[0], nc.sbuf_usable_end)

        bank = [ctx.enter_context(nc.psum_tensor(f"bank{i}", [128, 512], f32)) for i in range(8)]
        ident = tab[:, TB["ident"][0]:TB["ident"][1]]

        PRE = Stage(None, [f"Pxt{i}" for i in range(6)] + ["Pvec", "Pbqk", "Pvec2"])
        HEAD = Stage(PRE, ["Phist0", "Phist1", "Fub0", "Fub1", "Fua0", "Fua1", "Fq0", "Fq1", "Fk0", "Fk1",
                           "PuS", "PuP", "-vp0", "-vp1", "-vp2", "Pv0", "Pv1", "Pv2", "Pkt0", "Pkt1",
                           "Patt0", "Patt1", "Patt2", "Fg0", "Fg1", "Fg2", "Fg3", "Po0", "Po1", "Po2"]
                     + [f"Pst{b}{p}" for b in range(NB) for p in range(2)] + ["Pps0", "Pps1"]
                     + [f"PoT{i}" for i in range(NT)] + [f"Fwr{m}" for m in range(8)], H)
        MEAN = Stage(HEAD, ["Pmean"])
        GATE = Stage(MEAN, ["Fmc0", "Fmc1", "Fmr0", "Fmr1"], 4)
        VAR = Stage(GATE, ["Pvar"])
        CONV = Stage(VAR, ["Fc0", "Fc1", "Fc2", "Fc3"], 2)
        WOUT = Stage(CONV, [x for n in range(2) for x in [f"-wp{n}{t}" for t in range(NT)] + [f"Pw{n}{t}" for t in range(NT)]])
        X1T = Stage(WOUT, [f"Pxt{i}" for i in range(6)] + ["Plog", "Ppos"])
        MNAMES = [x for j in range(4) for x in (f"Fg{2 * j}", f"Fg{2 * j + 1}", f"Fu{2 * j}", f"Fu{2 * j + 1}")]
        MNAMES += [x for n in range(2) for x in [f"-dp{n}{t}" for t in range(NT)] + [f"Pd{n}{t}" for t in range(NT)]]
        MOE = Stage(X1T, MNAMES, NE)
        def expert_groups(p, following):
            return ([f"-g{p}0a", f"Fg{p}0", f"-u{p}0a", f"Fu{p}0"] + [f"Pxt{p}{j}" for j in range(2)] * following
                    + [f"-g{p}1a", f"Fg{p}1", f"Pht{p}0", f"-u{p}1a", f"Fu{p}1", f"-d{p}0a", f"-d{p}1a", f"Pht{p}1",
                       f"Pd{p}0", f"Pd{p}1"])
        FIRST = Stage(X1T, ["Pxt0", "Pxt1"])
        PAIR = Stage(FIRST, expert_groups(0, 1) + expert_groups(1, 1), NE // 2 - 1)
        LAST = Stage(PAIR, expert_groups(0, 1) + expert_groups(1, 0))

        U_HEAD = Units(None, 10, H, ["ub1", "ua1", "q1", "k1", "vp2", "v2", "g1", "g3", "wr3", "wr7"], [4])
        U_GATE = Units(U_HEAD, 2, 4, ["mc1", "mr1"], [2])
        U_CONV = Units(U_GATE, 2, 2, ["c1", "c3"], [2])
        U_WOUT = Units(U_CONV, 4, 1, ["wp02", "w02", "wp12", "w12"], [2])
        N_UNITS = U_WOUT.base + 4
        U_MOE = Units(None, 12, NE, [f"{x}{2 * j + 1}" for j in range(4) for x in "gu"] + ["dp02", "d02", "dp12", "d12"], [3, 3])

        def unit_groups(p):
            return [f"g{p}0a", f"g{p}0", f"u{p}0a", f"u{p}0", f"g{p}1a", f"g{p}1", f"u{p}1a", f"u{p}1",
                    f"d{p}0a", f"d{p}1a", f"d{p}0", f"d{p}1"]
        U_PAIR = Units(None, 24, NE // 2, unit_groups(0) + unit_groups(1), None)

        LEAD, MLEAD = 2, MR
        group_done = sem("group_done")
        evac = [sem(f"evac{i}") for i in range(8)]
        raw_full = [sem(f"raw_full{i}") for i in range(2)]
        hi_ready, lo_ready = sem("hi_ready"), sem("lo_ready")
        mraw_full = [sem(f"mraw_full{i}") for i in range(MR)]
        mhi_ready, mlo_ready = sem("mhi_ready"), sem("mlo_ready")
        s_tab, s_x, s_rows, s_xhi = sem("s_tab"), sem("s_x"), sem("s_rows"), sem("s_xhi")
        st_full = [sem(f"st_full{b}") for b in range(NB)]
        st_out = [sem(f"st_out{b}") for b in range(NB)]
        dec_full, hist_full, vb_full = sem("dec_full"), sem("hist_full"), sem("vb_full")
        hv_ready = sem("hv_ready")
        rope_ready, qdiag_ready = sem("rope_ready"), sem("qdiag_ready")
        sghi_ready, sglo_ready = sem("sghi_ready"), sem("sglo_ready")
        out_sem, ps_stored, u_stored = sem("out_sem"), sem("ps_stored"), sem("u_stored")
        rv_ready, rstd_done = sem("rv_ready"), sem("rstd_done")
        dve_step = sem("dve_step")
        tail_step = sem("tail_step")
        csub_ready, csq_ready, cn_ready, csilu_ready = (sem(n) for n in ("csub_ready", "csq_ready", "cn_ready", "csilu_ready"))
        chi_ready, clo_ready = sem("chi_ready"), sem("clo_ready")
        mf_ready, mhi_done, mlo_done = sem("mf_ready"), sem("mhi_done"), sem("mlo_done")
        s_xres, s_ln, s_ln2, s_wrt = sem("s_xres"), sem("s_ln"), sem("s_ln2"), sem("s_wrt")
        x1_ready, x1hi_ready, x1lo_ready = (sem(n) for n in ("x1_ready", "x1hi_ready", "x1lo_ready"))
        lg_ready, exp_ready, iota_ready = sem("lg_ready"), sem("exp_ready"), sem("iota_ready")
        hhi_ready, hlo_ready = sem("hhi_ready"), sem("hlo_ready")
        zeroed, zero_ready = sem("zeroed"), sem("zero_ready")
        most_ready, slots_ready, scattered, gathered = (sem(n) for n in ("most_ready", "slots_ready", "scattered", "gathered"))
        xg_full, xghi_ready, hthi_ready = sem("xg_full"), sem("xghi_ready"), sem("hthi_ready")
        turned = sem("turned")
        chosen_ready = sem("chosen_ready")
        yo_stored, yo_free, moe_done = sem("yo_stored"), sem("yo_free"), sem("moe_done")
        y_ready, moved_up = sem("y_ready"), sem("moved_up")
        head_stored = sem("head_stored")
        waits_met = sem("waits_met")

        w_in_v = w_in[0].rearrange("(t p) n -> p t n", p=128)
        w_ret_v = w_ret_o[0].rearrange("(t p) n -> p t n", p=128)
        w_conv_v = w_conv_o[0].rearrange("(t p) n -> p t n", p=128)
        w_out_v = w_out[0].rearrange("(t p) n -> p t n", p=128)

        nc_ok = ctx.enter_context(nc.allow_non_contiguous_dma("small vectors and slices of rows"))
        block = ctx.enter_context(nc.Block())

        def F_view(t, slot):
            return t[:, slot, :].rearrange("p (k n) -> p k n", k=KT)

        def T_view(t, slot):
            return t[:, slot, :].rearrange("p (k n) -> p k n", k=4)

        def samples(ap):
            return ap[:, 0:EL].rearrange("p (b w) -> p b w", b=NB)

        @block.sync
        def _(sp):
            sp.sem_inc(lo_ready, LEAD)
            sp.sem_inc(mlo_ready, MLEAD)
            for i in range(8):
                sp.sem_inc(evac[i], 1)
            sp.dma_start(tab[:], tables).then_inc(s_tab, 16)
            sp.dma_start(x_in[0:NS, 0, :], x_sample.rearrange("b i d -> (b i) d")).then_inc(s_x, 16)
            sp.dma_start(x_in[NS:NS + NM, 0, :], meta_tokens).then_inc(s_x, 16)
            sp.dma_start(x_in[NS + NM:TT, 0, :], x_prompt[0, 0:TT - NS - NM, :]).then_inc(s_x, 16)
            for t in range(1, NT):
                a = t * TT - NS - NM
                sp.dma_start(x_in[:, t, :], x_prompt[0, a:a + TT, :]).then_inc(s_x, 16)

            def unit(units, u, it, parts, view=F_view):
                c = units.idx(u, it)
                at_least(sp, lo_ready, c - 1 + LEAD)
                alone(sp, waits_met)
                slot = u % 2
                for a, b, src in parts:
                    sp.dma_start(view(raw, slot)[:, :, a:b], src).then_inc(raw_full[slot], 16)

            with sp.Fori(0, H) as h:
                for u, name in enumerate(("ub", "ua", "q", "k")):
                    unit(U_HEAD, u, h, [(0, 256, w_in_v[:, :, ds(h * 256 + OFF[name], 256)])])
                for j in range(2):
                    unit(U_HEAD, 4 + j, h, [(0, DV, w_in_v[:, 4 * j:4 * j + 4, ds(h * DV + OFF["v"], DV)])], T_view)
                for j in range(2):
                    unit(U_HEAD, 6 + j, h, [(0, 256, w_in_v[:, :, ds(h * DV + (OFF["g"] + 256 * j), 256)])])
                for j in range(2):
                    unit(U_HEAD, 8 + j, h, [(0, 512, w_ret_v[:, ds(h * 4, 4), 512 * j:512 * j + 512])], T_view)
            with sp.Fori(0, 4) as j:
                for u, name in enumerate(("mc", "mr")):
                    unit(U_GATE, u, j, [(0, 256, w_in_v[:, :, ds(j * 256 + OFF[name], 256)])])
            with sp.Fori(0, 2) as j:
                for u in range(2):
                    unit(U_CONV, u, j, [(0, 256, w_conv_v[:, :, ds(j * 512 + 256 * u, 256)])])
            for n in range(2):
                for half in range(2):
                    unit(U_WOUT, 2 * n + half, 0, [(0, 512, w_out_v[:, 4 * half:4 * half + 4, 512 * n:512 * n + 512])], T_view)

            def pair_unit(v, it):
                if v >= MR:
                    sp.wait_ge(mlo_ready, U_PAIR.idx(v, it) + (MLEAD + 1 - MR))
                    alone(sp, waits_met)
                more, v = divmod(v, 24)
                p, u = divmod(v, 12)
                w, n, half = ((w_gate, 0, u), (w_up, 0, u - 2), (w_gate, 1, u - 4), (w_up, 1, u - 6))[u // 2] if u < 8 else (w_down, u % 2, (u - 8) // 2)
                e = it * 2 + (2 * more + p)
                src = w[0][ds(e, 1)].rearrange("e (t p) n -> p (e t) n", p=128)
                sp.dma_start(T_view(mraw, v % MR), src[:, 4 * half:4 * half + 4, 512 * n:512 * n + 512]).then_inc(mraw_full[v % MR], 16)

            sp.wait_ge(mlo_done, 1)
            for v in range(MR):
                if v == MR - 1:
                    sp.wait_ge(group_done, WOUT.done("w12"))
                pair_unit(v, 0)
            sp.wait_ge(most_ready, 1)
            with sp.If(sp.value_load(most_i[0:1, 0:1], min_val=0, max_val=T) <= CAP):
                with sp.Fori(0, NE // 2 - 1) as it:
                    for v in range(MR, MR + 24):
                        pair_unit(v, it)
                for v in range(MR, 24):
                    pair_unit(v, NE // 2 - 1)
            with sp.Else():
                with sp.Fori(0, NE) as e:
                    for u in range(12):
                        c = U_MOE.idx(u, e)
                        sp.wait_ge(mlo_ready, c + (MLEAD + 1 - DR))
                        alone(sp, waits_met)
                        slot_ = u % DR
                        if u < 8:
                            src = (w_gate, w_up)[u % 2][0][ds(e, 1)].rearrange("e (t p) n -> p (e t) n", p=128)
                            sp.dma_start(F_view(mraw, slot_), src[:, :, 256 * (u // 2):256 * (u // 2) + 256]).then_inc(mraw_full[slot_], 16)
                        else:
                            n, half = divmod(u - 8, 2)
                            src = w_down[0][ds(e, 1)].rearrange("e (t p) n -> p (e t) n", p=128)
                            sp.dma_start(T_view(mraw, slot_), src[:, 4 * half:4 * half + 4, 512 * n:512 * n + 512]).then_inc(mraw_full[slot_], 16)
            sp.wait_ge(moe_done, 1)
            sp.dma_start(ln2_bc[:, 0, :], ln2_g.to_broadcast([TT, D])).then_inc(s_ln2, 16)
            sp.dma_start(ln2_bc[:, 1, :], ln2_b.to_broadcast([TT, D])).then_inc(s_ln2, 16)

            for t in range(NT):
                sp.wait_ge(y_ready, t + 1)
                if t == 0:
                    sp.dma_start(y_sample.rearrange("b i d -> (b i) d"), y[0:NS, 0, :]).then_inc(out_sem, 16)
                    sp.dma_start(y_prompt[0, 0:TT - NS - NM, :], y[NS + NM:TT, 0, :]).then_inc(out_sem, 16)
                else:
                    a = t * TT - NS - NM
                    sp.dma_start(y_prompt[0, a:a + TT, :], y[:, t, :]).then_inc(out_sem, 16)
            sp.wait_ge(out_sem, 16 * (NT + 1))

        N_ROWS = 12

        @block.gpsimd
        def _(pool):
            def rows(dst, src):
                pool.dma_start(dst, src).then_inc(s_rows, 16)

            b_v = b_in[0].rearrange("(a p) -> a p", p=128)
            hj = lambda off, j: b_in[0, off:off + H * j * 128].rearrange("(h j p) -> j h p", h=H, j=j)
            rows(vrows[VUB:VUB + 2, :, :], hj(OFF["ub"], 2))
            rows(vrows[VUA:VUA + 2, :, :], hj(OFF["ua"], 2))
            rows(vrows[VG:VG + 4, :, :], hj(OFF["g"], 4))
            rows(vrows[VCB:VCB + 2, :, :], conv_b[0].rearrange("(h j p) -> j h p", h=H, j=2))
            for j in range(2):
                rows(vrows[VCW + j * CW:VCW + (j + 1) * CW, :, :],
                     conv_w[0].rearrange("w (h j p) -> j w h p", h=H, j=2)[j])
            rows(qkrows[:, :], b_in[0, 0:2 * D].rearrange("(a p) -> a p", p=256))
            for name, src in (("mc", b_v[OFF["mc"] // 128:OFF["mc"] // 128 + 8, :]),
                              ("mr", b_v[OFF["mr"] // 128:OFF["mr"] // 128 + 8, :]),
                              ("lng", conv_ln_g[0].rearrange("(a p) -> a p", p=128)),
                              ("lnb", conv_ln_b[0].rearrange("(a p) -> a p", p=128)),
                              ("bco", b_conv_o[0].rearrange("(a p) -> a p", p=128))):
                rows(v2rows[V2[name]:V2[name] + 8, :], src)
            pool.dma_start(wr_sb[:], w_router.rearrange("(t p) n -> p t n", p=128)).then_inc(s_wrt, 16)
            pool.dma_start(br_bc[:], b_router.rearrange("(a n) -> a n", a=1).to_broadcast([TT, NE])).then_inc(s_wrt, 16)
            pool.dma_start(new_conv_sample[0, :, 0:CW - 1 - NI, :], state_conv[0, :, NI:CW - 1, :]).then_inc(moved_up, 16)
            pool.wait_ge(zero_ready, 1)
            for r in range(NE * CAP // 128):
                pool.dma_start(x_slots[r * 128:(r + 1) * 128, :].rearrange("p (a c) -> p a c", a=4),
                               zeros[:, :].unsqueeze(1).to_broadcast([128, 4, 256])).then_inc(zeroed, 16)
            pool.wait_ge(group_done, PRE.done("vec2"))
            pool.sem_inc(head_stored, 1)
            with pool.Fori(0, H) as h:
                at_least(pool, group_done, HEAD.start(h))
                alone(pool, waits_met)
                pool.dma_start(hist[:, :, :], state_conv[0].rearrange("(a b) w c -> (b w) a c", a=2)[:, :, ds(h * 256, 256)]
                               ).then_inc(hist_full, 16)
                pool.dma_start(vb[:, :], b_in[0:1, ds(h * DV + OFF["v"], DV)].to_broadcast([TT, DV])).then_inc(vb_full, 16)
                pool.dma_start(dec[:, :], decay[ds(h, 1)].rearrange("h p n -> p (h n)")).then_inc(dec_full, 16)
                for b in range(NB):
                    pool.dma_start(st[:, b, :, :], state_ret[0, b][ds(h, 1)].rearrange("h (p t) n -> p (h t) n", t=2)
                                   ).then_inc(st_full[b], 16)
                pool.wait_ge(evac[HEAD.bank["uS"]], HEAD.used("uS", h) + 1)
                alone(pool, waits_met)
                for b in range(NB):
                    pool.dma_start(new_conv_sample[0, b, CW - 1 - NI:CW - 1, ds(h * 256, 256)],
                                   u_tok[b * NI:(b + 1) * NI, :]).then_inc(u_stored, 16)
                pool.wait_ge(evac[HEAD.bank["uP"]], HEAD.used("uP", h) + 1)
                alone(pool, waits_met)
                pool.dma_start(new_conv_prompt[0, 0, :, ds(h * 256, 256)], up_tok[:, :]).then_inc(u_stored, 16)
                for b in range(NB):
                    for p in range(2):
                        n = f"st{b}{p}"
                        pool.wait_ge(evac[HEAD.bank[n]], HEAD.used(n, h) + 1)
                        alone(pool, waits_met)
                    pool.dma_start(new_ret_sample[0, b][ds(h, 1)].rearrange("h (p t) n -> p (h t) n", t=2), st[:, b, :, :]
                                   ).then_inc(st_out[b], 16)
                pool.wait_ge(evac[HEAD.bank["ps1"]], HEAD.used("ps1", h) + 1)
                alone(pool, waits_met)
                pool.dma_start(new_ret_prompt[0, 0][ds(h, 1)].rearrange("h (p t) n -> p (h t) n", t=2), ps_out[:, :, :]
                               ).then_inc(ps_stored, 16)
                for b in range(NB):
                    pool.wait_ge(st_out[b], h * 16 + 16)
                    alone(pool, waits_met)
                pool.wait_ge(ps_stored, h * 16 + 16)
                alone(pool, waits_met)
                pool.wait_ge(u_stored, h * (16 * (NB + 1)) + 16 * (NB + 1))
                pool.sem_inc(head_stored, 1)
            pool.wait_ge(group_done, MEAN.start())
            pool.wait_ge(evac[HEAD.bank["wr7"]], HEAD.used("wr7", H - 1) + 1)
            pool.dma_start(x_tok[0:NS, 0, :], x_sample.rearrange("b i d -> (b i) d")).then_inc(s_xres, 16)
            pool.dma_start(x_tok[NS:NS + NM, 0, :], meta_tokens).then_inc(s_xres, 16)
            pool.dma_start(x_tok[NS + NM:TT, 0, :], x_prompt[0, 0:TT - NS - NM, :]).then_inc(s_xres, 16)
            for t in range(1, NT):
                a = t * TT - NS - NM
                pool.dma_start(x_tok[:, t, :], x_prompt[0, a:a + TT, :]).then_inc(s_xres, 16)
            pool.dma_start(ln_bc[:, 0, :], ln1_g.to_broadcast([TT, D])).then_inc(s_ln, 16)
            pool.dma_start(ln_bc[:, 1, :], ln1_b.to_broadcast([TT, D])).then_inc(s_ln, 16)
            pool.wait_ge(group_done, WOUT.done("w12"))
            pool.wait_ge(x1_ready, NT)
            for e in range(NE):
                i = pool.memset(iota_r[:, :, e:e + 1], float(NE - e))
            i.then_inc(iota_ready, 1)
            pool.wait_ge(moved_up, 16)
            pool.wait_ge(zeroed, 16 * (NE * CAP // 128))
            pool.wait_ge(most_ready, 1)
            pool.wait_ge(slots_ready, 2)
            with pool.If(pool.value_load(most_i[0:1, 0:1], min_val=0, max_val=T) <= CAP):
                for k in range(2):
                    for t in range(NT):
                        pool.indirect_dma_start(x_slots, bass.IndirectOffsetOnAxis(slot[:, k, t:t + 1], 0), x1[:, t, :], None
                                                ).then_inc(scattered, 16)
                pool.wait_ge(scattered, 16 * 2 * NT)
                pool.sem_inc(yo_free, 2)
                pool.dma_start(xg_tok[:, 0, :], x_slots[0:CAP, :]).then_inc(xg_full, 16)

                def expert(stage, p, it, following):
                    if following:
                        pool.wait_ge(group_done, stage.start(it) + (0 if p == 0 else stage.at["xt01"] + 1))
                        alone(pool, waits_met)
                        pool.dma_start(xg_tok[:, 1 - p, :], x_slots[ds((it * 2 + (p + 1)) * CAP, CAP), :]).then_inc(xg_full, 16)
                    n = f"d{p}1"
                    pool.wait_ge(evac[stage.bank[n]], stage.used(n, it) + 1)
                    alone(pool, waits_met)
                    pool.dma_start(y_slots[ds((it * 2 + p) * CAP, CAP), :], yo[:, p, :]).then_inc(yo_stored, 16)
                    pool.wait_ge(yo_stored, it * 32 + (16 * p + 16))
                    pool.sem_inc(yo_free, 1)

                with pool.Fori(0, NE // 2 - 1) as it:
                    for p in range(2):
                        expert(PAIR, p, it, True)
                last = NE // 2 - 1
                for p in range(2):
                    if p == 0:
                        pool.wait_ge(group_done, LAST.start())
                        pool.dma_start(xg_tok[:, 1, :], x_slots[(NE - 1) * CAP:NE * CAP, :]).then_inc(xg_full, 16)
                    n = f"d{p}1"
                    pool.wait_ge(evac[LAST.bank[n]], LAST.used(n) + 1)
                    pool.dma_start(y_slots[(NE - 2 + p) * CAP:(NE - 1 + p) * CAP, :], yo[:, p, :]).then_inc(yo_stored, 16)
                pool.wait_ge(yo_stored, 16 * NE)
                for t in range(NT):
                    for k in range(2):
                        pool.indirect_dma_start(y_back[:, 2 * t + k, :], None, y_slots, bass.IndirectOffsetOnAxis(slot[:, k, t:t + 1], 0)
                                                ).then_inc(gathered, 16)
                pool.wait_ge(gathered, 16 * 2 * NT)

        @block.tensor
        def _(pe):
            def group(stage, name, it, mms, begin=True, m=128, n=512):
                for out, a, b, s, e in mms:
                    i = pe.matmul(out, a, b, start=s, stop=e)
                i.then_inc(group_done, 1)

            def room(stage, name, it):
                at_least(pe, evac[stage.bank[name]], stage.used(name, it))

            def split_ready(units, u, it):
                pe.wait_ge(lo_ready, units.idx(u, it) + (1 + LEAD))

            def three(out, w_h, w_l, x_h, x_l, first, last):
                return [(out, w_h, x_h, first, False), (out, w_h, x_l, False, False), (out, w_l, x_h, False, last)]

            def f_group(stage, name, it, wh, wl, cols, xh, xl, kts=KT):
                room(stage, name, it)
                out = bank[stage.bank[name]][:, 0:T]
                mms = []
                for k in range(kts):
                    mms += three(out, wh[:, k, cols], wl[:, k, cols], xh[:, k, :], xl[:, k, :], k == 0, k == kts - 1)
                group(stage, name, it, mms)

            def t_unit(stage, half, parts, finals, it, wh, wl, xh, xl):
                for t in range(NT):
                    name = finals[t]
                    if half == 0:
                        room(stage, name, it)
                    out = bank[stage.bank[name]][0:TT, :]
                    mms = []
                    for k in range(4):
                        kk = 4 * half + k
                        first, last = half == 0 and k == 0, half == 1 and k == 3
                        xs = slice(t * TT, (t + 1) * TT)
                        mms += [(out, xh[:, kk, xs], wh[:, k, :], first, False), (out, xh[:, kk, xs], wl[:, k, :], False, False),
                                (out, xl[:, kk, xs], wh[:, k, :], False, last)]
                    group(stage, name, it, mms)

            def turn(stage, name, it, parts):
                room(stage, name, it)
                alone(pe, waits_met)
                for out, in_, n in parts:
                    i = pe.transpose(out, in_, ident[0:n, 0:n])
                i.then_inc(group_done, 1)

            def gathered_path():
                def tokens(stage, names, q, it, value):
                    pe.wait_ge(xg_full, value)
                    for j, name in enumerate(names):
                        b = bank[stage.bank[name]]
                        turn(stage, name, it, [(b[:, i * CAP:(i + 1) * CAP], xg_tok[:, q, (4 * j + i) * 128:(4 * j + i + 1) * 128], CAP) for i in range(4)])

                def half(stage, v, it, wit, name, kh, xh, xl):
                    pe.wait_ge(mlo_ready, U_PAIR.idx(v, wit) + (1 + MLEAD))
                    if kh == 0:
                        room(stage, name, it)
                    out = bank[stage.bank[name]][0:CAP, :]
                    wh, wl = T_view(mhi, v % MH), T_view(mlo, v % MH)
                    mms = []
                    for k in range(4):
                        kk = 4 * kh + k
                        mms += [(out, xh[:, kk, :], wh[:, k, :], kk == 0, False), (out, xh[:, kk, :], wl[:, k, :], False, False),
                                (out, xl[:, kk, :], wh[:, k, :], False, kk == KT - 1)]
                    group(stage, name, it, mms)

                def h_turn(stage, p, j, it):
                    pe.wait_ge(evac[stage.bank[f"u{p}{j}"]], stage.used(f"u{p}{j}", it) + 1)
                    alone(pe, waits_met)
                    b = bank[stage.bank[f"ht{p}{j}"]]
                    turn(stage, f"ht{p}{j}", it, [(b[:, i * CAP:(i + 1) * CAP], h_tok[:, (4 * j + i) * 128:(4 * j + i + 1) * 128], CAP) for i in range(4)])

                def evacuated(stage, name, it):
                    pe.wait_ge(evac[stage.bank[name]], stage.used(name, it) + 1)

                def expert(stage, p, it, wit, following):
                    v = 12 * p
                    xh, xl = xg_hi[:, p], xg_lo[:, p]
                    if p:
                        for j in range(2):
                            evacuated(stage, f"xt0{j}", it)
                    for u, name in ((0, f"g{p}0"), (2, f"u{p}0")):
                        for kh in range(2):
                            half(stage, v + u + kh, it, wit, name, kh, xh, xl)
                    if following:
                        tokens(stage, (f"xt{p}0", f"xt{p}1"), 1 - p, it, wit * 32 + (16 * p + 32))
                    for kh in range(2):
                        half(stage, v + 4 + kh, it, wit, f"g{p}1", kh, xh, xl)
                    h_turn(stage, p, 0, it)
                    for kh in range(2):
                        half(stage, v + 6 + kh, it, wit, f"u{p}1", kh, xh, xl)
                    for kh in range(2):
                        evacuated(stage, f"ht{p}{kh}", it) if kh == 0 else None
                        if kh == 1:
                            h_turn(stage, p, 1, it)
                            evacuated(stage, f"ht{p}1", it)
                        for n in range(2):
                            half(stage, v + 8 + 2 * kh + n, it, wit, f"d{p}{n}", kh, hT_hi, hT_lo)

                tokens(FIRST, ("xt0", "xt1"), 0, 0, 16)
                for j in range(2):
                    evacuated(FIRST, f"xt{j}", 0)
                with pe.Fori(0, NE // 2 - 1) as it:
                    for p in range(2):
                        if p == 0:
                            pe.wait_ge(turned, it + 1)
                        expert(PAIR, p, it, it, True)
                pe.wait_ge(turned, NE // 2)
                expert(LAST, 0, 0, NE // 2 - 1, True)
                expert(LAST, 1, 0, NE // 2 - 1, False)

            def dense_path():
                pe.wait_ge(x1lo_ready, 6)
                with pe.Fori(0, NE) as e:
                    for u in range(12):
                        pe.wait_ge(mlo_ready, U_MOE.idx(u, e) + (1 + MLEAD))
                        s = u % MH
                        if u < 8:
                            for m in range(2):
                                f_group(MOE, f"{'gu'[u % 2]}{2 * (u // 2) + m}", e, F_view(mhi, s), F_view(mlo, s), slice(m * 128, (m + 1) * 128), x1T_hi, x1T_lo)
                        else:
                            n, half = divmod(u - 8, 2)
                            if u == 8:
                                pe.wait_ge(hlo_ready, e * 4 + 4)
                            t_unit(MOE, half, None, [f"d{n}{t}" for t in range(NT)], e, T_view(mhi, s), T_view(mlo, s), h_hi, h_lo)

            pe.wait_ge(s_tab, 16)
            pe.wait_ge(s_x, 16 * 5)
            for t in range(NT):
                for j in range(2):
                    n = f"xt{2 * t + j}"
                    b = bank[PRE.bank[n]]
                    turn(PRE, n, 0, [(b[:, i * TT:(i + 1) * TT], x_in[:, t, (4 * j + i) * 128:(4 * j + i + 1) * 128], TT) for i in range(4)])
            pe.wait_ge(s_rows, 16 * N_ROWS)
            b = bank[PRE.bank["vec"]]
            turn(PRE, "vec", 0, [(b[:, h * NV:(h + 1) * NV], vrows[:, h, :], NV) for h in range(H)])
            b = bank[PRE.bank["bqk"]]
            turn(PRE, "bqk", 0, [(b[:, 8 * p:8 * p + 8], qkrows[:, p:256:2], 8) for p in range(2)])
            b = bank[PRE.bank["vec2"]]
            turn(PRE, "vec2", 0, [(b[:, 0:40], v2rows[:, :], 40)])
            for n in [f"xt{i}" for i in range(6)]:
                pe.wait_ge(evac[PRE.bank[n]], PRE.used(n) + 1)

            with pe.Fori(0, H) as h:
                pe.wait_ge(hist_full, h * 16 + 16)
                for c in range(2):
                    b = bank[HEAD.bank[f"hist{c}"]]
                    turn(HEAD, f"hist{c}", h, [(b[:, a * 120:a * 120 + 120], hist[:, a, c * 128:(c + 1) * 128], 120) for a in range(2)])
                for u, name in enumerate(("ub", "ua", "q", "k")):
                    split_ready(U_HEAD, u, h)
                    wh, wl = F_view(hi, u % 2), F_view(lo, u % 2)
                    for m in range(2):
                        cols = slice(m * 128, (m + 1) * 128) if u < 2 else slice(m, 256, 2)
                        f_group(HEAD, f"{name}{m}", h, wh, wl, cols, xT_hi, xT_lo)
                for c in range(2):
                    pe.wait_ge(evac[HEAD.bank[f"ua{c}"]], HEAD.used(f"ua{c}", h) + 1)
                b = bank[HEAD.bank["uS"]]
                turn(HEAD, "uS", h, [(b[0:NS, c * 128:(c + 1) * 128], us[:, c, :], 128) for c in range(2)])
                b = bank[HEAD.bank["uP"]]
                turn(HEAD, "uP", h, [(b[0:CW - 1, c * 128:(c + 1) * 128], E[:, c, EXT - CW + 1:EXT], 128) for c in range(2)])
                for half in range(2):
                    split_ready(U_HEAD, 4 + half, h)
                    t_unit(HEAD, half, None, [f"v{t}" for t in range(NT)], h, T_view(hi, half), T_view(lo, half), xT_hi, xT_lo)
                pe.wait_ge(rope_ready, h * 4 + 4)
                for g, tiles in enumerate(((0, 1), (2,))):
                    b = bank[HEAD.bank[f"kt{g}"]]
                    turn(HEAD, f"kt{g}", h, [(b[0:TT, (2 * i + p) * 128:(2 * i + p + 1) * 128], kr[:, p, t * TT:(t + 1) * TT], 128)
                                             for i, t in enumerate(tiles) for p in range(2)])
                for i in range(NT):
                    name = f"att{i}"
                    room(HEAD, name, h)
                    out = bank[HEAD.bank[name]][0:TT, 0:ATT_W[i]]
                    group(HEAD, name, h, [(out, kr[:, p, i * TT:(i + 1) * TT], qr[:, p, i * TT:T], p == 0, p == 1) for p in range(2)])
                for j in range(2):
                    u = 6 + j
                    split_ready(U_HEAD, u, h)
                    for m in range(2):
                        f_group(HEAD, f"g{2 * j + m}", h, F_view(hi, u % 2), F_view(lo, u % 2), slice(m * 128, (m + 1) * 128), xT_hi, xT_lo)
                for t in range(NT):
                    pe.wait_ge(evac[HEAD.bank[f"v{t}"]], HEAD.used(f"v{t}", h) + 1)
                    pe.wait_ge(evac[HEAD.bank[f"att{t}"]], HEAD.used(f"att{t}", h) + 1)
                for t in range(NT):
                    name = f"o{t}"
                    room(HEAD, name, h)
                    out = bank[HEAD.bank[name]][0:TT, :]
                    mms = [(out, att[:, ATT_AT[i] + (t - i) * TT:ATT_AT[i] + (t - i + 1) * TT], v_tok[:, i, :], i == 0, i == t)
                           for i in range(t + 1)]
                    if t == 0:
                        for a, l, r, s, e in mms:
                            pe.matmul(a, l, r, start=s, stop=e)
                        pe.wait_ge(qdiag_ready, h * 2 + 2)
                        for b in range(NB):
                            pe.wait_ge(st_full[b], h * 16 + 16)
                        o64 = bank[HEAD.bank[name]][0:NS, :]
                        for b in range(NB):
                            for p in range(2):
                                i = pe.matmul(o64, qdiag[:, p, b * NS:(b + 1) * NS], st[:, b, p, :], start=False, stop=(b == NB - 1 and p == 1), skip_group_check=True)
                        i.then_inc(group_done, 1)
                    else:
                        group(HEAD, name, h, mms)
                pe.wait_ge(evac[HEAD.bank["kt0"]], HEAD.used("kt0", h) + 1)
                pe.wait_ge(evac[HEAD.bank["kt1"]], HEAD.used("kt1", h) + 1)
                for b in range(NB):
                    for p in range(2):
                        name = f"st{b}{p}"
                        room(HEAD, name, h)
                        group(HEAD, name, h, [(bank[HEAD.bank[name]][:, :], kds[:, b, p * 128:(p + 1) * 128], v_tok[0:NS, 0, :], True, True)])
                for p in range(2):
                    name = f"ps{p}"
                    room(HEAD, name, h)
                    group(HEAD, name, h, [(bank[HEAD.bank[name]][:, :], kdp[:, t, p * 128:(p + 1) * 128], v_tok[:, t, :], t == 0, t == NT - 1) for t in range(NT)])
                for t in range(NT):
                    pe.wait_ge(evac[HEAD.bank[f"o{t}"]], HEAD.used(f"o{t}", h) + 1)
                    b = bank[HEAD.bank[f"oT{t}"]]
                    turn(HEAD, f"oT{t}", h, [(b[:, j * TT:(j + 1) * TT], o_tok[:, t, j * 128:(j + 1) * 128], TT) for j in range(4)])
                pe.wait_ge(sglo_ready, h * NT + NT)
                for j in range(2):
                    split_ready(U_HEAD, 8 + j, h)
                    for m in range(4):
                        f_group(HEAD, f"wr{4 * j + m}", h, T_view(hi, j), T_view(lo, j), slice(m * 128, (m + 1) * 128), sg_hi, sg_lo, 4)

            ones = tab[:, TB["mean"][0]:TB["mean"][1]]
            pe.wait_ge(evac[HEAD.bank["wr7"]], HEAD.used("wr7", H - 1) + 1)
            room(MEAN, "mean", 0)
            group(MEAN, "mean", 0, [(bank[MEAN.bank["mean"]][:, 0:T], ones, cT[:, k, :], k == 0, k == KT - 1) for k in range(KT)])
            with pe.Fori(0, 4) as j:
                for u, name in enumerate(("mc", "mr")):
                    split_ready(U_GATE, u, j)
                    for m in range(2):
                        f_group(GATE, f"{name}{m}", j, F_view(hi, u), F_view(lo, u), slice(m * 128, (m + 1) * 128), xT_hi, xT_lo)
            pe.wait_ge(csq_ready, 1)
            room(VAR, "var", 0)
            group(VAR, "var", 0, [(bank[VAR.bank["var"]][:, 0:T], ones, csq[:, k, :], k == 0, k == KT - 1) for k in range(KT)])
            pe.wait_ge(clo_ready, 1)
            with pe.Fori(0, 2) as j:
                for u in range(2):
                    split_ready(U_CONV, u, j)
                    for m in range(2):
                        f_group(CONV, f"c{2 * u + m}", j, F_view(hi, u), F_view(lo, u), slice(m * 128, (m + 1) * 128), c_hi, c_lo)
            pe.wait_ge(mlo_done, 1)
            for n in range(2):
                for half in range(2):
                    split_ready(U_WOUT, 2 * n + half, 0)
                    t_unit(WOUT, half, None, [f"w{n}{t}" for t in range(NT)], 0, T_view(hi, half), T_view(lo, half), m_hi, m_lo)
            for t in range(NT):
                pe.wait_ge(x1_ready, t + 1)
                for j in range(2):
                    n = f"xt{2 * t + j}"
                    b = bank[X1T.bank[n]]
                    turn(X1T, n, 0, [(b[:, i * TT:(i + 1) * TT], x1[:, t, (4 * j + i) * 128:(4 * j + i + 1) * 128], TT) for i in range(4)])
            for n in range(6):
                pe.wait_ge(evac[X1T.bank[f"xt{n}"]], X1T.used(f"xt{n}") + 1)
            pe.wait_ge(s_wrt, 32)
            room(X1T, "log", 0)
            out = bank[X1T.bank["log"]]
            for t in range(NT):
                for k in range(KT):
                    i = pe.matmul(out[0:TT, t * NE:(t + 1) * NE], x1T_f[:, k, t * TT:(t + 1) * TT], wr_sb[:, k, :], start=(k == 0), stop=(k == KT - 1))
            i.then_inc(group_done, 1)
            pe.wait_ge(chosen_ready, 1)
            room(X1T, "pos", 0)
            before, ones_t = (tab[0:TT, TB[n][0]:TB[n][1]] for n in ("before", "ones"))
            out = bank[X1T.bank["pos"]]
            for t in range(NT + 1):
                o = out[0:TT, t * NE:(t + 1) * NE]
                for i in range(min(t, NT - 1) + 1):
                    last = pe.matmul(o, before if i == t else ones_t, gt[:, 7, i, :], start=(i == 0), stop=(i == min(t, NT - 1)))
            last.then_inc(group_done, 1)
            pe.wait_ge(most_ready, 1)
            with pe.If(pe.value_load(most_i[0:1, 0:1], min_val=0, max_val=T) <= CAP):
                gathered_path()
            with pe.Else():
                dense_path()


        def split_hi(act, units, stage, u, it, R, RH, src, dst, full, ready, used=0):
            slot, hslot = u % R, u % RH
            act.wait_ge(full[slot], (it * (units.n // R) + ((units.base + u) // R + 1 + used)) * 16)
            if u >= RH:
                act.wait_ge(group_done, stage.done(units.last[u - RH], it))
            else:
                act.wait_ge(group_done, stage.start(it) - sum(units.tail[:RH - 1 - u]))
            act.activation(dst[:, hslot, :], src[:, slot, :], ACT.Copy).then_inc(ready, 1)

        def split_lo(dve, units, u, it, R, RH, src, h, l, hready, lready):
            dve.wait_ge(hready, units.idx(u, it) + 1)
            dve.tensor_tensor(l[:, u % RH, :], src[:, u % R, :], h[:, u % RH, :].bitcast(f32), ALU.subtract).then_inc(lready, 1)

        def took(stage, name, it=0):
            return evac[stage.bank[name]], stage.used(name, it) + 1

        @block.scalar
        def _(act):
            def S(units, stage, u, it):
                split_hi(act, units, stage, u, it, 2, 2, raw, hi, raw_full, hi_ready)

            def SM(u, it):
                split_hi(act, U_MOE, MOE, u, it, DR, MH, mraw, mhi, mraw_full, mhi_ready, 1)

            def full(stage, name, it=0):
                act.wait_ge(group_done, stage.done(name, it))
                return bank[stage.bank[name]], evac[stage.bank[name]]

            for i in range(6):
                b, e = full(PRE, f"xt{i}")
                t, j = divmod(i, 2)
                act.activation(xT_hi[:, 4 * j:4 * j + 4, t * TT:(t + 1) * TT], b[:, 0:4 * TT].rearrange("p (k n) -> p k n", k=4), ACT.Copy).then_inc(s_xhi, 1)
            b, e = full(PRE, "vec")
            act.activation(vec[:, :, 0:NV], b[:, 0:H * NV].rearrange("p (h n) -> p h n", h=H), ACT.Copy).then_inc(e, 1)
            b, e = full(PRE, "bqk")
            for p in range(2):
                i = act.activation(vec[:, :, VQK:VQK + 4].rearrange("p h (q r) -> p r q h", r=2)[:, p],
                                   b[:, 8 * p:8 * p + 8].rearrange("p (q h) -> p q h", q=2), ACT.Copy)
            i.then_inc(e, 1)
            b, e = full(PRE, "vec2")
            act.activation(vec2[:, :], b[:, 0:40], ACT.Copy).then_inc(e, 1)

            with act.Fori(0, H) as h:
                S(U_HEAD, HEAD, 0, h)
                S(U_HEAD, HEAD, 1, h)
                act.wait_ge(hv_ready, h * 2 + 2)
                for c in range(2):
                    b, e = full(HEAD, f"hist{c}", h)
                    act.activation(samples(E[:, c, :])[:, :, 0:CW - 1], b[:, 0:240].rearrange("p (b w) -> p b w", b=NB), ACT.Copy).then_inc(e, 1)
                for c in range(2):
                    b, e = full(HEAD, f"ub{c}", h)
                    act.activation(sub[:, c, :], b[:, 0:T], ACT.Sigmoid, bias=hv[:, VUB + c:VUB + c + 1]).then_inc(e, 1)
                for u in (2, 3, 4, 5):
                    S(U_HEAD, HEAD, u, h)
                act.wait_ge(head_stored, h + 1)
                b, e = full(HEAD, "uS", h)
                act.activation(u_tok[:, :], b[0:NS, 0:256], ACT.Copy).then_inc(e, 1)
                b, e = full(HEAD, "uP", h)
                act.activation(up_tok[:, :], b[0:CW - 1, 0:256], ACT.Copy).then_inc(e, 1)
                S(U_HEAD, HEAD, 6, h)
                S(U_HEAD, HEAD, 7, h)
                b, e = full(HEAD, "kt0", h)
                for t in range(2):
                    act.activation(kdp[:, t, :], b[0:TT, t * 256:(t + 1) * 256], ACT.Copy, scale=hs[0:TT, HKP + t:HKP + t + 1])
                for s in range(NB):
                    i = act.activation(kds[:, s, :], b[0:NS, 0:256], ACT.Copy, scale=hs[0:NS, HKS + s:HKS + s + 1])
                i.then_inc(e, 1)
                b, e = full(HEAD, "kt1", h)
                act.activation(kdp[:, 2, :], b[0:TT, 0:256], ACT.Copy, scale=hs[0:TT, HKP + 2:HKP + 3]).then_inc(e, 1)
                act.wait_ge(rope_ready, h * 4 + 4)
                for j in range(2):
                    for m in range(2 * j, 2 * j + 2):
                        b, e = full(HEAD, f"g{m}", h)
                        act.activation(rt[:, m, :], b[:, 0:T], ACT.Silu, bias=hv[:, VG + m:VG + m + 1]).then_inc(e, 1)
                    S(U_HEAD, HEAD, 8 + j, h)
                act.wait_ge(rv_ready, h + 1)
                act.activation(rs[:, 1, :], rs[:, 0, :], ACT.Sqrt).then_inc(rstd_done, 1)
                for p in range(2):
                    b, e = full(HEAD, f"ps{p}", h)
                    act.activation(ps_out[:, p, :], b[:, :], ACT.Copy).then_inc(e, 1)
                for t in range(NT):
                    act.wait_ge(*took(HEAD, f"oT{t}", h))
                    act.activation(sg_hi[:, :, t * TT:(t + 1) * TT], sg_f[:, :, :], ACT.Copy).then_inc(sghi_ready, 1)

            act.wait_ge(head_stored, H + 1)
            act.wait_ge(csub_ready, 8)
            act.activation(csq[:, :, :], cT[:, :, :], ACT.Square).then_inc(csq_ready, 1)
            for j in range(4):
                for u, (name, g) in enumerate((("mc", gc), ("mr", gr))):
                    S(U_GATE, GATE, u, j)
                for u, (name, g) in enumerate((("mc", gc), ("mr", gr))):
                    for m in range(2):
                        b, e = full(GATE, f"{name}{m}", j)
                        k = 2 * j + m
                        act.activation(g[:, k, :], b[:, 0:T], ACT.Sigmoid, bias=vec2[:, V2[name] + k:V2[name] + k + 1]).then_inc(e, 1)
            S(U_CONV, CONV, 0, 0)
            act.wait_ge(rv_ready, H + 1)
            act.activation(rstd_c[:, :], rstd_c[:, :], ACT.Sqrt).then_inc(rstd_done, 1)
            for k in range(KT):
                act.wait_ge(cn_ready, k + 1)
                act.activation(cT[:, k, :], cT[:, k, :], ACT.Silu, scale=vec2[:, V2["lng"] + k:V2["lng"] + k + 1],
                               bias=vec2[:, V2["lnb"] + k:V2["lnb"] + k + 1]).then_inc(csilu_ready, 1)
            act.wait_ge(csilu_ready, KT)
            act.activation(c_hi[:, :, :], cT[:, :, :], ACT.Copy).then_inc(chi_ready, 1)
            S(U_CONV, CONV, 1, 0)
            S(U_CONV, CONV, 0, 1)
            S(U_CONV, CONV, 1, 1)
            S(U_WOUT, WOUT, 0, 0)
            S(U_WOUT, WOUT, 1, 0)
            act.wait_ge(mf_ready, 1)
            act.activation(m_hi[:, :, :], gc[:, :, :], ACT.Copy).then_inc(mhi_done, 1)
            S(U_WOUT, WOUT, 2, 0)
            S(U_WOUT, WOUT, 3, 0)
            for t in range(NT):
                act.wait_ge(rv_ready, H + 2 + t)
                act.activation(lnmv[:, t, 3:4], lnmv[:, t, 2:3], ACT.Sqrt).then_inc(rstd_done, 1)
            act.wait_ge(lg_ready, 1)
            act.activation(gt[:, 1, :, :], gt[:, 0, :, :], ACT.Exp).then_inc(exp_ready, 1)

            act.wait_ge(most_ready, 1)
            with act.If(act.value_load(most_i[0:1, 0:1], min_val=0, max_val=T) <= CAP):
                def hi_of(v, stage, it, wit):
                    act.wait_ge(mraw_full[v % MR], (wit * (24 // MR) + (v // MR + 1)) * 16)
                    if v >= MH:
                        act.wait_ge(group_done, stage.done(U_PAIR.last[v - MH], it))
                    elif stage is not FIRST:
                        act.wait_ge(group_done, stage.start(it))
                    act.activation(mhi[:, v % MH, :], mraw[:, v % MR, :], ACT.Copy).then_inc(mhi_ready, 1)

                def turned_hi(stage, name, it, dst, ready):
                    b, e = full(stage, name, it)
                    act.activation(dst, b[:, 0:4 * CAP].rearrange("p (k n) -> p k n", k=4), ACT.Copy).then_inc(ready, 1)

                def swish(stage, name, it):
                    b, e = full(stage, name, it)
                    act.activation(sgt[:, :], b[0:CAP, :], ACT.Silu).then_inc(e, 1)

                def expert(stage, p, it, wit, following):
                    v = 12 * p
                    for u in range(2, 14):
                        if following or u < 12:
                            hi_of(v + u, stage, it, wit)
                        if u == 3:
                            swish(stage, f"g{p}0", it)
                        if u == 5 and following:
                            for j in range(2):
                                turned_hi(stage, f"xt{p}{j}", it, xg_hi[:, 1 - p, 4 * j:4 * j + 4, :], xghi_ready)
                        if u == 7:
                            act.wait_ge(*took(stage, f"u{p}0", it))
                            swish(stage, f"g{p}1", it)
                        if u == 8:
                            turned_hi(stage, f"ht{p}0", it, hT_hi[:, 0:4, :], hthi_ready)
                        if u == 11:
                            turned_hi(stage, f"ht{p}1", it, hT_hi[:, 4:8, :], hthi_ready)
                    act.wait_ge(yo_free, wit * 2 + (p + 1))
                    for n in range(2):
                        b, e = full(stage, f"d{p}{n}", it)
                        act.activation(yo[:, p, 512 * n:512 * n + 512], b[0:CAP, :], ACT.Copy).then_inc(e, 1)

                for j in range(2):
                    turned_hi(FIRST, f"xt{j}", 0, xg_hi[:, 0, 4 * j:4 * j + 4, :], xghi_ready)
                hi_of(0, FIRST, 0, 0)
                hi_of(1, FIRST, 0, 0)
                with act.Fori(0, NE // 2 - 1) as it:
                    for p in range(2):
                        expert(PAIR, p, it, it, True)
                expert(LAST, 0, 0, NE // 2 - 1, True)
                expert(LAST, 1, 0, NE // 2 - 1, False)
            with act.Else():
                for i in range(MR):
                    act.wait_ge(mraw_full[i], 16)
                for i in range(6):
                    t, j = divmod(i, 2)
                    act.activation(x1T_hi[:, 4 * j:4 * j + 4, t * TT:(t + 1) * TT], x1T_f[:, 4 * j:4 * j + 4, t * TT:(t + 1) * TT], ACT.Copy).then_inc(x1hi_ready, 1)
                with act.Fori(0, NE) as e_:
                    for u in range(14):
                        if u < 12:
                            SM(u, e_)
                        v = u - 2
                        if v < 0 or v >= 8:
                            continue
                        j = v // 2
                        if v % 2 == 0:
                            for m in range(2):
                                b, e = full(MOE, f"g{2 * j + m}", e_)
                                act.activation(sgm[:, j % 2, m, :], b[:, 0:T], ACT.Silu).then_inc(e, 1)
                        else:
                            for m in range(2):
                                act.wait_ge(*took(MOE, f"u{2 * j + m}", e_))
                            act.activation(h_hi[:, 2 * j:2 * j + 2, :], h_f[:, :, :], ACT.Copy).then_inc(hhi_ready, 1)

            for t in range(NT):
                act.wait_ge(rv_ready, H + 2 + NT + t)
                act.activation(mmv[:, t, 3:4], mmv[:, t, 2:3], ACT.Sqrt).then_inc(rstd_done, 1)

        @block.vector
        def _(dve):
            step = {"base": 0, "it": 0, "n": 0, "local": 0, "sem": dve_step}

            def count(ins):
                ins.then_inc(step["sem"], 1)
                step["local"] += 1
                return step["it"] * step["n"] + (step["base"] + step["local"])

            def link(ins):
                dve.wait_ge(step["sem"], count(ins))

            def turns(it, n):
                step.update(base=step["base"] + step["local"], it=it, n=n, local=0)

            def turns_end(times):
                assert step["local"] == step["n"], step
                step.update(base=step["base"] + step["n"] * times, it=0, n=0, local=0)

            def L(units, u, it):
                split_lo(dve, units, u, it, 2, 2, raw, hi, lo, hi_ready, lo_ready)

            def LM(u, it):
                split_lo(dve, U_MOE, u, it, DR, MH, mraw, mhi, mlo, mhi_ready, mlo_ready)

            def full(stage, name, it=0):
                dve.wait_ge(group_done, stage.done(name, it))
                return bank[stage.bank[name]], evac[stage.bank[name]]

            dve.memset(zeros[:, :], 0.0).then_inc(zero_ready, 1)
            i = dve.memset(E[:, :, EL:EL + CW - 1], 0.0)
            count(i)
            count(dve.memset(retT[:, :, :], 0.0))
            count(dve.memset(qdiag[:, :, :], 0.0))
            for i in range(6):
                b, e = full(PRE, f"xt{i}")
                t, j = divmod(i, 2)
                a = (slice(None), slice(4 * j, 4 * j + 4), slice(t * TT, (t + 1) * TT))
                dve.wait_ge(s_xhi, i + 1)
                dve.tensor_tensor(xT_lo[a], b[:, 0:4 * TT].rearrange("p (k n) -> p k n", k=4), xT_hi[a].bitcast(f32), ALU.subtract).then_inc(e, 1)
            dve.wait_ge(s_tab, 16)
            for n in ("vec", "bqk", "vec2"):
                dve.wait_ge(*took(PRE, n))
            dve.wait_ge(dve_step, 3)

            def conv(c, h):
                out = cT[:, ds(h * 2 + c, 1), :].rearrange("p a n -> p (a n)")
                parts = [(out[:, NS:T], lambda w: E[:, c, EL + w:EL + w + NP]),
                         (out[:, 0:NS].rearrange("p (b i) -> p b i", b=NB), lambda w: samples(E[:, c, :])[:, :, w:w + NI])]
                last = [None, None]
                for w in range(CW):
                    tap = hv[:, VCW + c * CW + w:VCW + c * CW + w + 1]
                    for q, (o, src) in enumerate(parts):
                        if w == 0:
                            ins = dve.tensor_scalar(o, src(w), tap, hv[:, VCB + c:VCB + c + 1], ALU.mult, ALU.add)
                        else:
                            dve.wait_ge(dve_step, last[q])
                            ins = dve.scalar_tensor_tensor(o, src(w), tap, o, ALU.mult, ALU.add)
                        last[q] = count(ins)
                dve.wait_ge(dve_step, last[1])

            with dve.Fori(0, H) as h:
                turns(h, 4 * CW + 2 * NT + 1)
                dve.tensor_copy(hv[:, :], vec[:, ds(h, 1), :].rearrange("p a n -> p (a n)")).then_inc(hv_ready, 1)
                dve.tensor_copy(hs[:, :], tab[:, ds(h * HS + TB["heads"][0], HS)]).then_inc(hv_ready, 1)
                dve.wait_ge(hv_ready, h * 2 + 2)
                for u in range(3):
                    L(U_HEAD, u, h)
                for c in range(2):
                    b, e = full(HEAD, f"ua{c}", h)
                    dve.wait_ge(*took(HEAD, f"ub{c}", h))
                    bias = hv[:, VUA + c:VUA + c + 1]
                    dve.scalar_tensor_tensor(samples(E[:, c, :])[:, :, CW - 1:CW - 1 + NI], b[:, 0:NS].rearrange("p (b i) -> p b i", b=NB),
                                             bias, sub[:, c, 0:NS].rearrange("p (b i) -> p b i", b=NB), ALU.add, ALU.mult)
                    dve.scalar_tensor_tensor(us[:, c, :], b[:, 0:NS], bias, sub[:, c, 0:NS], ALU.add, ALU.mult)
                    dve.scalar_tensor_tensor(E[:, c, EL + CW - 1:EXT], b[:, NS:T], bias, sub[:, c, NS:T], ALU.add, ALU.mult).then_inc(e, 1)
                L(U_HEAD, 3, h)
                cos, sin = tab[:, TB["cos"][0]:TB["cos"][1]], tab[:, TB["sin"][0]:TB["sin"][1]]
                for n, (name, r) in enumerate((("q", qr), ("k", kr))):
                    for m, (f0, f1) in enumerate(((cos, sin), (sin, cos))):
                        b, e = full(HEAD, f"{name}{m}", h)
                        bias = hv[:, VQK + 2 * n + m:VQK + 2 * n + m + 1]
                        dve.scalar_tensor_tensor(rt[:, 2 * m, :], b[:, 0:T], bias, f0, ALU.add, ALU.mult)
                        dve.scalar_tensor_tensor(rt[:, 2 * m + 1, :], b[:, 0:T], bias, f1, ALU.add, ALU.mult).then_inc(e, 1)
                    for m in range(2):
                        dve.wait_ge(*took(HEAD, f"{name}{m}", h))
                    dve.tensor_tensor(r[:, 0, :], rt[:, 0, :], rt[:, 2, :], ALU.subtract).then_inc(rope_ready, 1)
                    dve.tensor_tensor(r[:, 1, :], rt[:, 1, :], rt[:, 3, :], ALU.add).then_inc(rope_ready, 1)
                    dve.wait_ge(rope_ready, h * 4 + (2 * n + 2))
                    L(U_HEAD, 4 + n, h)
                for p in range(2):
                    dve.tensor_tensor(qdiag[:, p, :].rearrange("p (b x) -> p b x", b=NB)[:, :, 0:NI],
                                      qr[:, p, 0:NS].rearrange("p (b i) -> p b i", b=NB),
                                      hs[:, HQ:HQ + NS].rearrange("p (b i) -> p b i", b=NB), ALU.mult).then_inc(qdiag_ready, 1)
                for c in range(2):
                    dve.wait_ge(*took(HEAD, f"hist{c}", h))
                    dve.wait_ge(*took(HEAD, f"ua{c}", h))
                conv(0, h)
                dve.wait_ge(vb_full, h * 16 + 16)
                for t in range(NT):
                    b, e = full(HEAD, f"v{t}", h)
                    dve.tensor_tensor(v_tok[:, t, :], b[0:TT, :], vb[:, :], ALU.add).then_inc(e, 1)
                L(U_HEAD, 6, h)
                L(U_HEAD, 7, h)
                dve.wait_ge(dec_full, h * 16 + 16)
                for t in range(NT):
                    b, e = full(HEAD, f"att{t}", h)
                    a = slice(ATT_AT[t], ATT_AT[t] + ATT_W[t])
                    dve.tensor_tensor(att[:, a], b[0:TT, 0:ATT_W[t]], dec[:, a], ALU.mult).then_inc(e, 1)
                conv(1, h)
                L(U_HEAD, 8, h)
                L(U_HEAD, 9, h)
                for t in range(NT):
                    b, e = full(HEAD, f"o{t}", h)
                    link(dve.bn_stats(stats[:, t, :], b[0:TT, :]))
                    alone(dve, waits_met)
                    link(dve.bn_aggr(mv[:, t, :], stats[:, t, :]))
                link(dve.tensor_scalar(rs[:, 0, :], mv[:, :, 1], EPS, None, ALU.add))
                dve.reciprocal(rs[:, 0, :], rs[:, 0, :]).then_inc(rv_ready, 1)
                dve.wait_ge(rstd_done, h + 1)
                for t in range(NT):
                    b, e = full(HEAD, f"o{t}", h)
                    dve.tensor_scalar(o_tok[:, t, :], b[0:TT, :], mv[:, t, 0:1], rs[:, 1, t:t + 1], ALU.subtract, ALU.mult).then_inc(e, 1)
                for s in range(NB):
                    for p in range(2):
                        b, e = full(HEAD, f"st{s}{p}", h)
                        dve.scalar_tensor_tensor(st[:, s, p, :], st[:, s, p, :], hs[:, HGAM:HGAM + 1], b[:, :], ALU.mult, ALU.add).then_inc(e, 1)
                for m in range(4):
                    dve.wait_ge(*took(HEAD, f"g{m}", h))
                for t in range(NT):
                    cols = slice(t * TT, (t + 1) * TT)
                    b, e = full(HEAD, f"oT{t}", h)
                    dve.tensor_tensor(sg_f[:, :, :], b[:, 0:4 * TT].rearrange("p (j n) -> p j n", j=4), rt[:, :, cols], ALU.mult).then_inc(e, 1)
                    dve.wait_ge(sghi_ready, h * NT + (t + 1))
                    dve.tensor_tensor(sg_lo[:, :, cols], sg_f[:, :, :], sg_hi[:, :, cols].bitcast(f32), ALU.subtract).then_inc(sglo_ready, 1)
                    dve.wait_ge(sglo_ready, h * NT + (t + 1))
                for m in range(8):
                    b, e = full(HEAD, f"wr{m}", h)
                    dve.tensor_tensor(retT[:, m, :], b[:, 0:T], retT[:, m, :], ALU.add).then_inc(e, 1)
                dve.wait_ge(*took(HEAD, "wr7", h))
                turns_end(H)

            b, e = full(MEAN, "mean")
            for k in range(KT):
                dve.tensor_tensor(cT[:, k, :], cT[:, k, :], b[:, 0:T], ALU.subtract).then_inc(csub_ready, 1)
            dve.wait_ge(csub_ready, KT)
            dve.tensor_copy(rstd_c[:, 0:1], b[:, 0:1]).then_inc(e, 1)
            for j in range(4):
                for u in range(2):
                    L(U_GATE, u, j)
            for n in ("mc0", "mc1", "mr0", "mr1"):
                dve.wait_ge(*took(GATE, n, 3))
            link(dve.tensor_tensor(retT[:, :, :], retT[:, :, :], gr[:, :, :], ALU.mult))
            b, e = full(VAR, "var")
            dve.tensor_scalar(rstd_c[:, :], b[:, 0:T], EPS, None, ALU.add).then_inc(e, 1)
            dve.wait_ge(*took(VAR, "var"))
            dve.reciprocal(rstd_c[:, :], rstd_c[:, :]).then_inc(rv_ready, 1)
            dve.wait_ge(rstd_done, H + 1)
            for k in range(KT):
                dve.tensor_tensor(cT[:, k, :], cT[:, k, :], rstd_c[:, :], ALU.mult).then_inc(cn_ready, 1)
            L(U_CONV, 0, 0)
            dve.wait_ge(chi_ready, 1)
            dve.tensor_tensor(c_lo[:, :, :], cT[:, :, :], c_hi[:, :, :].bitcast(f32), ALU.subtract).then_inc(clo_ready, 1)
            L(U_CONV, 1, 0)
            for j in range(2):
                if j:
                    L(U_CONV, 0, 1)
                for u in range(2):
                    if u == 1 and j:
                        L(U_CONV, 1, 1)
                    for m in range(2):
                        k = 4 * j + 2 * u + m
                        b, e = full(CONV, f"c{2 * u + m}", j)
                        dve.scalar_tensor_tensor(gc[:, k, :], b[:, 0:T], vec2[:, V2["bco"] + k:V2["bco"] + k + 1], gc[:, k, :], ALU.add, ALU.mult).then_inc(e, 1)
            L(U_WOUT, 0, 0)
            L(U_WOUT, 1, 0)
            for m in range(4):
                dve.wait_ge(*took(CONV, f"c{m}", 1))
            dve.tensor_tensor(gc[:, :, :], gc[:, :, :], retT[:, :, :], ALU.add).then_inc(mf_ready, 1)
            dve.wait_ge(mf_ready, 1)
            dve.wait_ge(mhi_done, 1)
            dve.tensor_tensor(m_lo[:, :, :], gc[:, :, :], m_hi[:, :, :].bitcast(f32), ALU.subtract).then_inc(mlo_done, 1)
            L(U_WOUT, 2, 0)
            L(U_WOUT, 3, 0)
            dve.wait_ge(s_xres, 16 * 5)
            dve.wait_ge(s_ln, 32)

            def layernorm(x, t, bc, mst_, mmv_, k, ready):
                for n in range(2):
                    link(dve.bn_stats(mst_[:, t, 6 * n:6 * n + 6], x[:, t, 512 * n:512 * n + 512]))
                link(dve.bn_aggr(mmv_[:, t, 0:2], mst_[:, t, 0:12]))
                link(dve.tensor_scalar(mmv_[:, t, 2:3], mmv_[:, t, 1:2], EPS, None, ALU.add))
                dve.reciprocal(mmv_[:, t, 2:3], mmv_[:, t, 2:3]).then_inc(rv_ready, 1)
                dve.wait_ge(rstd_done, k + t + 1)
                link(dve.tensor_scalar(x[:, t, :], x[:, t, :], mmv_[:, t, 0:1], mmv_[:, t, 3:4], ALU.subtract, ALU.mult))
                link(dve.tensor_tensor(x[:, t, :], x[:, t, :], bc[:, 0, :], ALU.mult))
                dve.tensor_tensor(x[:, t, :], x[:, t, :], bc[:, 1, :], ALU.add).then_inc(ready, 1)

            for n in range(2):
                for t in range(NT):
                    b, e = full(WOUT, f"w{n}{t}")
                    cols = slice(512 * n, 512 * n + 512)
                    dve.scalar_tensor_tensor(x1[:, t, cols], x_tok[:, t, cols], ALPHA, b[0:TT, :], ALU.mult, ALU.add).then_inc(e, 1)
                    if n:
                        for q in range(2):
                            dve.wait_ge(*took(WOUT, f"w{q}{t}"))
                        layernorm(x1, t, ln_bc, lnst, lnmv, H + 1, x1_ready)
            dve.wait_ge(x1_ready, NT)
            for i in range(6):
                t, j = divmod(i, 2)
                b, e = full(X1T, f"xt{i}")
                dve.tensor_copy(x1T_f[:, 4 * j:4 * j + 4, t * TT:(t + 1) * TT], b[:, 0:4 * TT].rearrange("p (k n) -> p k n", k=4)).then_inc(e, 1)
            count(dve.tensor_scalar(y[:, :, :], x1[:, :, :], ALPHA, None, ALU.mult))

            def wide(x):
                return x.unsqueeze(2).to_broadcast([TT, NT, NE])

            b, e = full(X1T, "log")
            for t in range(NT):
                i = dve.tensor_tensor(gt[:, 0, t, :], b[0:TT, t * NE:(t + 1) * NE], br_bc[:, :], ALU.add)
                if t < NT - 1:
                    count(i)
            i.then_inc(e, 1)
            dve.wait_ge(*took(X1T, "log"))
            link(dve.tensor_reduce(gs[:, 0, :], gt[:, 0, :, :], AX.X, ALU.max))
            dve.tensor_tensor(gt[:, 0, :, :], gt[:, 0, :, :], wide(gs[:, 0, :]), ALU.subtract).then_inc(lg_ready, 1)
            dve.wait_ge(exp_ready, 1)
            dve.wait_ge(iota_ready, 1)
            P = gt[:, 1, :, :]
            link(dve.tensor_reduce(gs[:, 1, :], P, AX.X, ALU.add))
            link(dve.reciprocal(gs[:, 2, :], gs[:, 1, :]))
            link(dve.tensor_tensor(P, P, wide(gs[:, 2, :]), ALU.mult))
            link(dve.tensor_reduce(gs[:, 3, :], P, AX.X, ALU.max))
            link(dve.tensor_tensor(gt[:, 2, :, :], P, wide(gs[:, 3, :]), ALU.is_equal))
            link(dve.tensor_tensor(gt[:, 2, :, :], gt[:, 2, :, :], iota_r[:, :, :], ALU.mult))
            link(dve.tensor_reduce(gs[:, 4, :], gt[:, 2, :, :], AX.X, ALU.max))
            link(dve.tensor_tensor(gt[:, 3, :, :], iota_r[:, :, :], wide(gs[:, 4, :]), ALU.is_equal))
            link(dve.tensor_reduce(gg[:, :, :], gt[:, 3, :, :].rearrange("p t (g e) -> p t g e", g=NG), AX.X, ALU.max))
            for q in range(EG):
                link(dve.tensor_tensor(gt[:, 4, :, q:NE:EG], gg[:, :, :], gt[:, 3, :, q:NE:EG], ALU.subtract))
            link(dve.tensor_tensor(gt[:, 5, :, :], P, gt[:, 4, :, :], ALU.mult))
            link(dve.tensor_reduce(gs[:, 5, :], gt[:, 5, :, :], AX.X, ALU.max))
            link(dve.tensor_tensor(gt[:, 6, :, :], gt[:, 5, :, :], wide(gs[:, 5, :]), ALU.is_equal))
            link(dve.tensor_tensor(gt[:, 6, :, :], gt[:, 6, :, :], gt[:, 4, :, :], ALU.mult))
            link(dve.tensor_tensor(gt[:, 6, :, :], gt[:, 6, :, :], iota_r[:, :, :], ALU.mult))
            link(dve.tensor_reduce(gs[:, 6, :], gt[:, 6, :, :], AX.X, ALU.max))
            link(dve.tensor_tensor(gt[:, 6, :, :], iota_r[:, :, :], wide(gs[:, 6, :]), ALU.is_equal))
            dve.tensor_tensor(gt[:, 7, :, :], gt[:, 3, :, :], gt[:, 6, :, :], ALU.add).then_inc(chosen_ready, 1)
            link(dve.tensor_tensor(gs[:, 7, :], gs[:, 3, :], gs[:, 5, :], ALU.add))
            link(dve.reciprocal(gs[:, 7, :], gs[:, 7, :]))
            link(dve.tensor_tensor(gs[:, 3, :], gs[:, 3, :], gs[:, 7, :], ALU.mult))
            link(dve.tensor_tensor(gs[:, 5, :], gs[:, 5, :], gs[:, 7, :], ALU.mult))
            b, e = full(X1T, "pos")
            link(dve.tensor_reduce(most[:, 0:1], b[0:TT, NT * NE:(NT + 1) * NE], AX.X, ALU.max))
            dve.tensor_copy(most_i[:, :], most[:, 0:1]).then_inc(most_ready, 1)
            link(dve.tensor_scalar(gt[:, 0, :, :], iota_r[:, :, :], -float(CAP), float(NE * CAP), ALU.mult, ALU.add))
            dve.tensor_tensor(gt[:, 0, :, :], b[0:TT, 0:NT * NE].rearrange("p (t e) -> p t e", t=NT), gt[:, 0, :, :], ALU.add).then_inc(e, 1)
            dve.wait_ge(*took(X1T, "pos"))
            for k, o in enumerate((3, 6)):
                link(dve.tensor_tensor(gt[:, 1 + k, :, :], gt[:, o, :, :], gt[:, 0, :, :], ALU.mult))
                link(dve.tensor_reduce(gs[:, 1 + k, :], gt[:, 1 + k, :, :], AX.X, ALU.add))
                dve.tensor_copy(slot[:, k, :], gs[:, 1 + k, :]).then_inc(slots_ready, 1)
            most_now = dve.value_load(most_i[0:1, 0:1], min_val=0, max_val=T)
            steps_before = dict(step)
            with dve.If(most_now <= CAP):
                def lo_of(v, wit):
                    dve.wait_ge(mhi_ready, U_PAIR.idx(v, wit) + 1)
                    dve.tensor_tensor(mlo[:, v % MH, :], mraw[:, v % MR, :], mhi[:, v % MH, :].bitcast(f32), ALU.subtract).then_inc(mlo_ready, 1)

                def turned_lo(stage, name, it, lo_, hi_, ready, value):
                    b, e = full(stage, name, it)
                    dve.wait_ge(ready, value)
                    dve.tensor_tensor(lo_, b[:, 0:4 * CAP].rearrange("p (k n) -> p k n", k=4), hi_.bitcast(f32), ALU.subtract).then_inc(e, 1)

                def hidden(stage, p, n, it):
                    b, e = full(stage, f"u{p}{n}", it)
                    dve.wait_ge(*took(stage, f"g{p}{n}", it))
                    dve.tensor_tensor(h_tok[:, 512 * n:512 * n + 512], b[0:CAP, :], sgt[:, :], ALU.mult).then_inc(e, 1)

                def expert(stage, p, it, wit, following):
                    v = 12 * p
                    for u in range(2, 14):
                        if following or u < 12:
                            lo_of(v + u, wit)
                        if u == 5:
                            hidden(stage, p, 0, it)
                            if following:
                                for j in range(2):
                                    turned_lo(stage, f"xt{p}{j}", it, xg_lo[:, 1 - p, 4 * j:4 * j + 4, :], xg_hi[:, 1 - p, 4 * j:4 * j + 4, :],
                                              xghi_ready, wit * 4 + (2 * p + j + 3))
                                if p:
                                    dve.wait_ge(*took(stage, "xt10", it))
                                    alone(dve, waits_met)
                                    dve.wait_ge(*took(stage, "xt11", it))
                                    dve.sem_inc(turned, 1)
                        if u == 8:
                            turned_lo(stage, f"ht{p}0", it, hT_lo[:, 0:4, :], hT_hi[:, 0:4, :], hthi_ready, wit * 4 + (2 * p + 1))
                        if u == 9:
                            hidden(stage, p, 1, it)
                        if u == 11:
                            turned_lo(stage, f"ht{p}1", it, hT_lo[:, 4:8, :], hT_hi[:, 4:8, :], hthi_ready, wit * 4 + (2 * p + 2))

                for j in range(2):
                    turned_lo(FIRST, f"xt{j}", 0, xg_lo[:, 0, 4 * j:4 * j + 4, :], xg_hi[:, 0, 4 * j:4 * j + 4, :], xghi_ready, j + 1)
                for j in range(2):
                    dve.wait_ge(*took(FIRST, f"xt{j}"))
                dve.sem_inc(turned, 1)
                lo_of(0, 0)
                lo_of(1, 0)
                with dve.Fori(0, NE // 2 - 1) as it:
                    for p in range(2):
                        expert(PAIR, p, it, it, True)
                expert(LAST, 0, 0, NE // 2 - 1, True)
                expert(LAST, 1, 0, NE // 2 - 1, False)
                for n in range(2):
                    dve.wait_ge(*took(LAST, f"d1{n}"))
                dve.sem_inc(moe_done, 1)
                for t in range(NT):
                    dve.wait_ge(gathered, 16 * 2 * NT)
                    for k in range(2):
                        g = gs[:, 3 + 2 * k, t:t + 1]
                        link(dve.scalar_tensor_tensor(y[:, t, :], y_back[:, 2 * t + k, :], g, y[:, t, :], ALU.mult, ALU.add))
            with dve.Else():
                steps_gathered, local_gathered = dict(step), step["local"]
                step.update(steps_before)
                link(dve.tensor_tensor(gt[:, 3, :, :], gt[:, 3, :, :], wide(gs[:, 3, :]), ALU.mult))
                link(dve.tensor_tensor(gt[:, 6, :, :], gt[:, 6, :, :], wide(gs[:, 5, :]), ALU.mult))
                link(dve.tensor_tensor(gates[:, :, :], gt[:, 3, :, :], gt[:, 6, :, :], ALU.add))
                for i in range(6):
                    t, j = divmod(i, 2)
                    a = (slice(None), slice(4 * j, 4 * j + 4), slice(t * TT, (t + 1) * TT))
                    dve.wait_ge(x1hi_ready, i + 1)
                    dve.tensor_tensor(x1T_lo[a], x1T_f[a], x1T_hi[a].bitcast(f32), ALU.subtract).then_inc(x1lo_ready, 1)
                with dve.Fori(0, NE) as e_:
                    turns(e_, 1)
                    at_least(dve, evac[MOE.bank["d12"]], MOE.emptied("d12", e_))
                    link(dve.tensor_copy(g_e[:, :], gates[:, :, ds(e_, 1)].rearrange("p t a -> p (t a)")))
                    for u in range(14):
                        if u < 12:
                            LM(u, e_)
                        v = u - 2
                        if v < 0:
                            continue
                        if v < 8 and v % 2:
                            j = v // 2
                            for m in range(2):
                                b, e = full(MOE, f"u{2 * j + m}", e_)
                                dve.wait_ge(*took(MOE, f"g{2 * j + m}", e_))
                                dve.tensor_tensor(h_f[:, m, :], b[:, 0:T], sgm[:, j % 2, m, :], ALU.mult).then_inc(e, 1)
                            for m in range(2):
                                dve.wait_ge(*took(MOE, f"u{2 * j + m}", e_))
                            dve.wait_ge(hhi_ready, e_ * 4 + (j + 1))
                            dve.tensor_tensor(h_lo[:, 2 * j:2 * j + 2, :], h_f[:, :, :], h_hi[:, 2 * j:2 * j + 2, :].bitcast(f32), ALU.subtract).then_inc(hlo_ready, 1)
                            dve.wait_ge(hlo_ready, e_ * 4 + (j + 1))
                        elif v in (9, 11):
                            n = (v - 8) // 2
                            for t in range(NT):
                                b, e = full(MOE, f"d{n}{t}", e_)
                                o = y[:, t, 512 * n:512 * n + 512]
                                at_least(dve, e, MOE.used(f"d{n}{t}", e_))
                                dve.scalar_tensor_tensor(o, b[0:TT, :], g_e[:, t:t + 1], o, ALU.mult, ALU.add).then_inc(e, 1)
                    turns_end(NE)
                for n in range(2):
                    for t in range(NT):
                        dve.wait_ge(*took(MOE, f"d{n}{t}", NE - 1))
                dve.sem_inc(moe_done, 1)
            step.update(base=0, it=0, n=0, local=0, sem=tail_step)
            dve.wait_ge(s_ln2, 32)
            for t in range(NT):
                layernorm(y, t, ln2_bc, mst, mmv, H + 1 + NT, y_ready)


_INS = ["x_prompt", "x_sample", "state_ret", "state_conv", "meta_tokens", "w_in", "b_in", "w_ret_o", "conv_w", "conv_b",
        "conv_ln_g", "conv_ln_b", "w_conv_o", "b_conv_o", "w_out", "ln1_g", "ln1_b", "ln2_g", "ln2_b", "w_router",
        "b_router", "w_gate", "w_up", "w_down", "tables", "decay"]
_OUTS = [((1, SEQ, D), "float32"), ((NB, NI, D), "float32"), ((1, 1, H, DK, DV), "float32"), ((1, 1, CW - 1, D), "float32"),
         ((1, NB, H, DK, DV), "float32"), ((1, NB, CW - 1, D), "float32")]


def kernel(**inputs):
    import numpy as _np
    import concourse.bacc as _bacc
    from concourse import mybir as _mybir
    from concourse.bass_utils import run_bass_kernel_spmd as _run

    nc = _bacc.Bacc("TRN2", target_bir_lowering=False, num_devices=1)
    inputs = {**inputs, **constants()}
    arrays, args = {}, []
    for name in _INS:
        a = _np.ascontiguousarray(inputs[name])
        arrays[f"in_{name}_dram"] = a
        args.append(nc.dram_tensor(f"in_{name}_dram", a.shape, _mybir.dt.from_np(a.dtype), kind="ExternalInput").ap())
    for i, (shape, dtype) in enumerate(_OUTS):
        args.append(nc.dram_tensor(f"out_{i}_dram", shape, _mybir.dt.from_np(_np.dtype(dtype)), kind="ExternalOutput").ap())
    for name in ("x_slots", "y_slots"):
        args.append(nc.dram_tensor(name, (NE * CAP, D), _mybir.dt.float32, kind="Internal").ap())
    program(nc, *args)
    r = _run(nc, [arrays], core_ids=[0])
    return tuple(r.results[0][f"out_{i}_dram"] for i in range(len(_OUTS)))
```

```python
import numpy as np
import concourse.bass as bass
from concourse import mybir
from contextlib import ExitStack

D = 1024
KT = D // 128
H = 4
DK, DV = 256, 512
NB, NI = 8, 8
NS = NB * NI
NM, SEQ = 16, 256
NP = NM + SEQ
T = NS + NP
TT = 112
NT = T // TT
CW = 31
EL = NB * (CW - 1 + NI)
EXT = EL + CW - 1 + NP
NE, NG, EG = 16, 4, 4
CAP = 96
PAST = 2048
EPS = 1e-5
ALPHA = 2.0 ** 0.25
OFF = dict(q=0, k=D, v=2 * D, g=4 * D, ua=6 * D, ub=7 * D, mr=8 * D, mc=9 * D)
ATT_W = [T - i * TT for i in range(NT)]
ATT_AT = [0, ATT_W[0], ATT_W[0] + ATT_W[1]]
HQ, HKP, HKS, HGAM, HS = 0, NS, NS + NT, NS + NT + NB, NS + NT + NB + 1
TB = {}
_at = 0
for _n, _w in (("cos", T), ("sin", T), ("heads", H * HS),
               ("ident", 128), ("mean", 128),
               ("before", TT), ("ones", TT)):
    TB[_n] = (_at, _at + _w)
    _at += _w
TBW = _at
VUB, VUA, VG, VCB, VCW = 0, 2, 4, 8, 10
NV = VCW + 2 * CW
VQK = NV
NVQ = NV + 4
V2 = dict(mc=0, mr=8, lng=16, lnb=24, bco=32)


def constants():
    f = np.float32
    log_g = np.log(f(1.0) - f(2.0) ** (f(-5.0) - np.arange(H, dtype=f))).astype(np.float64)
    pos = np.concatenate([PAST + np.arange(NS) % NI, np.arange(NP)]).astype(f)
    inv = (10000.0 ** (-np.arange(0, DK, 2, dtype=np.float64) / DK)).astype(f)
    ang = (pos[None, :] * inv[:, None]).astype(f).astype(np.float64)
    step = np.concatenate([np.arange(NS) % NI, np.arange(NP)])
    seq = np.concatenate([np.arange(NS) // NI, np.full(NP, NB)])
    diff = step[None, :] - step[:, None]
    ok = (seq[None, :] == seq[:, None]) & (diff >= 0)
    scale = DK ** -0.5
    dec = np.zeros((H, TT, sum(ATT_W)), f)
    tab = np.zeros((128, TBW), f)

    def put(name, a):
        tab[:a.shape[0], TB[name][0]:TB[name][1]] = a

    put("cos", np.cos(ang))
    put("sin", np.sin(ang))
    put("ident", np.eye(128))
    put("mean", np.full((128, 128), 1.0 / D))
    put("before", np.triu(np.ones((TT, TT)), 1))
    put("ones", np.ones((TT, TT)))
    heads = np.zeros((128, H, HS))
    for h in range(H):
        lg = log_g[h]
        full = np.where(ok, np.exp(np.maximum(diff, 0) * lg) * scale, 0.0)
        for i in range(NT):
            dec[h, :, ATT_AT[i]:ATT_AT[i] + ATT_W[i]] = full[i * TT:(i + 1) * TT, i * TT:]
        heads[:, h, HQ:HQ + NS] = np.exp((np.arange(NS) % NI + 1.0) * lg)[None, :]
        kp = np.where(seq == NB, np.exp((NP - 1.0 - step) * lg) * scale, 0.0)
        heads[:TT, h, HKP:HKP + NT] = kp.reshape(NT, TT).T
        for b in range(NB):
            heads[:NS, h, HKS + b] = np.where(np.arange(NS) // NI == b, np.exp((NI - 1.0 - np.arange(NS) % NI) * lg) * scale, 0.0)
        heads[:, h, HGAM] = np.exp(NI * lg)
    put("heads", heads.reshape(128, -1))
    return {"tables": tab, "decay": dec}


class Stage:

    def __init__(self, before, names, times=1):
        self.base = before.base + before.n * before.times if before else 0
        self.uses0 = before.uses_after() if before else [1] * 8
        self.n, self.times = len(names), times
        turn = list(before.turn) if before else [0, 0]
        self.at, self.bank, self.local = {}, {}, {}
        self.per = [0] * 8
        for i, name in enumerate(names):
            kind, name = name[0], name[1:]
            self.at[name] = i
            if kind == "-":
                continue
            k = "FP".index(kind)
            bank = 4 * k + turn[k] % 4
            turn[k] += 1
            self.bank[name] = bank
            self.local[name] = self.per[bank]
            self.per[bank] += 1
        self.turn = turn

    def uses_after(self):
        return [u + p * self.times for u, p in zip(self.uses0, self.per)]

    def done(self, name, it=0):
        return it * self.n + (self.base + self.at[name] + 1)

    def start(self, it=0):
        return it * self.n + self.base

    def used(self, name, it=0):
        b = self.bank[name]
        return it * self.per[b] + (self.uses0[b] + self.local[name])

    def emptied(self, name, it=0):
        b = self.bank[name]
        return it * self.per[b] + self.uses0[b]


def at_least(eng, sem, value):
    if not isinstance(value, int) or value > 0:
        eng.wait_ge(sem, value)


def alone(eng, waits_met):
    eng.sem_inc(waits_met, 1)


class Units:

    def __init__(self, before, n, times, last, tail):
        self.base = before.base + before.n * before.times if before else 0
        self.n, self.times, self.last, self.tail = n, times, last, tail

    def idx(self, u, it=0):
        return it * self.n + (self.base + u)


def program(nc, x_prompt, x_sample, state_ret, state_conv, meta_tokens, w_in, b_in, w_ret_o, conv_w, conv_b,
            conv_ln_g, conv_ln_b, w_conv_o, b_conv_o, w_out, ln1_g, ln1_b, ln2_g, ln2_b, w_router, b_router,
            w_gate, w_up, w_down, tables, decay,
            y_prompt, y_sample, new_ret_prompt, new_conv_prompt, new_ret_sample, new_conv_sample,
            x_slots, y_slots):
    f32, f32r = mybir.dt.float32, mybir.dt.float32r
    ALU, ACT, AX = mybir.AluOpType, mybir.ActivationFunctionType, mybir.AxisListType
    ds = bass.ds
    W2 = TT * 2

    ctx = ExitStack()
    with ctx:
        base = [(nc.sbuf_base + 31) // 32 * 32]
        high = [0]

        def sb(name, shape, dt=f32):
            size = 4 * int(np.prod(shape[1:]))
            t = nc.alloc_sbuf_tensor_at(name, shape, dt, offset=base[0])
            base[0] += (size + 31) // 32 * 32
            high[0] = max(high[0], base[0])
            return t

        def sem(name):
            return ctx.enter_context(nc.semaphore(name))

        tab = sb("tab", [128, TBW])
        vec = sb("vec", [128, H, NVQ])
        vec2 = sb("vec2", [128, 40])
        zeros = sb("zeros", [128, 256])
        wr_sb = sb("wr_sb", [128, KT, NE])
        br_bc = sb("br_bc", [TT, NE])
        persistent = base[0]
        xT_hi = sb("xT_hi", [128, KT, T], f32r)
        xT_lo = sb("xT_lo", [128, KT, T], f32r)
        raw = sb("raw", [128, 2, 2048])
        hi = sb("hi", [128, 2, 2048], f32r)
        lo = sb("lo", [128, 2, 2048], f32r)
        cT = sb("cT", [128, KT, T])
        retT = sb("retT", [128, KT, T])
        phase = base[0]
        st = sb("st", [128, NB, 2, DV])
        dec = sb("dec", [TT, sum(ATT_W)])
        E = sb("E", [128, 2, EXT])
        us = sb("us", [128, 2, NS])
        hist = sb("hist", [120, 2, 256])
        hv = sb("hv", [128, NVQ])
        hs = sb("hs", [128, HS])
        sub = sb("sub", [128, 2, T])
        qr = sb("qr", [128, 2, T])
        kr = sb("kr", [128, 2, T])
        rt = sb("rt", [128, 4, T])
        v_tok = sb("v_tok", [TT, NT, DV])
        vb = sb("vb", [TT, DV])
        kdp = sb("kdp", [TT, NT, 256])
        kds_hi = sb("kds_hi", [TT, NB, 256], f32r)
        v_hi = sb("v_hi", [TT, DV], f32r)
        att = sb("att", [TT, sum(ATT_W)])
        qdiag = sb("qdiag", [128, 2, NB * (NS + NI)])
        o_tok = sb("o_tok", [TT, NT, DV])
        sg_f = sb("sg_f", [128, 4, TT])
        sg_hi = sb("sg_hi", [128, 4, T], f32r)
        sg_lo = sb("sg_lo", [128, 4, T], f32r)
        after = base[0]
        base[0] -= 2 * 4 * 4 * T
        kds_lo = sb("kds_lo", [TT, NB, 256], f32r)
        v_lo = sb("v_lo", [TT, DV], f32r)
        assert base[0] <= after
        base[0] = after
        ps_out = sb("ps_out", [128, 2, DV])
        u_tok = sb("u_tok", [NS, 256])
        up_tok = sb("up_tok", [CW - 1, 256])
        stats = sb("stats", [TT, NT, 6])
        mv = sb("mv", [TT, NT, 2])
        rs = sb("rs", [TT, 2, NT])
        base[0] = phase
        x_in = sb("x_in", [TT, NT, D])
        vrows = sb("vrows", [NV, H, 128])
        qkrows = sb("qkrows", [8, 256])
        v2rows = sb("v2rows", [40, 128])
        assert base[0] <= phase + 4 * NB * 2 * DV
        base[0] = phase
        x_tok = sb("x_tok", [TT, NT, D])
        x1 = sb("x1", [TT, NT, D])
        c_hi = sb("c_hi", [128, KT, T], f32r)
        c_lo = sb("c_lo", [128, KT, T], f32r)
        gc = sb("gc", [128, KT, T])
        gr = sb("gr", [128, KT, T])
        m_hi = sb("m_hi", [128, KT, T], f32r)
        csq = nc.alloc_sbuf_tensor_at("csq", [128, KT, T], f32, offset=base[0] - 4 * KT * T)
        m_lo = xT_lo
        rstd_c = sb("rstd_c", [128, T])
        lnst = sb("lnst", [TT, NT, 12])
        lnmv = sb("lnmv", [TT, NT, 4])
        ln_bc = sb("ln_bc", [TT, 2, D])
        MR, MH = 8, 3
        DR = 4
        base[0] = persistent
        y = sb("y", [TT, NT, D])
        gates = sb("gates", [TT, NT, NE])
        gt = sb("gt", [TT, 8, NT, NE])
        gs = sb("gs", [TT, 8, NT])
        gg = sb("gg", [TT, NT, NG])
        g_e = sb("g_e", [TT, NT])
        iota_r = sb("iota_r", [TT, NT, NE])
        slot = sb("slot", [TT, 2, NT], mybir.dt.int32)
        most = sb("most", [TT, 2])
        most_i = sb("most_i", [TT, 1], mybir.dt.int32)
        mst = sb("mst", [TT, NT, 12])
        mmv = sb("mmv", [TT, NT, 4])
        mhi = sb("mhi", [128, MH, 2048], f32r)
        mlo = sb("mlo", [128, MH, 2048], f32r)
        x1T_f = sb("x1T_f", [128, KT, T])
        xg_hi = sb("xg_hi", [128, 2, KT, CAP], f32r)
        shared = base[0]
        xg_lo = sb("xg_lo", [128, 2, KT, CAP], f32r)
        assert base[0] <= phase, (base[0], phase)
        base[0] = phase
        h_tok = sb("h_tok", [CAP, D])
        hT_hi = sb("hT_hi", [128, KT, CAP], f32r)
        hT_lo = sb("hT_lo", [128, KT, CAP], f32r)
        assert base[0] <= phase + 4 * NT * D
        base[0] = phase + 4 * NT * D
        yo = sb("yo", [CAP, 2, D])
        base[0] = phase + 2 * 4 * NT * D
        mraw = sb("mraw", [128, MR, 2048])
        xg_tok = sb("xg_tok", [CAP, 2, D])
        sgt = sb("sgt", [CAP, 512])
        ln2_bc = sb("ln2_bc", [TT, 2, D])
        base[0] = phase + 2 * 4 * NT * D
        y_back = sb("y_back", [TT, 2 * NT, D])
        base[0] = phase
        h_hi = sb("h_hi", [128, KT, T], f32r)
        h_lo = sb("h_lo", [128, KT, T], f32r)
        base[0] = phase + 2 * 4 * NT * D + DR * 8192
        x1T_hi = sb("x1T_hi", [128, KT, T], f32r)
        x1T_lo = sb("x1T_lo", [128, KT, T], f32r)
        assert base[0] <= phase + 2 * 4 * NT * D + MR * 8192 + 2 * 4 * D
        base[0] = shared - 4 * 2 * KT * CAP
        sgm = sb("sgm", [128, 2, 2, T])
        h_f = sb("h_f", [128, 2, T])
        assert base[0] <= phase
        assert high[0] <= nc.sbuf_usable_end, (high[0], nc.sbuf_usable_end)

        bank = [ctx.enter_context(nc.psum_tensor(f"bank{i}", [128, 512], f32)) for i in range(8)]
        ident = tab[:, TB["ident"][0]:TB["ident"][1]]

        PRE = Stage(None, [f"Pxt{i}" for i in range(6)] + ["Pvec", "Pbqk", "Pvec2"])
        HEAD = Stage(PRE, ["Fub0", "Fub1", "Fua0", "Fua1", "Phist0", "Phist1", "Fq0", "Fq1", "Fk0", "Fk1",
                           "PuS", "PuP", "-vp0", "-vp1", "-vp2", "Pv0", "Pv1", "Pv2", "Pkt0", "Pkt1",
                           "Patt0", "Patt1", "Fg0", "Fg1", "Patt2", "Fg2", "Fg3", "Po0", "Po1", "Po2"]
                     + [f"Pst{b}{p}" for b in range(NB) for p in range(2)]
                     + [f"PoT{i}" for i in range(NT)] + ["Pps0", "Pps1"] + [f"Fwr{m}" for m in range(8)], H)
        GATE = Stage(HEAD, ["Fmc0", "Fmc1", "Fmr0", "Fmr1"])
        MEAN = Stage(GATE, ["Pmean"])
        GATE1 = Stage(MEAN, ["Fmc0", "Fmc1", "Fmr0", "Fmr1"])
        VAR = Stage(GATE1, ["Pvar"])
        GATE2 = Stage(VAR, ["Fmc0", "Fmc1", "Fmr0", "Fmr1"], 2)
        CONV = Stage(GATE2, ["Fc0", "Fc1", "Fc2", "Fc3"], 2)
        WOUT = Stage(CONV, [x for n in range(2) for x in [f"-wp{n}{t}" for t in range(NT)] + [f"Pw{n}{t}" for t in range(NT)]])
        X1T = Stage(WOUT, [x for t in range(NT) for x in (f"Pxt{2 * t}", f"Pxt{2 * t + 1}", f"Plog{t}")] + ["Ppos"])
        MNAMES = [x for j in range(4) for x in (f"Fg{2 * j}", f"Fg{2 * j + 1}", f"Fu{2 * j}", f"Fu{2 * j + 1}")]
        MNAMES += [x for n in range(2) for x in [f"-dp{n}{t}" for t in range(NT)] + [f"Pd{n}{t}" for t in range(NT)]]
        MOE = Stage(X1T, MNAMES, NE)
        def expert_groups(p, following):
            return ([f"-g{p}0a", f"Fg{p}0", f"-u{p}0a", f"Fu{p}0", f"-g{p}1a", f"Fg{p}1", f"Pht{p}0"]
                    + [f"Pxt{p}{j}" for j in range(2)] * following + [f"-u{p}1a", f"Fu{p}1", f"-d{p}0a", f"Pht{p}1", f"-d{p}1a",
                       f"Pd{p}0", f"Pd{p}1"])
        FIRST = Stage(X1T, ["Pxt0", "Pxt1"])
        PAIR = Stage(FIRST, expert_groups(0, 1) + expert_groups(1, 1), NE // 2 - 1)
        LAST = Stage(PAIR, expert_groups(0, 1) + expert_groups(1, 0))

        U_HEAD = Units(None, 10, H, ["ub1", "ua1", "q1", "k1", "vp2", "v2", "g1", "g3", "wr3", "wr7"], [4])
        U_GATE = Units(U_HEAD, 2, 4, ["mc1", "mr1"], [2])
        U_CONV = Units(U_GATE, 2, 2, ["c1", "c3"], [2])
        U_WOUT = Units(U_CONV, 4, 1, ["wp02", "w02", "wp12", "w12"], [2])
        NORMS = 2 * H
        U_MOE = Units(None, 12, NE, [f"{x}{2 * j + 1}" for j in range(4) for x in "gu"] + ["dp02", "d02", "dp12", "d12"], [3, 3])

        def unit_groups(p):
            return [f"g{p}0a", f"g{p}0", f"u{p}0a", f"u{p}0", f"g{p}1a", f"g{p}1", f"u{p}1a", f"u{p}1",
                    f"d{p}0a", f"d{p}1a", f"d{p}0", f"d{p}1"]
        U_PAIR = Units(None, 24, NE // 2, unit_groups(0) + unit_groups(1), None)

        LEAD, MLEAD = 2, MR
        group_done = sem("group_done")
        evac = [sem(f"evac{i}") for i in range(8)]
        raw_full = [sem(f"raw_full{i}") for i in range(2)]
        hi_ready, lo_ready = sem("hi_ready"), sem("lo_ready")
        mraw_full = [sem(f"mraw_full{i}") for i in range(MR)]
        mhi_ready, mlo_ready = sem("mhi_ready"), sem("mlo_ready")
        s_tab, s_x, s_rows, s_xhi = sem("s_tab"), sem("s_x"), sem("s_rows"), sem("s_xhi")
        st_full = [sem(f"st_full{b}") for b in range(NB)]
        st_out = [sem(f"st_out{b}") for b in range(NB)]
        dec_full, hist_full, vb_full = sem("dec_full"), sem("hist_full"), sem("vb_full")
        hv_ready = sem("hv_ready")
        rope_ready, qdiag_ready = sem("rope_ready"), sem("qdiag_ready")
        sghi_ready, sglo_ready = sem("sghi_ready"), sem("sglo_ready")
        out_sem, ps_stored, u_stored = sem("out_sem"), sem("ps_stored"), sem("u_stored")
        kds_ready, v_ready, vhi_ready, vlo_ready = (sem(n) for n in ("kds_ready", "v_ready", "vhi_ready", "vlo_ready"))
        conv_done = sem("conv_done")
        rv_ready, rstd_done = sem("rv_ready"), sem("rstd_done")
        dve_step = sem("dve_step")
        tail_step = sem("tail_step")
        csub_ready, csq_ready, cn_ready, csilu_ready = (sem(n) for n in ("csub_ready", "csq_ready", "cn_ready", "csilu_ready"))
        chi_ready, clo_ready = sem("chi_ready"), sem("clo_ready")
        mf_ready, mhi_done, mlo_done = sem("mf_ready"), sem("mhi_done"), sem("mlo_done")
        s_xres, s_ln, s_ln2, s_wrt = sem("s_xres"), sem("s_ln"), sem("s_ln2"), sem("s_wrt")
        x1_ready, x1hi_ready, x1lo_ready = (sem(n) for n in ("x1_ready", "x1hi_ready", "x1lo_ready"))
        lg_ready, exp_ready, iota_ready = sem("lg_ready"), sem("exp_ready"), sem("iota_ready")
        hhi_ready, hlo_ready = sem("hhi_ready"), sem("hlo_ready")
        zeroed, zero_ready = sem("zeroed"), sem("zero_ready")
        most_ready, slots_ready, scattered = (sem(n) for n in ("most_ready", "slots_ready", "scattered"))
        gathered = [sem(f"gathered{t}") for t in range(NT)]
        xg_full = [sem(f"xg_full{i}") for i in range(2)]
        xghi_ready, hthi_ready = sem("xghi_ready"), sem("hthi_ready")
        turned = sem("turned")
        chosen_ready = sem("chosen_ready")
        yo_stored, yo_free, moe_done = sem("yo_stored"), sem("yo_free"), sem("moe_done")
        y_ready, moved_up = sem("y_ready"), sem("moved_up")
        normed = sem("normed")
        head_stored = sem("head_stored")
        waits_met = sem("waits_met")

        w_in_v = w_in[0].rearrange("(t p) n -> p t n", p=128)
        w_ret_v = w_ret_o[0].rearrange("(t p) n -> p t n", p=128)
        w_conv_v = w_conv_o[0].rearrange("(t p) n -> p t n", p=128)
        w_out_v = w_out[0].rearrange("(t p) n -> p t n", p=128)

        nc_ok = ctx.enter_context(nc.allow_non_contiguous_dma("small vectors and slices of rows"))
        block = ctx.enter_context(nc.Block())

        def F_view(t, slot):
            return t[:, slot, :].rearrange("p (k n) -> p k n", k=KT)

        def T_view(t, slot):
            return t[:, slot, :].rearrange("p (k n) -> p k n", k=4)

        def samples(ap):
            return ap[:, 0:EL].rearrange("p (b w) -> p b w", b=NB)

        @block.sync
        def _(sp):
            sp.sem_inc(lo_ready, LEAD)
            sp.sem_inc(mlo_ready, MLEAD)
            for i in range(8):
                sp.sem_inc(evac[i], 1)
            sp.dma_start(tab[:], tables).then_inc(s_tab, 16)
            sp.dma_start(x_in[0:NS, 0, :], x_sample.rearrange("b i d -> (b i) d")).then_inc(s_x, 16)
            sp.dma_start(x_in[NS:NS + NM, 0, :], meta_tokens).then_inc(s_x, 16)
            sp.dma_start(x_in[NS + NM:TT, 0, :], x_prompt[0, 0:TT - NS - NM, :]).then_inc(s_x, 16)
            for t in range(1, NT):
                a = t * TT - NS - NM
                sp.dma_start(x_in[:, t, :], x_prompt[0, a:a + TT, :]).then_inc(s_x, 16)

            def unit(units, u, it, parts, view=F_view):
                c = units.idx(u, it)
                at_least(sp, lo_ready, c - 1 + LEAD)
                alone(sp, waits_met)
                slot = u % 2
                for a, b, src in parts:
                    sp.dma_start(view(raw, slot)[:, :, a:b], src).then_inc(raw_full[slot], 16)

            with sp.Fori(0, H) as h:
                for u, name in enumerate(("ub", "ua", "q", "k")):
                    unit(U_HEAD, u, h, [(0, 256, w_in_v[:, :, ds(h * 256 + OFF[name], 256)])])
                for j in range(2):
                    unit(U_HEAD, 4 + j, h, [(0, DV, w_in_v[:, 4 * j:4 * j + 4, ds(h * DV + OFF["v"], DV)])], T_view)
                for j in range(2):
                    unit(U_HEAD, 6 + j, h, [(0, 256, w_in_v[:, :, ds(h * DV + (OFF["g"] + 256 * j), 256)])])
                for j in range(2):
                    unit(U_HEAD, 8 + j, h, [(0, 512, w_ret_v[:, ds(h * 4, 4), 512 * j:512 * j + 512])], T_view)
            with sp.Fori(0, 4) as j:
                for u, name in enumerate(("mc", "mr")):
                    unit(U_GATE, u, j, [(0, 256, w_in_v[:, :, ds(j * 256 + OFF[name], 256)])])
            with sp.Fori(0, 2) as j:
                for u in range(2):
                    unit(U_CONV, u, j, [(0, 256, w_conv_v[:, :, ds(j * 512 + 256 * u, 256)])])
            for n in range(2):
                for half in range(2):
                    unit(U_WOUT, 2 * n + half, 0, [(0, 512, w_out_v[:, 4 * half:4 * half + 4, 512 * n:512 * n + 512])], T_view)

            def pair_unit(v, it):
                if v >= MR:
                    sp.wait_ge(mlo_ready, U_PAIR.idx(v, it) + (MLEAD + 1 - MR))
                    alone(sp, waits_met)
                more, v = divmod(v, 24)
                p, u = divmod(v, 12)
                w, n, half = ((w_gate, 0, u), (w_up, 0, u - 2), (w_gate, 1, u - 4), (w_up, 1, u - 6))[u // 2] if u < 8 else (w_down, u % 2, (u - 8) // 2)
                e = it * 2 + (2 * more + p)
                src = w[0][ds(e, 1)].rearrange("e (t p) n -> p (e t) n", p=128)
                sp.dma_start(T_view(mraw, v % MR), src[:, 4 * half:4 * half + 4, 512 * n:512 * n + 512]).then_inc(mraw_full[v % MR], 16)

            sp.wait_ge(mlo_done, 2)
            for v in range(MR):
                if v == 5:
                    sp.wait_ge(group_done, WOUT.done("w12"))
                if v == 6:
                    sp.wait_ge(x1_ready, NT)
                pair_unit(v, 0)
            sp.wait_ge(most_ready, 1)
            with sp.If(sp.value_load(most_i[0:1, 0:1], min_val=0, max_val=T) <= CAP):
                with sp.Fori(0, NE // 2 - 1) as it:
                    for v in range(MR, MR + 24):
                        pair_unit(v, it)
                for v in range(MR, 24):
                    pair_unit(v, NE // 2 - 1)
            with sp.Else():
                for i in range(MR):
                    sp.wait_ge(mraw_full[i], 16)
                with sp.Fori(0, NE) as e:
                    for u in range(12):
                        c = U_MOE.idx(u, e)
                        sp.wait_ge(mlo_ready, c + (MLEAD + 1 - DR))
                        alone(sp, waits_met)
                        slot_ = u % DR
                        if u < 8:
                            src = (w_gate, w_up)[u % 2][0][ds(e, 1)].rearrange("e (t p) n -> p (e t) n", p=128)
                            sp.dma_start(F_view(mraw, slot_), src[:, :, 256 * (u // 2):256 * (u // 2) + 256]).then_inc(mraw_full[slot_], 16)
                        else:
                            n, half = divmod(u - 8, 2)
                            src = w_down[0][ds(e, 1)].rearrange("e (t p) n -> p (e t) n", p=128)
                            sp.dma_start(T_view(mraw, slot_), src[:, 4 * half:4 * half + 4, 512 * n:512 * n + 512]).then_inc(mraw_full[slot_], 16)
            sp.wait_ge(moe_done, 1)
            sp.dma_start(ln2_bc[:, 0, :], ln2_g.to_broadcast([TT, D])).then_inc(s_ln2, 16)
            sp.dma_start(ln2_bc[:, 1, :], ln2_b.to_broadcast([TT, D])).then_inc(s_ln2, 16)

            for t in range(NT):
                if t < NT - 1:
                    sp.wait_ge(y_ready, t + 1)
                else:
                    sp.wait_ge(normed, NT)
                if t == 0:
                    sp.dma_start(y_sample.rearrange("b i d -> (b i) d"), y[0:NS, 0, :]).then_inc(out_sem, 16)
                    sp.dma_start(y_prompt[0, 0:TT - NS - NM, :], y[NS + NM:TT, 0, :]).then_inc(out_sem, 16)
                else:
                    a = t * TT - NS - NM
                    sp.dma_start(y_prompt[0, a:a + TT, :], y[:, t, :]).then_inc(out_sem, 16)
            sp.wait_ge(out_sem, 16 * (NT + 1))

        N_ROWS = 12

        @block.gpsimd
        def _(pool):
            def rows(dst, src):
                pool.dma_start(dst, src).then_inc(s_rows, 16)

            b_v = b_in[0].rearrange("(a p) -> a p", p=128)
            hj = lambda off, j: b_in[0, off:off + H * j * 128].rearrange("(h j p) -> j h p", h=H, j=j)
            rows(vrows[VUB:VUB + 2, :, :], hj(OFF["ub"], 2))
            rows(vrows[VUA:VUA + 2, :, :], hj(OFF["ua"], 2))
            rows(vrows[VG:VG + 4, :, :], hj(OFF["g"], 4))
            rows(vrows[VCB:VCB + 2, :, :], conv_b[0].rearrange("(h j p) -> j h p", h=H, j=2))
            for j in range(2):
                rows(vrows[VCW + j * CW:VCW + (j + 1) * CW, :, :],
                     conv_w[0].rearrange("w (h j p) -> j w h p", h=H, j=2)[j])
            rows(qkrows[:, :], b_in[0, 0:2 * D].rearrange("(a p) -> a p", p=256))
            for name, src in (("mc", b_v[OFF["mc"] // 128:OFF["mc"] // 128 + 8, :]),
                              ("mr", b_v[OFF["mr"] // 128:OFF["mr"] // 128 + 8, :]),
                              ("lng", conv_ln_g[0].rearrange("(a p) -> a p", p=128)),
                              ("lnb", conv_ln_b[0].rearrange("(a p) -> a p", p=128)),
                              ("bco", b_conv_o[0].rearrange("(a p) -> a p", p=128))):
                rows(v2rows[V2[name]:V2[name] + 8, :], src)
            pool.dma_start(wr_sb[:], w_router.rearrange("(t p) n -> p t n", p=128)).then_inc(s_wrt, 16)
            pool.dma_start(br_bc[:], b_router.rearrange("(a n) -> a n", a=1).to_broadcast([TT, NE])).then_inc(s_wrt, 16)
            pool.wait_ge(group_done, PRE.done("vec2"))
            pool.sem_inc(head_stored, 1)
            with pool.Fori(0, H) as h:
                at_least(pool, group_done, HEAD.start(h))
                alone(pool, waits_met)
                pool.dma_start(hist[:, :, :], state_conv[0].rearrange("(a b) w c -> (b w) a c", a=2)[:, :, ds(h * 256, 256)]
                               ).then_inc(hist_full, 16)
                pool.dma_start(vb[:, :], b_in[0:1, ds(h * DV + OFF["v"], DV)].to_broadcast([TT, DV])).then_inc(vb_full, 16)
                pool.dma_start(dec[:, :], decay[ds(h, 1)].rearrange("h p n -> p (h n)")).then_inc(dec_full, 16)
                for b in range(NB):
                    pool.dma_start(st[:, b, :, :], state_ret[0, b][ds(h, 1)].rearrange("h (p t) n -> p (h t) n", t=2)
                                   ).then_inc(st_full[b], 16)
                pool.wait_ge(evac[HEAD.bank["uS"]], HEAD.used("uS", h) + 1)
                alone(pool, waits_met)
                for b in range(NB):
                    pool.dma_start(new_conv_sample[0, b, CW - 1 - NI:CW - 1, ds(h * 256, 256)],
                                   u_tok[b * NI:(b + 1) * NI, :]).then_inc(u_stored, 16)
                pool.wait_ge(evac[HEAD.bank["uP"]], HEAD.used("uP", h) + 1)
                alone(pool, waits_met)
                pool.dma_start(new_conv_prompt[0, 0, :, ds(h * 256, 256)], up_tok[:, :]).then_inc(u_stored, 16)
                for b in range(NB):
                    for p in range(2):
                        n = f"st{b}{p}"
                        pool.wait_ge(evac[HEAD.bank[n]], HEAD.used(n, h) + 1)
                        alone(pool, waits_met)
                    pool.dma_start(new_ret_sample[0, b][ds(h, 1)].rearrange("h (p t) n -> p (h t) n", t=2), st[:, b, :, :]
                                   ).then_inc(st_out[b], 16)
                pool.wait_ge(evac[HEAD.bank["ps1"]], HEAD.used("ps1", h) + 1)
                alone(pool, waits_met)
                pool.dma_start(new_ret_prompt[0, 0][ds(h, 1)].rearrange("h (p t) n -> p (h t) n", t=2), ps_out[:, :, :]
                               ).then_inc(ps_stored, 16)
                for b in range(NB):
                    pool.wait_ge(st_out[b], h * 16 + 16)
                    alone(pool, waits_met)
                pool.wait_ge(ps_stored, h * 16 + 16)
                alone(pool, waits_met)
                pool.wait_ge(u_stored, h * (16 * (NB + 1)) + 16 * (NB + 1))
                pool.sem_inc(head_stored, 1)
            pool.wait_ge(group_done, GATE.start())
            pool.wait_ge(evac[HEAD.bank["wr7"]], HEAD.used("wr7", H - 1) + 1)
            pool.dma_start(x_tok[0:NS, 0, :], x_sample.rearrange("b i d -> (b i) d")).then_inc(s_xres, 16)
            pool.dma_start(x_tok[NS:NS + NM, 0, :], meta_tokens).then_inc(s_xres, 16)
            pool.dma_start(x_tok[NS + NM:TT, 0, :], x_prompt[0, 0:TT - NS - NM, :]).then_inc(s_xres, 16)
            for t in range(1, NT):
                a = t * TT - NS - NM
                pool.dma_start(x_tok[:, t, :], x_prompt[0, a:a + TT, :]).then_inc(s_xres, 16)
            pool.dma_start(ln_bc[:, 0, :], ln1_g.to_broadcast([TT, D])).then_inc(s_ln, 16)
            pool.dma_start(ln_bc[:, 1, :], ln1_b.to_broadcast([TT, D])).then_inc(s_ln, 16)
            pool.dma_start(new_conv_sample[0, :, 0:CW - 1 - NI, :], state_conv[0, :, NI:CW - 1, :]).then_inc(moved_up, 16)
            pool.wait_ge(zero_ready, 1)
            for r in range(NE * CAP // 128):
                pool.dma_start(x_slots[r * 128:(r + 1) * 128, :].rearrange("p (a c) -> p a c", a=4),
                               zeros[:, :].unsqueeze(1).to_broadcast([128, 4, 256])).then_inc(zeroed, 16)
            pool.wait_ge(group_done, WOUT.done("w12"))
            pool.wait_ge(x1_ready, NT)
            for e in range(NE):
                i = pool.memset(iota_r[:, :, e:e + 1], float(NE - e))
            i.then_inc(iota_ready, 1)
            pool.wait_ge(moved_up, 16)
            pool.wait_ge(zeroed, 16 * (NE * CAP // 128))
            pool.wait_ge(most_ready, 1)
            pool.wait_ge(slots_ready, 2)
            with pool.If(pool.value_load(most_i[0:1, 0:1], min_val=0, max_val=T) <= CAP):
                for k in range(2):
                    for t in range(NT):
                        pool.indirect_dma_start(x_slots, bass.IndirectOffsetOnAxis(slot[:, k, t:t + 1], 0), x1[:, t, :], None
                                                ).then_inc(scattered, 16)
                pool.wait_ge(scattered, 16 * 2 * NT)
                pool.sem_inc(yo_free, 2)
                for e in range(2):
                    pool.dma_start(xg_tok[:, e, :], x_slots[e * CAP:(e + 1) * CAP, :]).then_inc(xg_full[e], 16)

                def stored(stage, p, it):
                    n = f"d{p}1"
                    pool.wait_ge(evac[stage.bank[n]], stage.used(n, it) + 1)
                    alone(pool, waits_met)

                with pool.Fori(0, NE // 2 - 1) as it:
                    for p in range(2):
                        stored(PAIR, p, it)
                        pool.dma_start(y_slots[ds((it * 2 + p) * CAP, CAP), :], yo[:, p, :]).then_inc(yo_stored, 16)
                        pool.dma_start(xg_tok[:, p, :], x_slots[ds((it * 2 + (p + 2)) * CAP, CAP), :]).then_inc(xg_full[p], 16)
                        pool.wait_ge(yo_stored, it * 32 + (16 * p + 16))
                        pool.sem_inc(yo_free, 1)
                for p in range(2):
                    stored(LAST, p, 0)
                    pool.dma_start(y_slots[(NE - 2 + p) * CAP:(NE - 1 + p) * CAP, :], yo[:, p, :]).then_inc(yo_stored, 16)
                pool.wait_ge(yo_stored, 16 * NE)
                for t in range(NT):
                    for k in range(2):
                        pool.indirect_dma_start(y_back[:, 2 * t + k, :], None, y_slots, bass.IndirectOffsetOnAxis(slot[:, k, t:t + 1], 0)
                                                ).then_inc(gathered[t], 16)
                for t in range(NT):
                    pool.wait_ge(gathered[t], 32)
            pool.wait_ge(s_ln2, 32)
            for t in range(NT - 1):
                pool.wait_ge(normed, t + 1)
                pool.tensor_tensor(y[:, t, :], y[:, t, :], ln2_bc[:, 1, :], ALU.add).then_inc(y_ready, 1)

        @block.tensor
        def _(pe):
            def group(stage, name, it, mms, begin=True, m=128, n=512):
                for out, a, b, s, e in mms:
                    i = pe.matmul(out, a, b, start=s, stop=e)
                i.then_inc(group_done, 1)

            def room(stage, name, it):
                at_least(pe, evac[stage.bank[name]], stage.used(name, it))

            def split_ready(units, u, it):
                pe.wait_ge(lo_ready, units.idx(u, it) + (1 + LEAD))

            def three(out, w_h, w_l, x_h, x_l, first, last):
                return [(out, w_h, x_h, first, False), (out, w_h, x_l, False, False), (out, w_l, x_h, False, last)]

            def f_group(stage, name, it, wh, wl, cols, xh, xl, kts=KT):
                room(stage, name, it)
                out = bank[stage.bank[name]][:, 0:T]
                mms = []
                for k in range(kts):
                    mms += three(out, wh[:, k, cols], wl[:, k, cols], xh[:, k, :], xl[:, k, :], k == 0, k == kts - 1)
                group(stage, name, it, mms)

            def t_unit(stage, half, parts, finals, it, wh, wl, xh, xl):
                for t in range(NT):
                    name = finals[t]
                    if half == 0:
                        room(stage, name, it)
                    out = bank[stage.bank[name]][0:TT, :]
                    mms = []
                    for k in range(4):
                        kk = 4 * half + k
                        first, last = half == 0 and k == 0, half == 1 and k == 3
                        xs = slice(t * TT, (t + 1) * TT)
                        mms += [(out, xh[:, kk, xs], wh[:, k, :], first, False), (out, xh[:, kk, xs], wl[:, k, :], False, False),
                                (out, xl[:, kk, xs], wh[:, k, :], False, last)]
                    group(stage, name, it, mms)

            def turn(stage, name, it, parts):
                room(stage, name, it)
                alone(pe, waits_met)
                for out, in_, n in parts:
                    i = pe.transpose(out, in_, ident[0:n, 0:n])
                i.then_inc(group_done, 1)

            def gathered_path():
                def tokens(stage, names, q, it, value):
                    pe.wait_ge(xg_full[q], value)
                    for j, name in enumerate(names):
                        b = bank[stage.bank[name]]
                        turn(stage, name, it, [(b[:, i * CAP:(i + 1) * CAP], xg_tok[:, q, (4 * j + i) * 128:(4 * j + i + 1) * 128], CAP) for i in range(4)])

                def half(stage, v, it, wit, name, kh, xh, xl):
                    pe.wait_ge(mlo_ready, U_PAIR.idx(v, wit) + (1 + MLEAD))
                    if kh == 0:
                        room(stage, name, it)
                    out = bank[stage.bank[name]][0:CAP, :]
                    wh, wl = T_view(mhi, v % MH), T_view(mlo, v % MH)
                    mms = []
                    for k in range(4):
                        kk = 4 * kh + k
                        mms += [(out, xh[:, kk, :], wh[:, k, :], kk == 0, False), (out, xh[:, kk, :], wl[:, k, :], False, False),
                                (out, xl[:, kk, :], wh[:, k, :], False, kk == KT - 1)]
                    group(stage, name, it, mms)

                def h_turn(stage, p, j, it):
                    pe.wait_ge(evac[stage.bank[f"u{p}{j}"]], stage.used(f"u{p}{j}", it) + 1)
                    alone(pe, waits_met)
                    b = bank[stage.bank[f"ht{p}{j}"]]
                    turn(stage, f"ht{p}{j}", it, [(b[:, i * CAP:(i + 1) * CAP], h_tok[:, (4 * j + i) * 128:(4 * j + i + 1) * 128], CAP) for i in range(4)])

                def evacuated(stage, name, it):
                    pe.wait_ge(evac[stage.bank[name]], stage.used(name, it) + 1)

                def expert(stage, p, it, wit, following):
                    v = 12 * p
                    xh, xl = xg_hi[:, p], xg_lo[:, p]
                    if p:
                        for j in range(2):
                            evacuated(stage, f"xt0{j}", it)
                    for u, name in ((0, f"g{p}0"), (2, f"u{p}0")):
                        for kh in range(2):
                            half(stage, v + u + kh, it, wit, name, kh, xh, xl)
                    for kh in range(2):
                        half(stage, v + 4 + kh, it, wit, f"g{p}1", kh, xh, xl)
                    h_turn(stage, p, 0, it)
                    if following:
                        tokens(stage, (f"xt{p}0", f"xt{p}1"), 1 - p, it, wit * 16 + (16 * p + 16))
                    for kh in range(2):
                        half(stage, v + 6 + kh, it, wit, f"u{p}1", kh, xh, xl)
                    for kh in range(2):
                        evacuated(stage, f"ht{p}{kh}", it)
                        for n in range(2):
                            half(stage, v + 8 + 2 * kh + n, it, wit, f"d{p}{n}", kh, hT_hi, hT_lo)
                            if kh == 0 and n == 0:
                                h_turn(stage, p, 1, it)

                tokens(FIRST, ("xt0", "xt1"), 0, 0, 16)
                for j in range(2):
                    evacuated(FIRST, f"xt{j}", 0)
                with pe.Fori(0, NE // 2 - 1) as it:
                    for p in range(2):
                        if p == 0:
                            pe.wait_ge(turned, it + 1)
                        expert(PAIR, p, it, it, True)
                pe.wait_ge(turned, NE // 2)
                expert(LAST, 0, 0, NE // 2 - 1, True)
                expert(LAST, 1, 0, NE // 2 - 1, False)

            def dense_path():
                pe.wait_ge(x1lo_ready, 6)
                with pe.Fori(0, NE) as e:
                    for u in range(12):
                        pe.wait_ge(mlo_ready, U_MOE.idx(u, e) + (1 + MLEAD))
                        s = u % MH
                        if u < 8:
                            for m in range(2):
                                f_group(MOE, f"{'gu'[u % 2]}{2 * (u // 2) + m}", e, F_view(mhi, s), F_view(mlo, s), slice(m * 128, (m + 1) * 128), x1T_hi, x1T_lo)
                        else:
                            n, half = divmod(u - 8, 2)
                            if u == 8:
                                pe.wait_ge(hlo_ready, e * 4 + 4)
                            t_unit(MOE, half, None, [f"d{n}{t}" for t in range(NT)], e, T_view(mhi, s), T_view(mlo, s), h_hi, h_lo)

            pe.wait_ge(s_tab, 16)
            pe.wait_ge(s_x, 16 * 5)
            for t in range(NT):
                for j in range(2):
                    n = f"xt{2 * t + j}"
                    b = bank[PRE.bank[n]]
                    turn(PRE, n, 0, [(b[:, i * TT:(i + 1) * TT], x_in[:, t, (4 * j + i) * 128:(4 * j + i + 1) * 128], TT) for i in range(4)])
            pe.wait_ge(s_rows, 16 * N_ROWS)
            b = bank[PRE.bank["vec"]]
            turn(PRE, "vec", 0, [(b[:, h * NV:(h + 1) * NV], vrows[:, h, :], NV) for h in range(H)])
            b = bank[PRE.bank["bqk"]]
            turn(PRE, "bqk", 0, [(b[:, 8 * p:8 * p + 8], qkrows[:, p:256:2], 8) for p in range(2)])
            b = bank[PRE.bank["vec2"]]
            turn(PRE, "vec2", 0, [(b[:, 0:40], v2rows[:, :], 40)])
            for n in [f"xt{i}" for i in range(6)]:
                pe.wait_ge(evac[PRE.bank[n]], PRE.used(n) + 1)

            with pe.Fori(0, H) as h:
                for u, name in enumerate(("ub", "ua", "q", "k")):
                    if u == 2:
                        pe.wait_ge(hist_full, h * 16 + 16)
                        for c in range(2):
                            b = bank[HEAD.bank[f"hist{c}"]]
                            turn(HEAD, f"hist{c}", h, [(b[:, a * 120:a * 120 + 120], hist[:, a, c * 128:(c + 1) * 128], 120) for a in range(2)])
                    split_ready(U_HEAD, u, h)
                    wh, wl = F_view(hi, u % 2), F_view(lo, u % 2)
                    for m in range(2):
                        cols = slice(m * 128, (m + 1) * 128) if u < 2 else slice(m, 256, 2)
                        f_group(HEAD, f"{name}{m}", h, wh, wl, cols, xT_hi, xT_lo)
                for c in range(2):
                    pe.wait_ge(evac[HEAD.bank[f"ua{c}"]], HEAD.used(f"ua{c}", h) + 1)
                b = bank[HEAD.bank["uS"]]
                turn(HEAD, "uS", h, [(b[0:NS, c * 128:(c + 1) * 128], us[:, c, :], 128) for c in range(2)])
                b = bank[HEAD.bank["uP"]]
                turn(HEAD, "uP", h, [(b[0:CW - 1, c * 128:(c + 1) * 128], E[:, c, EXT - CW + 1:EXT], 128) for c in range(2)])
                for half in range(2):
                    split_ready(U_HEAD, 4 + half, h)
                    t_unit(HEAD, half, None, [f"v{t}" for t in range(NT)], h, T_view(hi, half), T_view(lo, half), xT_hi, xT_lo)
                pe.wait_ge(rope_ready, h * 4 + 4)
                for g, tiles in enumerate(((0, 1), (2,))):
                    b = bank[HEAD.bank[f"kt{g}"]]
                    turn(HEAD, f"kt{g}", h, [(b[0:TT, (2 * i + p) * 128:(2 * i + p + 1) * 128], kr[:, p, t * TT:(t + 1) * TT], 128)
                                             for i, t in enumerate(tiles) for p in range(2)])
                def scores(i):
                    name = f"att{i}"
                    room(HEAD, name, h)
                    out = bank[HEAD.bank[name]][0:TT, 0:ATT_W[i]]
                    group(HEAD, name, h, [(out, kr[:, p, i * TT:(i + 1) * TT], qr[:, p, i * TT:T], p == 0, p == 1) for p in range(2)])

                scores(0)
                scores(1)
                for j in range(2):
                    u = 6 + j
                    split_ready(U_HEAD, u, h)
                    for m in range(2):
                        f_group(HEAD, f"g{2 * j + m}", h, F_view(hi, u % 2), F_view(lo, u % 2), slice(m * 128, (m + 1) * 128), xT_hi, xT_lo)
                    if j == 0:
                        scores(2)
                for t in range(NT):
                    pe.wait_ge(evac[HEAD.bank[f"v{t}"]], HEAD.used(f"v{t}", h) + 1)
                    pe.wait_ge(evac[HEAD.bank[f"att{t}"]], HEAD.used(f"att{t}", h) + 1)
                for t in range(NT):
                    name = f"o{t}"
                    room(HEAD, name, h)
                    out = bank[HEAD.bank[name]][0:TT, :]
                    mms = [(out, att[:, ATT_AT[i] + (t - i) * TT:ATT_AT[i] + (t - i + 1) * TT], v_tok[:, i, :], i == 0, i == t)
                           for i in range(t + 1)]
                    if t == 0:
                        for a, l, r, s, e in mms:
                            pe.matmul(a, l, r, start=s, stop=e)
                        pe.wait_ge(qdiag_ready, h * 2 + 2)
                        for b in range(NB):
                            pe.wait_ge(st_full[b], h * 16 + 16)
                        o64 = bank[HEAD.bank[name]][0:NS, :]
                        for b in range(NB):
                            for p in range(2):
                                i = pe.matmul(o64, qdiag[:, p, b * NS:(b + 1) * NS], st[:, b, p, :], start=False, stop=(b == NB - 1 and p == 1), skip_group_check=True)
                        i.then_inc(group_done, 1)
                    else:
                        group(HEAD, name, h, mms)
                pe.wait_ge(vlo_ready, h + 1)
                pe.wait_ge(evac[HEAD.bank["kt0"]], HEAD.used("kt0", h) + 1)
                pe.wait_ge(evac[HEAD.bank["kt1"]], HEAD.used("kt1", h) + 1)
                alone(pe, waits_met)
                for b in range(NB):
                    for p in range(2):
                        name = f"st{b}{p}"
                        room(HEAD, name, h)
                        out, cols = bank[HEAD.bank[name]][:, :], slice(p * 128, (p + 1) * 128)
                        group(HEAD, name, h, [(out, kds_hi[:, b, cols], v_hi[:, :], True, False), (out, kds_hi[:, b, cols], v_lo[:, :], False, False),
                                              (out, kds_lo[:, b, cols], v_hi[:, :], False, True)])
                for t in range(NT):
                    pe.wait_ge(evac[HEAD.bank[f"o{t}"]], HEAD.used(f"o{t}", h) + 1)
                    b = bank[HEAD.bank[f"oT{t}"]]
                    turn(HEAD, f"oT{t}", h, [(b[:, j * TT:(j + 1) * TT], o_tok[:, t, j * 128:(j + 1) * 128], TT) for j in range(4)])
                for p in range(2):
                    name = f"ps{p}"
                    room(HEAD, name, h)
                    group(HEAD, name, h, [(bank[HEAD.bank[name]][:, :], kdp[:, t, p * 128:(p + 1) * 128], v_tok[:, t, :], t == 0, t == NT - 1) for t in range(NT)])
                pe.wait_ge(sglo_ready, h * NT + NT)
                for j in range(2):
                    split_ready(U_HEAD, 8 + j, h)
                    for m in range(4):
                        f_group(HEAD, f"wr{4 * j + m}", h, T_view(hi, j), T_view(lo, j), slice(m * 128, (m + 1) * 128), sg_hi, sg_lo, 4)

            def gates(stage, first, j):
                for u, name in enumerate(("mc", "mr")):
                    split_ready(U_GATE, u + 2 * first, j)
                    for m in range(2):
                        f_group(stage, f"{name}{m}", j, F_view(hi, u), F_view(lo, u), slice(m * 128, (m + 1) * 128), xT_hi, xT_lo)

            gates(GATE, 0, 0)
            pe.wait_ge(conv_done, 1)
            ones = tab[:, TB["mean"][0]:TB["mean"][1]]
            pe.wait_ge(evac[HEAD.bank["wr7"]], HEAD.used("wr7", H - 1) + 1)
            room(MEAN, "mean", 0)
            group(MEAN, "mean", 0, [(bank[MEAN.bank["mean"]][:, 0:T], ones, cT[:, k, :], k == 0, k == KT - 1) for k in range(KT)])
            gates(GATE1, 1, 0)
            pe.wait_ge(csq_ready, 1)
            room(VAR, "var", 0)
            group(VAR, "var", 0, [(bank[VAR.bank["var"]][:, 0:T], ones, csq[:, k, :], k == 0, k == KT - 1) for k in range(KT)])
            with pe.Fori(0, 2) as j:
                gates(GATE2, 2, j)
            pe.wait_ge(clo_ready, 1)
            with pe.Fori(0, 2) as j:
                for u in range(2):
                    split_ready(U_CONV, u, j)
                    for m in range(2):
                        f_group(CONV, f"c{2 * u + m}", j, F_view(hi, u), F_view(lo, u), slice(m * 128, (m + 1) * 128), c_hi, c_lo)
            for n in range(2):
                for half in range(2):
                    pe.wait_ge(mlo_done, half + 1)
                    split_ready(U_WOUT, 2 * n + half, 0)
                    t_unit(WOUT, half, None, [f"w{n}{t}" for t in range(NT)], 0, T_view(hi, half), T_view(lo, half), m_hi, m_lo)
            def router(t):
                for n in (2 * t, 2 * t + 1):
                    pe.wait_ge(evac[X1T.bank[f"xt{n}"]], X1T.used(f"xt{n}") + 1)
                room(X1T, f"log{t}", 0)
                out = bank[X1T.bank[f"log{t}"]]
                group(X1T, f"log{t}", 0, [(out[0:TT, 0:NE], x1T_f[:, k, t * TT:(t + 1) * TT], wr_sb[:, k, :], k == 0, k == KT - 1) for k in range(KT)])

            pe.wait_ge(s_wrt, 32)
            for t in range(NT):
                pe.wait_ge(x1_ready, t + 1)
                for j in range(2):
                    n = f"xt{2 * t + j}"
                    b = bank[X1T.bank[n]]
                    turn(X1T, n, 0, [(b[:, i * TT:(i + 1) * TT], x1[:, t, (4 * j + i) * 128:(4 * j + i + 1) * 128], TT) for i in range(4)])
                router(t)
            pe.wait_ge(chosen_ready, 1)
            room(X1T, "pos", 0)
            before, ones_t = (tab[0:TT, TB[n][0]:TB[n][1]] for n in ("before", "ones"))
            out = bank[X1T.bank["pos"]]
            for t in range(NT + 1):
                o = out[0:TT, t * NE:(t + 1) * NE]
                for i in range(min(t, NT - 1) + 1):
                    last = pe.matmul(o, before if i == t else ones_t, gt[:, 7, i, :], start=(i == 0), stop=(i == min(t, NT - 1)))
            last.then_inc(group_done, 1)
            pe.wait_ge(most_ready, 1)
            with pe.If(pe.value_load(most_i[0:1, 0:1], min_val=0, max_val=T) <= CAP):
                gathered_path()
            with pe.Else():
                dense_path()


        def split_hi(act, units, stage, u, it, R, RH, src, dst, full, ready, used=0):
            slot, hslot = u % R, u % RH
            act.wait_ge(full[slot], (it * (units.n // R) + ((units.base + u) // R + 1 + used)) * 16)
            if u >= RH:
                act.wait_ge(group_done, stage.done(units.last[u - RH], it))
            else:
                act.wait_ge(group_done, stage.start(it) - sum(units.tail[:RH - 1 - u]))
            act.activation(dst[:, hslot, :], src[:, slot, :], ACT.Copy).then_inc(ready, 1)

        def split_lo(dve, units, u, it, R, RH, src, h, l, hready, lready):
            dve.wait_ge(hready, units.idx(u, it) + 1)
            dve.tensor_tensor(l[:, u % RH, :], src[:, u % R, :], h[:, u % RH, :].bitcast(f32), ALU.subtract).then_inc(lready, 1)

        def took(stage, name, it=0):
            return evac[stage.bank[name]], stage.used(name, it) + 1

        @block.scalar
        def _(act):
            def S(units, stage, u, it):
                split_hi(act, units, stage, u, it, 2, 2, raw, hi, raw_full, hi_ready)

            def SM(u, it):
                split_hi(act, U_MOE, MOE, u, it, DR, MH, mraw, mhi, mraw_full, mhi_ready, 1)

            def full(stage, name, it=0):
                act.wait_ge(group_done, stage.done(name, it))
                return bank[stage.bank[name]], evac[stage.bank[name]]

            for i in range(6):
                b, e = full(PRE, f"xt{i}")
                t, j = divmod(i, 2)
                act.activation(xT_hi[:, 4 * j:4 * j + 4, t * TT:(t + 1) * TT], b[:, 0:4 * TT].rearrange("p (k n) -> p k n", k=4), ACT.Copy).then_inc(s_xhi, 1)
            b, e = full(PRE, "vec")
            act.activation(vec[:, :, 0:NV], b[:, 0:H * NV].rearrange("p (h n) -> p h n", h=H), ACT.Copy).then_inc(e, 1)
            b, e = full(PRE, "bqk")
            for p in range(2):
                i = act.activation(vec[:, :, VQK:VQK + 4].rearrange("p h (q r) -> p r q h", r=2)[:, p],
                                   b[:, 8 * p:8 * p + 8].rearrange("p (q h) -> p q h", q=2), ACT.Copy)
            i.then_inc(e, 1)
            b, e = full(PRE, "vec2")
            act.activation(vec2[:, :], b[:, 0:40], ACT.Copy).then_inc(e, 1)

            act.wait_ge(raw_full[0], 16)
            act.activation(hi[:, 0, :], raw[:, 0, :], ACT.Copy).then_inc(hi_ready, 1)
            with act.Fori(0, H) as h:
                S(U_HEAD, HEAD, 1, h)
                act.wait_ge(hv_ready, h * 2 + 2)
                for c in range(2):
                    b, e = full(HEAD, f"ub{c}", h)
                    act.activation(sub[:, c, :], b[:, 0:T], ACT.Sigmoid, bias=hv[:, VUB + c:VUB + c + 1]).then_inc(e, 1)
                S(U_HEAD, HEAD, 2, h)
                S(U_HEAD, HEAD, 3, h)
                for c in range(2):
                    b, e = full(HEAD, f"hist{c}", h)
                    act.activation(samples(E[:, c, :])[:, :, 0:CW - 1], b[:, 0:240].rearrange("p (b w) -> p b w", b=NB), ACT.Copy).then_inc(e, 1)
                for u in (4, 5):
                    S(U_HEAD, HEAD, u, h)
                act.wait_ge(head_stored, h + 1)
                b, e = full(HEAD, "uS", h)
                act.activation(u_tok[:, :], b[0:NS, 0:256], ACT.Copy).then_inc(e, 1)
                b, e = full(HEAD, "uP", h)
                act.activation(up_tok[:, :], b[0:CW - 1, 0:256], ACT.Copy).then_inc(e, 1)
                S(U_HEAD, HEAD, 6, h)
                S(U_HEAD, HEAD, 7, h)
                b, e = full(HEAD, "kt0", h)
                for t in range(2):
                    act.activation(kdp[:, t, :], b[0:TT, t * 256:(t + 1) * 256], ACT.Copy, scale=hs[0:TT, HKP + t:HKP + t + 1])
                for s in range(NB):
                    i = act.activation(kds_hi[:, s, :], b[0:TT, 0:256], ACT.Copy, scale=hs[0:TT, HKS + s:HKS + s + 1])
                i.then_inc(kds_ready, 1)
                b, e = full(HEAD, "kt1", h)
                act.activation(kdp[:, 2, :], b[0:TT, 0:256], ACT.Copy, scale=hs[0:TT, HKP + 2:HKP + 3]).then_inc(e, 1)
                act.wait_ge(v_ready, h + 1)
                act.activation(v_hi[:, :], v_tok[:, 0, :], ACT.Copy).then_inc(vhi_ready, 1)
                act.wait_ge(rope_ready, h * 4 + 4)
                for j in range(2):
                    for m in range(2 * j, 2 * j + 2):
                        b, e = full(HEAD, f"g{m}", h)
                        act.activation(rt[:, m, :], b[:, 0:T], ACT.Silu, bias=hv[:, VG + m:VG + m + 1]).then_inc(e, 1)
                    S(U_HEAD, HEAD, 8 + j, h)
                for n, tt in enumerate((slice(0, 2), slice(2, 3))):
                    act.wait_ge(rv_ready, h * 2 + (n + 1))
                    act.activation(rs[:, 1, tt], rs[:, 0, tt], ACT.Sqrt).then_inc(rstd_done, 1)
                for t in range(NT):
                    act.wait_ge(*took(HEAD, f"oT{t}", h))
                    act.activation(sg_hi[:, :, t * TT:(t + 1) * TT], sg_f[:, :, :], ACT.Copy).then_inc(sghi_ready, 1)
                for p in range(2):
                    b, e = full(HEAD, f"ps{p}", h)
                    act.activation(ps_out[:, p, :], b[:, :], ACT.Copy).then_inc(e, 1)
                S(U_HEAD, HEAD, 10, h)

            act.wait_ge(head_stored, H + 1)
            S(U_GATE, GATE, 1, 0)
            def normalised():
                act.wait_ge(rv_ready, NORMS + 1)
                act.activation(rstd_c[:, :], rstd_c[:, :], ACT.Sqrt).then_inc(rstd_done, 1)
                for k in range(KT):
                    act.wait_ge(cn_ready, k + 1)
                    act.activation(cT[:, k, :], cT[:, k, :], ACT.Silu, scale=vec2[:, V2["lng"] + k:V2["lng"] + k + 1],
                                   bias=vec2[:, V2["lnb"] + k:V2["lnb"] + k + 1]).then_inc(csilu_ready, 1)

            def gates(stage, it, j, between=None):
                for u, (name, g) in enumerate((("mc", gc), ("mr", gr))):
                    if u and between:
                        between()
                    for m in range(2):
                        b, e = full(stage, f"{name}{m}", it)
                        k = 2 * j + m
                        act.activation(g[:, k, :], b[:, 0:T], ACT.Sigmoid, bias=vec2[:, V2[name] + k:V2[name] + k + 1]).then_inc(e, 1)
                    slot = u
                    act.wait_ge(raw_full[slot], 16 * ((U_GATE.base + 2 * j + 2 + u) // 2 + 1))
                    act.activation(hi[:, slot, :], raw[:, slot, :], ACT.Copy).then_inc(hi_ready, 1)

            gates(GATE, 0, 0)
            act.wait_ge(csub_ready, 8)
            act.activation(csq[:, :, :], cT[:, :, :], ACT.Square).then_inc(csq_ready, 1)
            gates(GATE1, 0, 1)
            gates(GATE2, 0, 2, normalised)
            act.wait_ge(csilu_ready, KT)
            act.activation(c_hi[:, :, :], cT[:, :, :], ACT.Copy).then_inc(chi_ready, 1)
            gates(GATE2, 1, 3)
            for j in range(2):
                S(U_CONV, CONV, 2, j)
                S(U_CONV, CONV, 3, j)
                act.wait_ge(mf_ready, j + 1)
                act.activation(m_hi[:, 4 * j:4 * j + 4, :], gc[:, 4 * j:4 * j + 4, :], ACT.Copy).then_inc(mhi_done, 1)
            S(U_WOUT, WOUT, 2, 0)
            S(U_WOUT, WOUT, 3, 0)
            for t in range(NT):
                act.wait_ge(rv_ready, NORMS + 2 + t)
                act.activation(lnmv[:, t, 3:4], lnmv[:, t, 2:3], ACT.Sqrt).then_inc(rstd_done, 1)
                for j in range(2):
                    b, e = full(X1T, f"xt{2 * t + j}")
                    act.activation(x1T_f[:, 4 * j:4 * j + 4, t * TT:(t + 1) * TT], b[:, 0:4 * TT].rearrange("p (k n) -> p k n", k=4), ACT.Copy).then_inc(e, 1)
            act.wait_ge(lg_ready, 1)
            act.activation(gt[:, 1, :, :], gt[:, 0, :, :], ACT.Exp).then_inc(exp_ready, 1)

            act.wait_ge(most_ready, 1)
            with act.If(act.value_load(most_i[0:1, 0:1], min_val=0, max_val=T) <= CAP):
                def hi_of(v, stage, it, wit):
                    act.wait_ge(mraw_full[v % MR], (wit * (24 // MR) + (v // MR + 1)) * 16)
                    if v >= MH:
                        act.wait_ge(group_done, stage.done(U_PAIR.last[v - MH], it))
                    elif stage is not FIRST:
                        act.wait_ge(group_done, stage.start(it))
                    act.activation(mhi[:, v % MH, :], mraw[:, v % MR, :], ACT.Copy).then_inc(mhi_ready, 1)

                def turned_hi(stage, name, it, dst, ready):
                    b, e = full(stage, name, it)
                    act.activation(dst, b[:, 0:4 * CAP].rearrange("p (k n) -> p k n", k=4), ACT.Copy).then_inc(ready, 1)

                def swish(stage, name, it):
                    b, e = full(stage, name, it)
                    act.activation(sgt[:, :], b[0:CAP, :], ACT.Silu).then_inc(e, 1)

                def expert(stage, p, it, wit, following):
                    v = 12 * p
                    for u in range(2, 14):
                        if following or u < 12:
                            hi_of(v + u, stage, it, wit)
                        if u == 3:
                            swish(stage, f"g{p}0", it)
                        if u == 7:
                            act.wait_ge(*took(stage, f"u{p}0", it))
                            swish(stage, f"g{p}1", it)
                        if u == 8:
                            turned_hi(stage, f"ht{p}0", it, hT_hi[:, 0:4, :], hthi_ready)
                            for j in range(2 * following):
                                turned_hi(stage, f"xt{p}{j}", it, xg_hi[:, 1 - p, 4 * j:4 * j + 4, :], xghi_ready)
                        if u == 10:
                            turned_hi(stage, f"ht{p}1", it, hT_hi[:, 4:8, :], hthi_ready)
                    act.wait_ge(yo_free, wit * 2 + (p + 1))
                    for n in range(2):
                        b, e = full(stage, f"d{p}{n}", it)
                        act.activation(yo[:, p, 512 * n:512 * n + 512], b[0:CAP, :], ACT.Copy).then_inc(e, 1)

                hi_of(0, FIRST, 0, 0)
                hi_of(1, FIRST, 0, 0)
                for j in range(2):
                    turned_hi(FIRST, f"xt{j}", 0, xg_hi[:, 0, 4 * j:4 * j + 4, :], xghi_ready)
                with act.Fori(0, NE // 2 - 1) as it:
                    for p in range(2):
                        expert(PAIR, p, it, it, True)
                expert(LAST, 0, 0, NE // 2 - 1, True)
                expert(LAST, 1, 0, NE // 2 - 1, False)
            with act.Else():
                for i in range(MR):
                    act.wait_ge(mraw_full[i], 16)
                for i in range(6):
                    t, j = divmod(i, 2)
                    act.activation(x1T_hi[:, 4 * j:4 * j + 4, t * TT:(t + 1) * TT], x1T_f[:, 4 * j:4 * j + 4, t * TT:(t + 1) * TT], ACT.Copy).then_inc(x1hi_ready, 1)
                with act.Fori(0, NE) as e_:
                    for u in range(14):
                        if u < 12:
                            SM(u, e_)
                        v = u - 2
                        if v < 0 or v >= 8:
                            continue
                        j = v // 2
                        if v % 2 == 0:
                            for m in range(2):
                                b, e = full(MOE, f"g{2 * j + m}", e_)
                                act.activation(sgm[:, j % 2, m, :], b[:, 0:T], ACT.Silu).then_inc(e, 1)
                        else:
                            for m in range(2):
                                act.wait_ge(*took(MOE, f"u{2 * j + m}", e_))
                            act.activation(h_hi[:, 2 * j:2 * j + 2, :], h_f[:, :, :], ACT.Copy).then_inc(hhi_ready, 1)

            for t in range(NT):
                act.wait_ge(rv_ready, NORMS + 2 + NT + t)
                act.activation(mmv[:, t, 3:4], mmv[:, t, 2:3], ACT.Sqrt).then_inc(rstd_done, 1)

        @block.vector
        def _(dve):
            step = {"base": 0, "it": 0, "n": 0, "local": 0, "sem": dve_step}

            def count(ins):
                ins.then_inc(step["sem"], 1)
                step["local"] += 1
                return step["it"] * step["n"] + (step["base"] + step["local"])

            def link(ins):
                dve.wait_ge(step["sem"], count(ins))

            def turns(it, n):
                step.update(base=step["base"] + step["local"], it=it, n=n, local=0)

            def turns_end(times):
                assert step["local"] == step["n"], step
                step.update(base=step["base"] + step["n"] * times, it=0, n=0, local=0)

            def L(units, u, it):
                split_lo(dve, units, u, it, 2, 2, raw, hi, lo, hi_ready, lo_ready)

            def LM(u, it):
                split_lo(dve, U_MOE, u, it, DR, MH, mraw, mhi, mlo, mhi_ready, mlo_ready)

            def full(stage, name, it=0):
                dve.wait_ge(group_done, stage.done(name, it))
                return bank[stage.bank[name]], evac[stage.bank[name]]

            dve.memset(zeros[:, :], 0.0).then_inc(zero_ready, 1)
            i = dve.memset(E[:, :, EL:EL + CW - 1], 0.0)
            count(i)
            count(dve.memset(retT[:, :, :], 0.0))
            count(dve.memset(qdiag[:, :, :], 0.0))
            for i in range(6):
                b, e = full(PRE, f"xt{i}")
                t, j = divmod(i, 2)
                a = (slice(None), slice(4 * j, 4 * j + 4), slice(t * TT, (t + 1) * TT))
                dve.wait_ge(s_xhi, i + 1)
                dve.tensor_tensor(xT_lo[a], b[:, 0:4 * TT].rearrange("p (k n) -> p k n", k=4), xT_hi[a].bitcast(f32), ALU.subtract).then_inc(e, 1)
            dve.wait_ge(s_tab, 16)
            for n in ("vec", "bqk", "vec2"):
                dve.wait_ge(*took(PRE, n))
            dve.wait_ge(dve_step, 3)

            conv_last = [None, None]

            def conv(c, h, w0, w1):
                out = cT[:, ds(h * 2 + c, 1), :].rearrange("p a n -> p (a n)")
                parts = [(out[:, NS:T], lambda w: E[:, c, EL + w:EL + w + NP]),
                         (out[:, 0:NS].rearrange("p (b i) -> p b i", b=NB), lambda w: samples(E[:, c, :])[:, :, w:w + NI])]
                for w in range(w0, w1):
                    tap = hv[:, VCW + c * CW + w:VCW + c * CW + w + 1]
                    for q, (o, src) in enumerate(parts):
                        if w == 0:
                            ins = dve.tensor_scalar(o, src(w), tap, hv[:, VCB + c:VCB + c + 1], ALU.mult, ALU.add)
                        else:
                            dve.wait_ge(dve_step, conv_last[q])
                            ins = dve.scalar_tensor_tensor(o, src(w), tap, o, ALU.mult, ALU.add)
                        conv_last[q] = count(ins)
                if w1 == CW:
                    dve.wait_ge(dve_step, conv_last[1])

            L(U_HEAD, 0, 0)
            with dve.Fori(0, H) as h:
                turns(h, 4 * CW + 2 * NT + 2)
                dve.tensor_copy(hv[:, :], vec[:, ds(h, 1), :].rearrange("p a n -> p (a n)")).then_inc(hv_ready, 1)
                dve.tensor_copy(hs[:, :], tab[:, ds(h * HS + TB["heads"][0], HS)]).then_inc(hv_ready, 1)
                dve.wait_ge(hv_ready, h * 2 + 2)
                for u in (1, 2):
                    L(U_HEAD, u, h)
                for c in range(2):
                    b, e = full(HEAD, f"ua{c}", h)
                    dve.wait_ge(*took(HEAD, f"ub{c}", h))
                    bias = hv[:, VUA + c:VUA + c + 1]
                    dve.scalar_tensor_tensor(samples(E[:, c, :])[:, :, CW - 1:CW - 1 + NI], b[:, 0:NS].rearrange("p (b i) -> p b i", b=NB),
                                             bias, sub[:, c, 0:NS].rearrange("p (b i) -> p b i", b=NB), ALU.add, ALU.mult)
                    dve.scalar_tensor_tensor(us[:, c, :], b[:, 0:NS], bias, sub[:, c, 0:NS], ALU.add, ALU.mult)
                    dve.scalar_tensor_tensor(E[:, c, EL + CW - 1:EXT], b[:, NS:T], bias, sub[:, c, NS:T], ALU.add, ALU.mult).then_inc(e, 1)
                L(U_HEAD, 3, h)
                cos, sin = tab[:, TB["cos"][0]:TB["cos"][1]], tab[:, TB["sin"][0]:TB["sin"][1]]
                for n, (name, r) in enumerate((("q", qr), ("k", kr))):
                    for m, (f0, f1) in enumerate(((cos, sin), (sin, cos))):
                        b, e = full(HEAD, f"{name}{m}", h)
                        bias = hv[:, VQK + 2 * n + m:VQK + 2 * n + m + 1]
                        dve.scalar_tensor_tensor(rt[:, 2 * m, :], b[:, 0:T], bias, f0, ALU.add, ALU.mult)
                        dve.scalar_tensor_tensor(rt[:, 2 * m + 1, :], b[:, 0:T], bias, f1, ALU.add, ALU.mult).then_inc(e, 1)
                    for m in range(2):
                        dve.wait_ge(*took(HEAD, f"{name}{m}", h))
                    dve.tensor_tensor(r[:, 0, :], rt[:, 0, :], rt[:, 2, :], ALU.subtract).then_inc(rope_ready, 1)
                    dve.tensor_tensor(r[:, 1, :], rt[:, 1, :], rt[:, 3, :], ALU.add).then_inc(rope_ready, 1)
                    dve.wait_ge(rope_ready, h * 4 + (2 * n + 2))
                    L(U_HEAD, 4 + n, h)
                for p in range(2):
                    dve.tensor_tensor(qdiag[:, p, :].rearrange("p (b x) -> p b x", b=NB)[:, :, 0:NI],
                                      qr[:, p, 0:NS].rearrange("p (b i) -> p b i", b=NB),
                                      hs[:, HQ:HQ + NS].rearrange("p (b i) -> p b i", b=NB), ALU.mult).then_inc(qdiag_ready, 1)
                for c in range(2):
                    dve.wait_ge(*took(HEAD, f"hist{c}", h))
                    dve.wait_ge(*took(HEAD, f"ua{c}", h))
                conv(0, h, 0, 12)
                L(U_HEAD, 6, h)
                dve.wait_ge(vb_full, h * 16 + 16)
                for t in range(NT):
                    b, e = full(HEAD, f"v{t}", h)
                    dve.tensor_tensor(v_tok[:, t, :], b[0:TT, :], vb[:, :], ALU.add).then_inc(e, 1)
                dve.wait_ge(*took(HEAD, "v0", h))
                dve.sem_inc(v_ready, 1)
                conv(0, h, 12, 18)
                L(U_HEAD, 7, h)
                dve.wait_ge(kds_ready, h + 1)
                b, e = full(HEAD, "kt0", h)
                for s in range(NB):
                    i = dve.scalar_tensor_tensor(kds_lo[:, s, :], b[0:TT, 0:256], hs[0:TT, HKS + s:HKS + s + 1],
                                                 kds_hi[:, s, :].bitcast(f32), ALU.mult, ALU.subtract)
                i.then_inc(e, 1)
                dve.wait_ge(dec_full, h * 16 + 16)
                def decayed(t):
                    b, e = full(HEAD, f"att{t}", h)
                    a = slice(ATT_AT[t], ATT_AT[t] + ATT_W[t])
                    dve.tensor_tensor(att[:, a], b[0:TT, 0:ATT_W[t]], dec[:, a], ALU.mult).then_inc(e, 1)

                decayed(0)
                decayed(1)
                dve.wait_ge(vhi_ready, h + 1)
                dve.tensor_tensor(v_lo[:, :], v_tok[:, 0, :], v_hi[:, :].bitcast(f32), ALU.subtract).then_inc(vlo_ready, 1)
                conv(0, h, 18, 23)
                decayed(2)
                conv(0, h, 23, CW)
                L(U_HEAD, 8, h)
                conv(1, h, 0, 15)
                L(U_HEAD, 9, h)
                for n, ts in enumerate(((0, 1), (2,))):
                    for t in ts:
                        b, e = full(HEAD, f"o{t}", h)
                        link(dve.bn_stats(stats[:, t, :], b[0:TT, :]))
                        alone(dve, waits_met)
                        link(dve.bn_aggr(mv[:, t, :], stats[:, t, :]))
                    tt = slice(ts[0], ts[-1] + 1)
                    link(dve.tensor_scalar(rs[:, 0, tt], mv[:, tt, 1], EPS, None, ALU.add))
                    dve.reciprocal(rs[:, 0, tt], rs[:, 0, tt]).then_inc(rv_ready, 1)
                    dve.wait_ge(rstd_done, h * 2 + (n + 1))
                    for t in ts:
                        b, e = full(HEAD, f"o{t}", h)
                        dve.tensor_scalar(o_tok[:, t, :], b[0:TT, :], mv[:, t, 0:1], rs[:, 1, t:t + 1], ALU.subtract, ALU.mult).then_inc(e, 1)
                for s in range(NB):
                    for p in range(2):
                        b, e = full(HEAD, f"st{s}{p}", h)
                        dve.scalar_tensor_tensor(st[:, s, p, :], st[:, s, p, :], hs[:, HGAM:HGAM + 1], b[:, :], ALU.mult, ALU.add).then_inc(e, 1)
                for m in range(4):
                    dve.wait_ge(*took(HEAD, f"g{m}", h))
                for t in range(NT):
                    cols = slice(t * TT, (t + 1) * TT)
                    b, e = full(HEAD, f"oT{t}", h)
                    dve.tensor_tensor(sg_f[:, :, :], b[:, 0:4 * TT].rearrange("p (j n) -> p j n", j=4), rt[:, :, cols], ALU.mult).then_inc(e, 1)
                    dve.wait_ge(sghi_ready, h * NT + (t + 1))
                    dve.tensor_tensor(sg_lo[:, :, cols], sg_f[:, :, :], sg_hi[:, :, cols].bitcast(f32), ALU.subtract).then_inc(sglo_ready, 1)
                    dve.wait_ge(sglo_ready, h * NT + (t + 1))
                for m in range(8):
                    b, e = full(HEAD, f"wr{m}", h)
                    dve.tensor_tensor(retT[:, m, :], b[:, 0:T], retT[:, m, :], ALU.add).then_inc(e, 1)
                    conv(1, h, 15 + 2 * m, min(17 + 2 * m, CW))
                    if m == 4:
                        L(U_HEAD, 10, h)
                dve.wait_ge(*took(HEAD, "wr7", h))
                turns_end(H)

            dve.sem_inc(conv_done, 1)
            for v in range(1, 4):
                L(U_GATE, v, 0)
            b, e = full(MEAN, "mean")
            for k in range(KT):
                dve.tensor_tensor(cT[:, k, :], cT[:, k, :], b[:, 0:T], ALU.subtract).then_inc(csub_ready, 1)
            dve.wait_ge(csub_ready, KT)
            dve.sem_inc(e, 1)
            for v in range(4, 6):
                L(U_GATE, v, 0)
            b, e = full(VAR, "var")
            dve.tensor_scalar(rstd_c[:, :], b[:, 0:T], EPS, None, ALU.add).then_inc(e, 1)
            dve.wait_ge(*took(VAR, "var"))
            dve.reciprocal(rstd_c[:, :], rstd_c[:, :]).then_inc(rv_ready, 1)
            L(U_GATE, 6, 0)
            dve.wait_ge(rstd_done, NORMS + 1)
            for k in range(KT):
                dve.tensor_tensor(cT[:, k, :], cT[:, k, :], rstd_c[:, :], ALU.mult).then_inc(cn_ready, 1)
            L(U_GATE, 7, 0)
            dve.wait_ge(chi_ready, 1)
            dve.tensor_tensor(c_lo[:, :, :], cT[:, :, :], c_hi[:, :, :].bitcast(f32), ALU.subtract).then_inc(clo_ready, 1)
            L(U_CONV, 0, 0)
            L(U_CONV, 1, 0)
            for n in ("mc0", "mc1", "mr0", "mr1"):
                dve.wait_ge(*took(GATE2, n, 1))
            link(dve.tensor_tensor(retT[:, :, :], retT[:, :, :], gr[:, :, :], ALU.mult))
            for j in range(2):
                for u in range(2):
                    for m in range(2):
                        k = 4 * j + 2 * u + m
                        b, e = full(CONV, f"c{2 * u + m}", j)
                        dve.scalar_tensor_tensor(gc[:, k, :], b[:, 0:T], vec2[:, V2["bco"] + k:V2["bco"] + k + 1], gc[:, k, :], ALU.add, ALU.mult).then_inc(e, 1)
                    L(U_CONV, 2 + u, j)
                for m in range(4):
                    dve.wait_ge(*took(CONV, f"c{m}", j))
                ks = slice(4 * j, 4 * j + 4)
                dve.tensor_tensor(gc[:, ks, :], gc[:, ks, :], retT[:, ks, :], ALU.add).then_inc(mf_ready, 1)
                dve.wait_ge(mf_ready, j + 1)
                dve.wait_ge(mhi_done, j + 1)
                dve.tensor_tensor(m_lo[:, ks, :], gc[:, ks, :], m_hi[:, ks, :].bitcast(f32), ALU.subtract).then_inc(mlo_done, 1)
            L(U_WOUT, 2, 0)
            L(U_WOUT, 3, 0)
            dve.wait_ge(s_xres, 16 * 5)
            dve.wait_ge(s_ln, 32)

            def layernorm(x, t, bc, mst_, mmv_, k, ready):
                for n in range(2):
                    link(dve.bn_stats(mst_[:, t, 6 * n:6 * n + 6], x[:, t, 512 * n:512 * n + 512]))
                link(dve.bn_aggr(mmv_[:, t, 0:2], mst_[:, t, 0:12]))
                link(dve.tensor_scalar(mmv_[:, t, 2:3], mmv_[:, t, 1:2], EPS, None, ALU.add))
                dve.reciprocal(mmv_[:, t, 2:3], mmv_[:, t, 2:3]).then_inc(rv_ready, 1)
                dve.wait_ge(rstd_done, k + t + 1)
                i = dve.tensor_scalar(x[:, t, :], x[:, t, :], mmv_[:, t, 0:1], mmv_[:, t, 3:4], ALU.subtract, ALU.mult)
                link(i)
                i = dve.tensor_tensor(x[:, t, :], x[:, t, :], bc[:, 0, :], ALU.mult)
                if ready is normed and t < NT - 1:
                    i.then_inc(ready, 1)
                    return
                link(i)
                dve.tensor_tensor(x[:, t, :], x[:, t, :], bc[:, 1, :], ALU.add).then_inc(ready, 1)

            for n in range(2):
                for t in range(NT):
                    b, e = full(WOUT, f"w{n}{t}")
                    cols = slice(512 * n, 512 * n + 512)
                    dve.scalar_tensor_tensor(x1[:, t, cols], x_tok[:, t, cols], ALPHA, b[0:TT, :], ALU.mult, ALU.add).then_inc(e, 1)
                    if n:
                        for q in range(2):
                            dve.wait_ge(*took(WOUT, f"w{q}{t}"))
                        layernorm(x1, t, ln_bc, lnst, lnmv, NORMS + 1, x1_ready)
            dve.wait_ge(x1_ready, NT)
            count(dve.tensor_scalar(y[:, :, :], x1[:, :, :], ALPHA, None, ALU.mult))

            def wide(x):
                return x.unsqueeze(2).to_broadcast([TT, NT, NE])

            for t in range(NT):
                b, e = full(X1T, f"log{t}")
                dve.tensor_tensor(gt[:, 0, t, :], b[0:TT, 0:NE], br_bc[:, :], ALU.add).then_inc(e, 1)
            for t in range(NT):
                dve.wait_ge(*took(X1T, f"log{t}"))
            link(dve.tensor_reduce(gs[:, 0, :], gt[:, 0, :, :], AX.X, ALU.max))
            dve.tensor_tensor(gt[:, 0, :, :], gt[:, 0, :, :], wide(gs[:, 0, :]), ALU.subtract).then_inc(lg_ready, 1)
            dve.wait_ge(exp_ready, 1)
            dve.wait_ge(iota_ready, 1)
            P = gt[:, 1, :, :]
            link(dve.tensor_reduce(gs[:, 1, :], P, AX.X, ALU.add))
            link(dve.reciprocal(gs[:, 2, :], gs[:, 1, :]))
            link(dve.tensor_tensor(P, P, wide(gs[:, 2, :]), ALU.mult))
            link(dve.tensor_reduce(gs[:, 3, :], P, AX.X, ALU.max))
            link(dve.tensor_tensor(gt[:, 2, :, :], P, wide(gs[:, 3, :]), ALU.is_equal))
            link(dve.tensor_tensor(gt[:, 2, :, :], gt[:, 2, :, :], iota_r[:, :, :], ALU.mult))
            link(dve.tensor_reduce(gs[:, 4, :], gt[:, 2, :, :], AX.X, ALU.max))
            link(dve.tensor_tensor(gt[:, 3, :, :], iota_r[:, :, :], wide(gs[:, 4, :]), ALU.is_equal))
            link(dve.tensor_reduce(gg[:, :, :], gt[:, 3, :, :].rearrange("p t (g e) -> p t g e", g=NG), AX.X, ALU.max))
            for q in range(EG):
                link(dve.tensor_tensor(gt[:, 4, :, q:NE:EG], gg[:, :, :], gt[:, 3, :, q:NE:EG], ALU.subtract))
            link(dve.tensor_tensor(gt[:, 5, :, :], P, gt[:, 4, :, :], ALU.mult))
            link(dve.tensor_reduce(gs[:, 5, :], gt[:, 5, :, :], AX.X, ALU.max))
            link(dve.tensor_tensor(gt[:, 6, :, :], gt[:, 5, :, :], wide(gs[:, 5, :]), ALU.is_equal))
            link(dve.tensor_tensor(gt[:, 6, :, :], gt[:, 6, :, :], gt[:, 4, :, :], ALU.mult))
            link(dve.tensor_tensor(gt[:, 6, :, :], gt[:, 6, :, :], iota_r[:, :, :], ALU.mult))
            link(dve.tensor_reduce(gs[:, 6, :], gt[:, 6, :, :], AX.X, ALU.max))
            link(dve.tensor_tensor(gt[:, 6, :, :], iota_r[:, :, :], wide(gs[:, 6, :]), ALU.is_equal))
            dve.tensor_tensor(gt[:, 7, :, :], gt[:, 3, :, :], gt[:, 6, :, :], ALU.add).then_inc(chosen_ready, 1)
            link(dve.tensor_tensor(gs[:, 7, :], gs[:, 3, :], gs[:, 5, :], ALU.add))
            link(dve.reciprocal(gs[:, 7, :], gs[:, 7, :]))
            link(dve.tensor_tensor(gs[:, 3, :], gs[:, 3, :], gs[:, 7, :], ALU.mult))
            link(dve.tensor_tensor(gs[:, 5, :], gs[:, 5, :], gs[:, 7, :], ALU.mult))
            b, e = full(X1T, "pos")
            link(dve.tensor_reduce(most[:, 0:1], b[0:TT, NT * NE:(NT + 1) * NE], AX.X, ALU.max))
            dve.tensor_copy(most_i[:, :], most[:, 0:1]).then_inc(most_ready, 1)
            link(dve.tensor_scalar(gt[:, 0, :, :], iota_r[:, :, :], -float(CAP), float(NE * CAP), ALU.mult, ALU.add))
            dve.tensor_tensor(gt[:, 0, :, :], b[0:TT, 0:NT * NE].rearrange("p (t e) -> p t e", t=NT), gt[:, 0, :, :], ALU.add).then_inc(e, 1)
            dve.wait_ge(*took(X1T, "pos"))
            for k, o in enumerate((3, 6)):
                link(dve.tensor_tensor(gt[:, 1 + k, :, :], gt[:, o, :, :], gt[:, 0, :, :], ALU.mult))
                link(dve.tensor_reduce(gs[:, 1 + k, :], gt[:, 1 + k, :, :], AX.X, ALU.add))
                dve.tensor_copy(slot[:, k, :], gs[:, 1 + k, :]).then_inc(slots_ready, 1)
            most_now = dve.value_load(most_i[0:1, 0:1], min_val=0, max_val=T)
            steps_before = dict(step)
            with dve.If(most_now <= CAP):
                def lo_of(v, wit):
                    dve.wait_ge(mhi_ready, U_PAIR.idx(v, wit) + 1)
                    dve.tensor_tensor(mlo[:, v % MH, :], mraw[:, v % MR, :], mhi[:, v % MH, :].bitcast(f32), ALU.subtract).then_inc(mlo_ready, 1)

                def turned_lo(stage, name, it, lo_, hi_, ready, value):
                    b, e = full(stage, name, it)
                    dve.wait_ge(ready, value)
                    dve.tensor_tensor(lo_, b[:, 0:4 * CAP].rearrange("p (k n) -> p k n", k=4), hi_.bitcast(f32), ALU.subtract).then_inc(e, 1)

                def hidden(stage, p, n, it):
                    b, e = full(stage, f"u{p}{n}", it)
                    dve.wait_ge(*took(stage, f"g{p}{n}", it))
                    dve.tensor_tensor(h_tok[:, 512 * n:512 * n + 512], b[0:CAP, :], sgt[:, :], ALU.mult).then_inc(e, 1)

                def expert(stage, p, it, wit, following):
                    v = 12 * p
                    for u in range(2, 14):
                        if following or u < 12:
                            lo_of(v + u, wit)
                        if u == 5:
                            hidden(stage, p, 0, it)
                        if u == 8:
                            turned_lo(stage, f"ht{p}0", it, hT_lo[:, 0:4, :], hT_hi[:, 0:4, :], hthi_ready, wit * 4 + (2 * p + 1))
                            if following:
                                for j in range(2):
                                    turned_lo(stage, f"xt{p}{j}", it, xg_lo[:, 1 - p, 4 * j:4 * j + 4, :], xg_hi[:, 1 - p, 4 * j:4 * j + 4, :],
                                              xghi_ready, wit * 4 + (2 * p + j + 3))
                                if p:
                                    dve.wait_ge(*took(stage, "xt10", it))
                                    alone(dve, waits_met)
                                    dve.wait_ge(*took(stage, "xt11", it))
                                    dve.sem_inc(turned, 1)
                        if u == 9:
                            hidden(stage, p, 1, it)
                        if u == 10:
                            turned_lo(stage, f"ht{p}1", it, hT_lo[:, 4:8, :], hT_hi[:, 4:8, :], hthi_ready, wit * 4 + (2 * p + 2))

                lo_of(0, 0)
                lo_of(1, 0)
                for j in range(2):
                    turned_lo(FIRST, f"xt{j}", 0, xg_lo[:, 0, 4 * j:4 * j + 4, :], xg_hi[:, 0, 4 * j:4 * j + 4, :], xghi_ready, j + 1)
                for j in range(2):
                    dve.wait_ge(*took(FIRST, f"xt{j}"))
                dve.sem_inc(turned, 1)
                with dve.Fori(0, NE // 2 - 1) as it:
                    for p in range(2):
                        expert(PAIR, p, it, it, True)
                expert(LAST, 0, 0, NE // 2 - 1, True)
                expert(LAST, 1, 0, NE // 2 - 1, False)
                for n in range(2):
                    dve.wait_ge(*took(LAST, f"d1{n}"))
                dve.sem_inc(moe_done, 1)
                for t in range(NT):
                    dve.wait_ge(gathered[t], 32)
                    for k in range(2):
                        g = gs[:, 3 + 2 * k, t:t + 1]
                        link(dve.scalar_tensor_tensor(y[:, t, :], y_back[:, 2 * t + k, :], g, y[:, t, :], ALU.mult, ALU.add))
            with dve.Else():
                steps_gathered, local_gathered = dict(step), step["local"]
                step.update(steps_before)
                link(dve.tensor_tensor(gt[:, 3, :, :], gt[:, 3, :, :], wide(gs[:, 3, :]), ALU.mult))
                link(dve.tensor_tensor(gt[:, 6, :, :], gt[:, 6, :, :], wide(gs[:, 5, :]), ALU.mult))
                link(dve.tensor_tensor(gates[:, :, :], gt[:, 3, :, :], gt[:, 6, :, :], ALU.add))
                for i in range(6):
                    t, j = divmod(i, 2)
                    a = (slice(None), slice(4 * j, 4 * j + 4), slice(t * TT, (t + 1) * TT))
                    dve.wait_ge(x1hi_ready, i + 1)
                    dve.tensor_tensor(x1T_lo[a], x1T_f[a], x1T_hi[a].bitcast(f32), ALU.subtract).then_inc(x1lo_ready, 1)
                with dve.Fori(0, NE) as e_:
                    turns(e_, 1)
                    at_least(dve, evac[MOE.bank["d12"]], MOE.emptied("d12", e_))
                    link(dve.tensor_copy(g_e[:, :], gates[:, :, ds(e_, 1)].rearrange("p t a -> p (t a)")))
                    for u in range(14):
                        if u < 12:
                            LM(u, e_)
                        v = u - 2
                        if v < 0:
                            continue
                        if v < 8 and v % 2:
                            j = v // 2
                            for m in range(2):
                                b, e = full(MOE, f"u{2 * j + m}", e_)
                                dve.wait_ge(*took(MOE, f"g{2 * j + m}", e_))
                                dve.tensor_tensor(h_f[:, m, :], b[:, 0:T], sgm[:, j % 2, m, :], ALU.mult).then_inc(e, 1)
                            for m in range(2):
                                dve.wait_ge(*took(MOE, f"u{2 * j + m}", e_))
                            dve.wait_ge(hhi_ready, e_ * 4 + (j + 1))
                            dve.tensor_tensor(h_lo[:, 2 * j:2 * j + 2, :], h_f[:, :, :], h_hi[:, 2 * j:2 * j + 2, :].bitcast(f32), ALU.subtract).then_inc(hlo_ready, 1)
                            dve.wait_ge(hlo_ready, e_ * 4 + (j + 1))
                        elif v in (9, 11):
                            n = (v - 8) // 2
                            for t in range(NT):
                                b, e = full(MOE, f"d{n}{t}", e_)
                                o = y[:, t, 512 * n:512 * n + 512]
                                at_least(dve, e, MOE.used(f"d{n}{t}", e_))
                                dve.scalar_tensor_tensor(o, b[0:TT, :], g_e[:, t:t + 1], o, ALU.mult, ALU.add).then_inc(e, 1)
                    turns_end(NE)
                for n in range(2):
                    for t in range(NT):
                        dve.wait_ge(*took(MOE, f"d{n}{t}", NE - 1))
                dve.sem_inc(moe_done, 1)
            step.update(base=0, it=0, n=0, local=0, sem=tail_step)
            dve.wait_ge(s_ln2, 32)
            for t in range(NT):
                layernorm(y, t, ln2_bc, mst, mmv, NORMS + 1 + NT, normed)


_INS = ["x_prompt", "x_sample", "state_ret", "state_conv", "meta_tokens", "w_in", "b_in", "w_ret_o", "conv_w", "conv_b",
        "conv_ln_g", "conv_ln_b", "w_conv_o", "b_conv_o", "w_out", "ln1_g", "ln1_b", "ln2_g", "ln2_b", "w_router",
        "b_router", "w_gate", "w_up", "w_down", "tables", "decay"]
_OUTS = [((1, SEQ, D), "float32"), ((NB, NI, D), "float32"), ((1, 1, H, DK, DV), "float32"), ((1, 1, CW - 1, D), "float32"),
         ((1, NB, H, DK, DV), "float32"), ((1, NB, CW - 1, D), "float32")]


def kernel(**inputs):
    import numpy as _np
    import concourse.bacc as _bacc
    from concourse import mybir as _mybir
    from concourse.bass_utils import run_bass_kernel_spmd as _run

    nc = _bacc.Bacc("TRN2", target_bir_lowering=False, num_devices=1)
    inputs = {**inputs, **constants()}
    arrays, args = {}, []
    for name in _INS:
        a = _np.ascontiguousarray(inputs[name])
        arrays[f"in_{name}_dram"] = a
        args.append(nc.dram_tensor(f"in_{name}_dram", a.shape, _mybir.dt.from_np(a.dtype), kind="ExternalInput").ap())
    for i, (shape, dtype) in enumerate(_OUTS):
        args.append(nc.dram_tensor(f"out_{i}_dram", shape, _mybir.dt.from_np(_np.dtype(dtype)), kind="ExternalOutput").ap())
    for name in ("x_slots", "y_slots"):
        args.append(nc.dram_tensor(name, (NE * CAP, D), _mybir.dt.float32, kind="Internal").ap())
    program(nc, *args)
    r = _run(nc, [arrays], core_ids=[0])
    return tuple(r.results[0][f"out_{i}_dram"] for i in range(len(_OUTS)))
```
